# Optimizing a Trainium2 kernel written in Bass

```python
import math
import jax, jax.numpy as jnp
from jax import lax
import numpy as np

D_MODEL = 1024
BATCH = 1
SEQ = 256
DEPTH = 2

ATT_HEADS = 8
ATT_HEAD_DIM = 64
ATT_WIDTH = ATT_HEADS * ATT_HEAD_DIM
DILATED_PATTERNS = ((128, 1), (512, 4), (2048, 16))
ATT_BLOCK = 128
ROPE_THETA = 500000.0
ROPE_DIM = ATT_HEAD_DIM // 4

MLSTM_HEADS = 4
MLSTM_HEAD_DIM = 128
MLSTM_WIDTH = MLSTM_HEADS * MLSTM_HEAD_DIM
MLSTM_CHUNK = 64
CONV_WIDTH = 4
FORGET_BIAS = 3.0

D_FF = 4 * D_MODEL
NORM_EPS = 1e-6

COL_AQ = 0
COL_AK = COL_AQ + ATT_WIDTH
COL_AV = COL_AK + ATT_WIDTH
COL_MQ = COL_AV + ATT_WIDTH
COL_MK = COL_MQ + MLSTM_WIDTH
COL_MV = COL_MK + MLSTM_WIDTH
COL_MO = COL_MV + MLSTM_WIDTH
COL_MI = COL_MO + MLSTM_WIDTH
COL_MF = COL_MI + MLSTM_HEADS
COL_GA = COL_MF + MLSTM_HEADS
COL_GB = COL_GA + D_MODEL
D_IN = COL_GB + D_MODEL


def rms_norm(x, w):
    xf = x.astype(jnp.float32)
    y = xf * lax.rsqrt(jnp.mean(xf * xf, axis=-1, keepdims=True) + NORM_EPS)
    return (y * w.astype(jnp.float32)).astype(x.dtype)

def rope_tables(positions):
    inv_freq = ROPE_THETA ** (-jnp.arange(0, ROPE_DIM, 2, dtype=jnp.float32) / ROPE_DIM)
    ang = positions.astype(jnp.float32)[..., None] * inv_freq
    return jnp.cos(ang)[:, :, None, :], jnp.sin(ang)[:, :, None, :]

def apply_partial_rope(t, cos, sin):
    half = ROPE_DIM // 2
    t1 = t[..., :half]
    t2 = t[..., half:ROPE_DIM]
    return jnp.concatenate([t1 * cos - t2 * sin, t2 * cos + t1 * sin, t[..., ROPE_DIM:]], axis=-1)

def dilated_window_attention(q, k, v, window, dilation):
    B, S, H, Dh = q.shape
    span = window // dilation
    L = S // dilation
    nb = -(-L // ATT_BLOCK)
    Lp = nb * ATT_BLOCK
    BD = B * dilation

    def to_sub(t):
        return t.reshape(B, L, dilation, H, Dh).transpose(0, 2, 1, 3, 4).reshape(BD, L, H, Dh)

    qs, ks, vs = to_sub(q), to_sub(k), to_sub(v)
    qb = jnp.pad(qs, ((0, 0), (0, Lp - L), (0, 0), (0, 0))).reshape(BD, nb, ATT_BLOCK, H, Dh)

    def key_blocks(t):
        tp = jnp.pad(t, ((0, 0), (ATT_BLOCK, Lp - L), (0, 0), (0, 0)))
        tp = tp.reshape(BD, nb + 1, ATT_BLOCK, H, Dh)
        return jnp.concatenate([tp[:, :-1], tp[:, 1:]], axis=2)

    kb, vb = key_blocks(ks), key_blocks(vs)
    blk = jnp.arange(nb)[:, None, None]
    qa = jnp.arange(ATT_BLOCK)[None, :, None]
    kc = jnp.arange(2 * ATT_BLOCK)[None, None, :]
    dist = qa + ATT_BLOCK - kc
    key_idx = blk * ATT_BLOCK - ATT_BLOCK + kc
    mask = (dist >= 0) & (dist <= span) & (key_idx >= 0)

    s = jnp.einsum('bnqhd,bnkhd->bnhqk', qb, kb) * (Dh ** -0.5)
    s = jnp.where(mask[None, :, None], s, -jnp.inf)
    m = jnp.max(s, axis=-1, keepdims=True)
    p = jnp.exp(s - m)
    l = jnp.sum(p, axis=-1)
    o = jnp.einsum('bnhqk,bnkhd->bnqhd', p, vb) / jnp.transpose(l, (0, 1, 3, 2))[..., None]
    lse = jnp.transpose(m[..., 0] + jnp.log(l), (0, 1, 3, 2))

    o = o.reshape(BD, Lp, H, Dh)[:, :L].reshape(B, dilation, L, H, Dh)
    o = o.transpose(0, 2, 1, 3, 4).reshape(B, S, H, Dh)
    lse = lse.reshape(BD, Lp, H)[:, :L].reshape(B, dilation, L, H)
    lse = lse.transpose(0, 2, 1, 3).reshape(B, S, H)
    return o, lse

def dilated_mixture_attention(q, k, v):
    outs, lses = [], []
    for window, dilation in DILATED_PATTERNS:
        o, lse = dilated_window_attention(q, k, v, window, dilation)
        outs.append(o)
        lses.append(lse)
    wts = jax.nn.softmax(jnp.stack(lses), axis=0)
    return jnp.einsum('gbsh,gbshd->bshd', wts, jnp.stack(outs))

def causal_short_conv(u, w, b):
    S = u.shape[1]
    up = jnp.pad(u, ((0, 0), (CONV_WIDTH - 1, 0), (0, 0)))
    out = b
    for j in range(CONV_WIDTH):
        out = out + w[j] * up[:, j:j + S]
    return out

def mlstm_chunkwise(q, k, v, ig, fg):
    B, S, H, D = q.shape
    L = MLSTM_CHUNK
    NC = S // L

    def chunks(t):
        return t.reshape(B, NC, L, H, D).transpose(0, 3, 1, 2, 4)

    def gchunks(t):
        return t.reshape(B, NC, L, H).transpose(0, 3, 1, 2)

    q = chunks(q) * (D ** -0.5)
    k = chunks(k)
    v = chunks(v)
    ig = gchunks(ig)
    lf = gchunks(jax.nn.log_sigmoid(fg))
    bcum = jnp.cumsum(lf, axis=-1)
    g = bcum[..., -1]

    a = g[..., None] - bcum + ig
    m_loc = jnp.max(a, axis=-1)
    wk = jnp.exp(a - m_loc[..., None])
    kv_c = jnp.einsum('bhcl,bhclk,bhclv->bhckv', wk, k, v)
    n_c = jnp.einsum('bhcl,bhclk->bhck', wk, k)

    def step(carry, xs):
        C, n, m = carry
        g_c, ml, kv, nn = xs
        m_new = jnp.maximum(g_c + m, ml)
        decay = jnp.exp(g_c + m - m_new)
        inj = jnp.exp(ml - m_new)
        C_new = decay[..., None, None] * C + inj[..., None, None] * kv
        n_new = decay[..., None] * n + inj[..., None] * nn
        return (C_new, n_new, m_new), (C, n, m)

    init = (jnp.zeros((B, H, D, D), jnp.float32), jnp.zeros((B, H, D), jnp.float32),
            jnp.zeros((B, H), jnp.float32))
    xs = (g.transpose(2, 0, 1), m_loc.transpose(2, 0, 1),
          kv_c.transpose(2, 0, 1, 3, 4), n_c.transpose(2, 0, 1, 3))
    _, (C_prev, n_prev, m_prev) = lax.scan(step, init, xs)
    C_prev = C_prev.transpose(1, 2, 0, 3, 4)
    n_prev = n_prev.transpose(1, 2, 0, 3)
    m_prev = m_prev.transpose(1, 2, 0)

    causal = jnp.tril(jnp.ones((L, L), dtype=bool))
    dmat = bcum[..., :, None] - bcum[..., None, :] + ig[..., None, :]
    dmat = jnp.where(causal, dmat, -jnp.inf)
    m_inter = bcum + m_prev[..., None]
    m_t = jnp.maximum(jnp.max(dmat, axis=-1), m_inter)
    p = jnp.exp(dmat - m_t[..., None]) * jnp.einsum('bhcld,bhcsd->bhcls', q, k)
    w_inter = jnp.exp(m_inter - m_t)
    num = (w_inter[..., None] * jnp.einsum('bhcld,bhcdv->bhclv', q, C_prev)
           + jnp.einsum('bhcls,bhcsv->bhclv', p, v))
    den = w_inter * jnp.einsum('bhcld,bhcd->bhcl', q, n_prev) + jnp.sum(p, axis=-1)
    h = num / jnp.maximum(jnp.abs(den), jnp.exp(-m_t))[..., None]
    return h.transpose(0, 2, 3, 1, 4).reshape(B, S, H, D)

def hybrid_layer(x, cos, sin, norm_mix_w, w_in, b_in, conv_w, conv_b, mlstm_norm_w,
                 w_proj_att, w_proj_mlstm, w_out, norm_mlp_w, w_ff1, w_ff2):
    B, S, _ = x.shape
    f32 = jnp.float32
    h = rms_norm(x, norm_mix_w)
    z = h @ w_in + b_in

    aq = z[..., COL_AQ:COL_AK].astype(f32).reshape(B, S, ATT_HEADS, ATT_HEAD_DIM)
    ak = z[..., COL_AK:COL_AV].astype(f32).reshape(B, S, ATT_HEADS, ATT_HEAD_DIM)
    av = z[..., COL_AV:COL_MQ].astype(f32).reshape(B, S, ATT_HEADS, ATT_HEAD_DIM)
    aq = apply_partial_rope(aq, cos, sin)
    ak = apply_partial_rope(ak, cos, sin)
    ya = dilated_mixture_attention(aq, ak, av).reshape(B, S, ATT_WIDTH).astype(x.dtype)

    qk = jax.nn.silu(causal_short_conv(z[..., COL_MQ:COL_MV].astype(f32),
                                       conv_w.astype(f32), conv_b.astype(f32)))
    mq = qk[..., :MLSTM_WIDTH].reshape(B, S, MLSTM_HEADS, MLSTM_HEAD_DIM)
    mk = qk[..., MLSTM_WIDTH:].reshape(B, S, MLSTM_HEADS, MLSTM_HEAD_DIM)
    mv = z[..., COL_MV:COL_MO].astype(f32).reshape(B, S, MLSTM_HEADS, MLSTM_HEAD_DIM)
    mi = z[..., COL_MI:COL_MF].astype(f32)
    mf = z[..., COL_MF:COL_GA].astype(f32)
    hm = mlstm_chunkwise(mq, mk, mv, mi, mf)
    hm = hm * lax.rsqrt(jnp.mean(hm * hm, axis=-1, keepdims=True) + NORM_EPS)
    hm = hm.reshape(B, S, MLSTM_WIDTH) * mlstm_norm_w.astype(f32)
    yb = (jax.nn.sigmoid(z[..., COL_MO:COL_MI].astype(f32)) * hm).astype(x.dtype)

    ga = jax.nn.sigmoid(z[..., COL_GA:COL_GB])
    gb = jax.nn.sigmoid(z[..., COL_GB:D_IN])
    mixed = ga * (ya @ w_proj_att) + gb * (yb @ w_proj_mlstm)
    x = x + mixed @ w_out

    h2 = rms_norm(x, norm_mlp_w)
    x = x + jnp.square(jax.nn.relu(h2 @ w_ff1)) @ w_ff2
    return x

def first_inputs(seed: int = 0) -> dict:
    key = jax.random.key(seed)
    ks = jax.random.split(key, 16)
    nrm = jax.random.normal
    x = nrm(ks[0], (BATCH, SEQ, D_MODEL), jnp.float32)
    offsets = jax.random.randint(ks[1], (BATCH, 1), 0, 1024, dtype=jnp.int32)
    positions = offsets + jnp.arange(SEQ, dtype=jnp.int32)[None, :]
    norm_mix_w = 1.0 + 0.05 * nrm(ks[2], (DEPTH, D_MODEL), jnp.float32)
    w_in = nrm(ks[3], (DEPTH, D_MODEL, D_IN), jnp.float32) * D_MODEL ** -0.5
    b_in = 0.02 * nrm(ks[4], (DEPTH, D_IN), jnp.float32)
    b_in = b_in.at[:, COL_MF:COL_GA].add(FORGET_BIAS)
    conv_w = nrm(ks[5], (DEPTH, CONV_WIDTH, 2 * MLSTM_WIDTH), jnp.float32) * CONV_WIDTH ** -0.5
    conv_b = 0.02 * nrm(ks[6], (DEPTH, 2 * MLSTM_WIDTH), jnp.float32)
    mlstm_norm_w = 1.0 + 0.05 * nrm(ks[7], (DEPTH, MLSTM_WIDTH), jnp.float32)
    w_proj_att = nrm(ks[8], (DEPTH, ATT_WIDTH, D_MODEL), jnp.float32) * ATT_WIDTH ** -0.5
    w_proj_mlstm = nrm(ks[9], (DEPTH, MLSTM_WIDTH, D_MODEL), jnp.float32) * MLSTM_WIDTH ** -0.5
    w_out = nrm(ks[10], (DEPTH, D_MODEL, D_MODEL), jnp.float32) * D_MODEL ** -0.5
    norm_mlp_w = 1.0 + 0.05 * nrm(ks[11], (DEPTH, D_MODEL), jnp.float32)
    w_ff1 = nrm(ks[12], (DEPTH, D_MODEL, D_FF), jnp.float32) * D_MODEL ** -0.5
    w_ff2 = nrm(ks[13], (DEPTH, D_FF, D_MODEL), jnp.float32) * (0.5 * D_FF ** -0.5)
    final_norm_w = 1.0 + 0.05 * nrm(ks[14], (D_MODEL,), jnp.float32)
    return {"x": x, "positions": positions, "norm_mix_w": norm_mix_w, "w_in": w_in,
            "b_in": b_in, "conv_w": conv_w, "conv_b": conv_b, "mlstm_norm_w": mlstm_norm_w,
            "w_proj_att": w_proj_att, "w_proj_mlstm": w_proj_mlstm, "w_out": w_out,
            "norm_mlp_w": norm_mlp_w, "w_ff1": w_ff1, "w_ff2": w_ff2,
            "final_norm_w": final_norm_w}

def first_block(x, positions, norm_mix_w, w_in, b_in, conv_w, conv_b, mlstm_norm_w,
              w_proj_att, w_proj_mlstm, w_out, norm_mlp_w, w_ff1, w_ff2, final_norm_w):
    cos, sin = rope_tables(positions)
    for l in range(DEPTH):
        x = hybrid_layer(x, cos, sin, norm_mix_w[l], w_in[l], b_in[l], conv_w[l], conv_b[l],
                         mlstm_norm_w[l], w_proj_att[l], w_proj_mlstm[l], w_out[l],
                         norm_mlp_w[l], w_ff1[l], w_ff2[l])
    return rms_norm(x, final_norm_w)


N_BRANCH = 4
BRANCH_W = 256
GM_GROUPS = 4
GM_CHUNK = 128
GM_GD = BRANCH_W // GM_GROUPS
POOL_WINDOWS = (2, 4, 8, 16)
POOL_GD = BRANCH_W // len(POOL_WINDOWS)
ATT_HEADS_2 = 4
ATT_HD = BRANCH_W // ATT_HEADS_2
IDX_HEADS = 4
IDX_HD = 32
TOPK_MAX = 256
Q_BLOCK = 128
REL_BUCKETS = 32
REL_MAX_DIST = 128
CONV_K = 31
D_FF_2 = 2816
EPS = 1e-6

IN_SIZES = (2 * BRANCH_W, BRANCH_W, BRANCH_W, BRANCH_W, BRANCH_W, IDX_HEADS * IDX_HD, IDX_HD, IDX_HEADS, 2 * BRANCH_W, N_BRANCH * D_MODEL)
IN_COLS = 2 * BRANCH_W + 4 * BRANCH_W + IDX_HEADS * IDX_HD + IDX_HD + IDX_HEADS + 2 * BRANCH_W + N_BRANCH * D_MODEL


def rmsnorm(x, g):
    xf = x.astype(jnp.float32)
    y = xf * lax.rsqrt(jnp.mean(xf * xf, axis=-1, keepdims=True) + EPS)
    return (y * g.astype(jnp.float32)).astype(x.dtype)

def layernorm(x, g, b):
    xf = x.astype(jnp.float32)
    mu = jnp.mean(xf, axis=-1, keepdims=True)
    xc = xf - mu
    y = xc * lax.rsqrt(jnp.mean(xc * xc, axis=-1, keepdims=True) + EPS)
    return (y * g.astype(jnp.float32) + b.astype(jnp.float32)).astype(x.dtype)

def swiglu_ffn(h, w_gu, w_down):
    a, b = jnp.split(h @ w_gu, 2, axis=-1)
    return (jax.nn.silu(a) * b) @ w_down

def gmlp_mixer(uv, v_g, ws, wb):
    B, S, _ = uv.shape
    u, v = jnp.split(jax.nn.gelu(uv), 2, axis=-1)
    v = rmsnorm(v, v_g)
    vc = v.reshape(B, S // GM_CHUNK, GM_CHUNK, GM_GROUPS, GM_GD)
    causal = jnp.tril(jnp.ones((GM_CHUNK, GM_CHUNK), dtype=bool))
    wsm = jnp.where(causal[None], ws, 0.0).astype(v.dtype)
    mixed = jnp.einsum('gts,bcsgd->bctgd', wsm, vc) + wb.T[None, None, :, :, None]
    return u * mixed.reshape(B, S, BRANCH_W)

def pool_mixer(p, pw, scale):
    B, S, _ = p.shape
    wmax = POOL_WINDOWS[-1]
    pf = p.astype(jnp.float32)
    csp = jnp.pad(jnp.cumsum(pf, axis=1), ((0, 0), (wmax, 0), (0, 0)))
    count = jnp.arange(1, S + 1, dtype=jnp.float32)[:, None]
    outs = []
    for g, w in enumerate(POOL_WINDOWS):
        sl = slice(g * POOL_GD, (g + 1) * POOL_GD)
        win = csp[:, wmax:, sl] - csp[:, wmax - w:wmax - w + S, sl]
        outs.append(win / jnp.minimum(count, float(w)) - pf[:, :, sl])
    d = jnp.stack(outs, axis=2).astype(p.dtype)
    y = jnp.einsum('bsgc,gcd->bsgd', d, pw).reshape(B, S, BRANCH_W)
    return y * scale

def conv_mixer(ab, dw, db, ln_g, ln_b):
    a, gt = jnp.split(ab, 2, axis=-1)
    h = a * jax.nn.sigmoid(gt)
    h = lax.conv_general_dilated(h, dw[:, None, :].astype(h.dtype), window_strides=(1,),
                                 padding=[(CONV_K - 1, 0)], dimension_numbers=('NWC', 'WIO', 'NWC'),
                                 feature_group_count=BRANCH_W) + db
    return jax.nn.silu(layernorm(h, ln_g, ln_b))

def t5_bucket(n):
    n = jnp.maximum(n, 0)
    max_exact = REL_BUCKETS // 2
    large = max_exact + (jnp.log(jnp.maximum(n, 1).astype(jnp.float32) / max_exact)
                         / math.log(REL_MAX_DIST / max_exact) * (REL_BUCKETS - max_exact)).astype(jnp.int32)
    return jnp.where(n < max_exact, n, jnp.minimum(large, REL_BUCKETS - 1))

def sparse_attention(q, k, v, q_idx, k_idx, w_idx, rel_bias):
    B, S, _ = q.shape
    topk = min(TOPK_MAX, S // 4)
    q = q.reshape(B, S, ATT_HEADS_2, ATT_HD)
    k = k.reshape(B, S, ATT_HEADS_2, ATT_HD)
    v = v.reshape(B, S, ATT_HEADS_2, ATT_HD)
    q_idx = q_idx.reshape(B, S, IDX_HEADS, IDX_HD)
    w_idx = w_idx.astype(jnp.float32) * (IDX_HEADS ** -0.5)
    s_pos = jnp.arange(S)
    gather = jax.vmap(lambda a, i: a[i])

    def block(i):
        t0 = i * Q_BLOCK
        t_pos = t0 + jnp.arange(Q_BLOCK)
        qb = lax.dynamic_slice_in_dim(q, t0, Q_BLOCK, axis=1)
        qib = lax.dynamic_slice_in_dim(q_idx, t0, Q_BLOCK, axis=1)
        wib = lax.dynamic_slice_in_dim(w_idx, t0, Q_BLOCK, axis=1)
        rel = jax.nn.relu(jnp.einsum('bqhd,bsd->bqhs', qib, k_idx).astype(jnp.float32) * (IDX_HD ** -0.5))
        score = jnp.einsum('bqh,bqhs->bqs', wib, rel)
        score = jnp.where(s_pos[None, None, :] <= t_pos[None, :, None], score, -jnp.inf)
        _, idx = lax.top_k(score, topk)
        valid = idx <= t_pos[None, :, None]
        ks = gather(k, idx)
        vs = gather(v, idx)
        bias = rel_bias[t5_bucket(t_pos[None, :, None] - idx)]
        logits = (jnp.einsum('bqhd,bqkhd->bqhk', qb, ks).astype(jnp.float32) * (ATT_HD ** -0.5)
                  + bias.astype(jnp.float32).transpose(0, 1, 3, 2))
        logits = jnp.where(valid[:, :, None, :], logits, -jnp.inf)
        p = jax.nn.softmax(logits, axis=-1).astype(v.dtype)
        o = jnp.einsum('bqhk,bqkhd->bqhd', p, vs)
        return o.reshape(B, Q_BLOCK, BRANCH_W)

    out = lax.map(block, jnp.arange(S // Q_BLOCK))
    return out.transpose(1, 0, 2, 3).reshape(B, S, BRANCH_W)

def mixing_sublayer(h, w_in, gm_v_g, gm_ws, gm_b, pool_w, pool_scale, conv_dw, conv_b,
                    conv_ln_g, conv_ln_b, w_branch, w_out, rel_bias):
    B, S, _ = h.shape
    z = h @ w_in
    uv, pz, qz, kz, vz, qi, ki, wi, cz, gz = jnp.split(z, list(np.cumsum(IN_SIZES)[:-1]), axis=-1)
    branches = (
        gmlp_mixer(uv, gm_v_g, gm_ws, gm_b),
        pool_mixer(pz, pool_w, pool_scale),
        sparse_attention(qz, kz, vz, qi, ki, wi, rel_bias),
        conv_mixer(cz, conv_dw, conv_b, conv_ln_g, conv_ln_b),
    )
    gates = jax.nn.sigmoid(gz.reshape(B, S, N_BRANCH, D_MODEL))
    y = gates[:, :, 0] * (branches[0] @ w_branch[0])
    for n in range(1, N_BRANCH):
        y = y + gates[:, :, n] * (branches[n] @ w_branch[n])
    return y @ w_out

def second_inputs(seed: int = 0) -> dict:
    key = jax.random.key(seed)
    ks = jax.random.split(key, 24)
    f32 = jnp.float32

    def nrm(k, shape, scale):
        return jax.random.normal(k, shape, f32) * scale

    def gain(k, shape):
        return 1.0 + 0.05 * jax.random.normal(k, shape, f32)

    L, D, C, F = DEPTH, D_MODEL, BRANCH_W, D_FF_2
    return {
        'x': nrm(ks[0], (BATCH, SEQ, D), 1.0),
        'ffn1_pre_g': gain(ks[1], (L, D)),
        'ffn1_post_g': gain(ks[2], (L, D)),
        'ffn1_w_gu': nrm(ks[3], (L, D, 2 * F), D ** -0.5),
        'ffn1_w_down': nrm(ks[4], (L, F, D), F ** -0.5),
        'mix_pre_g': gain(ks[5], (L, D)),
        'mix_post_g': gain(ks[6], (L, D)),
        'w_in': nrm(ks[7], (L, D, IN_COLS), D ** -0.5),
        'gm_v_g': gain(ks[8], (L, C)),
        'gm_ws': nrm(ks[9], (L, GM_GROUPS, GM_CHUNK, GM_CHUNK), GM_CHUNK ** -0.5),
        'gm_b': 1.0 + 0.1 * jax.random.normal(ks[10], (L, GM_GROUPS, GM_CHUNK), f32),
        'pool_w': nrm(ks[11], (L, len(POOL_WINDOWS), POOL_GD, POOL_GD), POOL_GD ** -0.5),
        'pool_scale': gain(ks[12], (L, C)),
        'conv_dw': nrm(ks[13], (L, CONV_K, C), CONV_K ** -0.5),
        'conv_b': nrm(ks[14], (L, C), 0.02),
        'conv_ln_g': gain(ks[15], (L, C)),
        'conv_ln_b': nrm(ks[16], (L, C), 0.02),
        'w_branch': nrm(ks[17], (L, N_BRANCH, C, D), C ** -0.5),
        'w_out': nrm(ks[18], (L, D, D), D ** -0.5),
        'ffn2_pre_g': gain(ks[19], (L, D)),
        'ffn2_post_g': gain(ks[20], (L, D)),
        'ffn2_w_gu': nrm(ks[21], (L, D, 2 * F), D ** -0.5),
        'ffn2_w_down': nrm(ks[22], (L, F, D), F ** -0.5),
        'rel_bias': nrm(ks[23], (REL_BUCKETS, ATT_HEADS_2), 0.5),
    }

def second_block(x, ffn1_pre_g, ffn1_post_g, ffn1_w_gu, ffn1_w_down, mix_pre_g, mix_post_g, w_in,
              gm_v_g, gm_ws, gm_b, pool_w, pool_scale, conv_dw, conv_b, conv_ln_g, conv_ln_b,
              w_branch, w_out, ffn2_pre_g, ffn2_post_g, ffn2_w_gu, ffn2_w_down, rel_bias):
    for l in range(DEPTH):
        h = swiglu_ffn(rmsnorm(x, ffn1_pre_g[l]), ffn1_w_gu[l], ffn1_w_down[l])
        x = x + 0.5 * rmsnorm(h, ffn1_post_g[l])
        h = mixing_sublayer(rmsnorm(x, mix_pre_g[l]), w_in[l], gm_v_g[l], gm_ws[l], gm_b[l],
                            pool_w[l], pool_scale[l], conv_dw[l], conv_b[l], conv_ln_g[l],
                            conv_ln_b[l], w_branch[l], w_out[l], rel_bias)
        x = x + rmsnorm(h, mix_post_g[l])
        h = swiglu_ffn(rmsnorm(x, ffn2_pre_g[l]), ffn2_w_gu[l], ffn2_w_down[l])
        x = x + 0.5 * rmsnorm(h, ffn2_post_g[l])
    return x


def setup_inputs(seed=0):
    out = dict(first_inputs(seed))
    for name, value in second_inputs(seed + 1).items():
        if name != "x":
            out[name + "_2"] = value
    return out


def reference(
    x, positions, norm_mix_w, w_in, b_in, conv_w, conv_b, mlstm_norm_w, w_proj_att,
    w_proj_mlstm, w_out, norm_mlp_w, w_ff1, w_ff2, final_norm_w, ffn1_pre_g_2, ffn1_post_g_2,
    ffn1_w_gu_2, ffn1_w_down_2, mix_pre_g_2, mix_post_g_2, w_in_2, gm_v_g_2, gm_ws_2, gm_b_2,
    pool_w_2, pool_scale_2, conv_dw_2, conv_b_2, conv_ln_g_2, conv_ln_b_2, w_branch_2, w_out_2,
    ffn2_pre_g_2, ffn2_post_g_2, ffn2_w_gu_2, ffn2_w_down_2, rel_bias_2,
):
    x = first_block(
        x, positions, norm_mix_w, w_in, b_in, conv_w, conv_b, mlstm_norm_w, w_proj_att,
        w_proj_mlstm, w_out, norm_mlp_w, w_ff1, w_ff2, final_norm_w,
    )
    return second_block(
        x, ffn1_pre_g_2, ffn1_post_g_2, ffn1_w_gu_2, ffn1_w_down_2, mix_pre_g_2, mix_post_g_2,
        w_in_2, gm_v_g_2, gm_ws_2, gm_b_2, pool_w_2, pool_scale_2, conv_dw_2, conv_b_2,
        conv_ln_g_2, conv_ln_b_2, w_branch_2, w_out_2, ffn2_pre_g_2, ffn2_post_g_2, ffn2_w_gu_2,
        ffn2_w_down_2, rel_bias_2,
    )


_drawn_inputs = setup_inputs


def setup_inputs(seed=0):
    import zlib

    import numpy as np

    out = dict(_drawn_inputs(seed))
    spreads = {}
    factors = {'gm_v_g_2': 3.214, 'conv_ln_b_2': 4.981, 'conv_b_2': 3.331, 'conv_ln_g_2': 2.841}
    for name, (base, spread) in spreads.items():
        noise = np.random.default_rng([zlib.crc32(name.encode()), seed]).standard_normal(out[name].shape)
        drawn = base * np.exp(spread * noise) if base else spread * noise
        out[name] = __import__('jax').numpy.asarray(drawn.astype(out[name].dtype))
    for name, factor in factors.items():
        out[name] = (out[name] * factor).astype(out[name].dtype)
    return out
```

```python
import math
from contextlib import ExitStack

import numpy as np
import concourse.bass as bass
from concourse import mybir
from concourse.alu_op_type import AluOpType as ALU

F32, F32R, I32 = mybir.dt.float32, mybir.dt.float32r, mybir.dt.int32
ACT = mybir.ActivationFunctionType
AX = mybir.AxisListType

P = 128
SEQ, DM, DEPTH = 256, 1024, 2
TT = SEQ // P
KT = DM // P
CH = 2048
SLOTS = 3
EPS = 1e-6
NEG = -1e30

AH, AD = 8, 64
MH, MD = 4, 128
RH = 8
CONV = 4
CA = 63
FF_A = 16
BW, BH, BD = 256, 4, 64
IH, ID = 4, 32
TOPK = 64
TAPS = 31
CB = 99
FF_B = 11
NBR = 4

PA_NORM, PA_MLP, PA_BQK, PA_BMO, PA_BG, PA_CW, PA_CB, PA_MN, PA_END = np.cumsum([0, 8, 8, 8, 4, 16, 32, 8, 4])
ROWS_A = 4 * 512 + 8

KA_ID, KA_ADD, KA_MULT, KA_CAUS, KA_SEL, KA_FREQ, KA_END = np.cumsum([0, P, 3 * P, 3 * P, 3 * P, MH * P, RH])


DVE_A = 114


class Signal:

    def __init__(self, sem, per, start=0):
        self.sem, self.per, self.start = sem, per, start

    def at(self, layer, n):
        return layer * self.per + (self.start + n)


def held(eng, value):
    return eng.snap(eng.to_reg(value))


class Chain:

    def __init__(self, sem, per):
        self.sem, self.per, self.n = sem, per, 0

    def one(self):
        self.n += 1
        return 1

    def at(self, layer, later=0):
        return layer * self.per + (self.n - later)


class Stream:

    def __init__(self, base, per):
        assert base % SLOTS == 0 and per % SLOTS == 0
        self.base, self.per = base, per

    def count(self, layer, c, trips=0):
        return (layer * (self.per // SLOTS) + trips) * SLOTS + (self.base + c + 1)

    def results(self, layer, c, trips=0):
        return self.count(layer, c, trips) + SLOTS

    def loads(self, layer, c, trips=0):
        return (layer * (self.per // SLOTS) + trips) * 16 + 16 * (self.base // SLOTS + c // SLOTS + 1)


def mid(ap, n):
    return ap.unsqueeze(1).broadcast_to([ap.shape[0], n, ap.shape[1]])


def last(ap, n):
    return ap.unsqueeze(len(ap.shape)).broadcast_to([*ap.shape, n])


def rsqrt(dve, ch, layer, y, v, t):
    dve.tensor_single_scalar(t.bitcast(I32), v.bitcast(I32), 1, ALU.arith_shift_right).then_inc(ch.sem, ch.one())
    dve.wait_ge(ch.sem, ch.at(layer))
    dve.tensor_scalar(y.bitcast(I32), t.bitcast(I32), -1.0, float(0x5F3759DF), ALU.mult, ALU.add).then_inc(ch.sem, ch.one())
    dve.wait_ge(ch.sem, ch.at(layer))
    for _ in range(3):
        dve.scalar_tensor_tensor(t, y, -0.5, v, ALU.mult, ALU.mult).then_inc(ch.sem, ch.one())
        dve.wait_ge(ch.sem, ch.at(layer))
        dve.tensor_tensor(t, t, y, ALU.mult).then_inc(ch.sem, ch.one())
        dve.wait_ge(ch.sem, ch.at(layer))
        dve.scalar_tensor_tensor(y, t, 1.5, y, ALU.add, ALU.mult).then_inc(ch.sem, ch.one())
        dve.wait_ge(ch.sem, ch.at(layer))



def split_high(k, act, st, layer, c, trips=0):
    s = c % SLOTS
    act.wait_ge(k.raw_loaded[s], st.loads(layer, c, trips))
    act.wait_ge(k.chunk_done, st.count(layer, c, trips))
    act.activation(k.w_hi[:, s, :], k.raw[:, s, :], ACT.Copy).then_inc(k.hi_ready, 1)


def split_low(k, dve, st, layer, c, trips=0):
    s = c % SLOTS
    dve.wait_ge(k.hi_ready, st.count(layer, c, trips))
    dve.tensor_tensor(k.w_lo[:, s, :], k.raw[:, s, :], k.w_hi[:, s, :].bitcast(F32),
                      ALU.subtract).then_inc(k.lo_ready, 1)


class Splitter:

    def __init__(self, split, k, eng, st, layer):
        self.args, self.split, self.next = (k, eng, st, layer), split, 0

    def upto(self, c):
        while self.next <= c:
            self.split(*self.args, self.next)
            self.next += 1


def product(pe, out, a, b, first, end):
    pe.matmul(out, a[0], b[0], start=first, stop=False)
    pe.matmul(out, a[0], b[1], start=False, stop=False)
    return pe.matmul(out, a[1], b[0], start=False, stop=end)


def f_chunk(k, pe, c, banks, rows, act):
    s = c % SLOTS
    hi = k.w_hi[:, s, :].rearrange("p (k n) -> p k n", k=8)
    lo = k.w_lo[:, s, :].rearrange("p (k n) -> p k n", k=8)
    for bank, kts in zip(banks, rows):
        for n in range(2):
            out = k.ps[:, bank, n * SEQ:(n + 1) * SEQ]
            for i, kt in enumerate(kts):
                cols = slice(n * P, (n + 1) * P)
                end = product(pe, out, (hi[:, kt, cols], lo[:, kt, cols]), act(kt), i == 0, i == len(kts) - 1)
    end.then_inc(k.chunk_done, 1)


def t_chunk(k, pe, c, kts, cols, act, out, first, end):
    s = c % SLOTS
    w = CH // len(kts)
    hi = k.w_hi[:, s, :].rearrange("p (k n) -> p k n", k=len(kts))
    lo = k.w_lo[:, s, :].rearrange("p (k n) -> p k n", k=len(kts))
    step = min(cols, 512)
    for tt in range(TT):
        for h in range(max(1, cols // 512)):
            for i, kt in enumerate(kts):
                a = [x[:, tt * P:(tt + 1) * P] for x in act(kt)]
                b = (hi[:, i, h * step:(h + 1) * step], lo[:, i, h * step:(h + 1) * step])
                ins = product(pe, out(tt, h), a, b, first and i == 0, end and i == len(kts) - 1)
    ins.then_inc(k.chunk_done, 1)


def norm_stats(k, act, layer, n):
    act.wait_ge(k.x_new.sem, k.x_new.at(layer, n))
    for tt in range(TT):
        act.activation(k.aL[:, 4 * tt:4 * tt + 4, :], k.x[:, tt, :].rearrange("p (a b) -> p a b", a=4),
                       ACT.Square, accum_out=k.ss[:, tt:tt + 1]).then_inc(k.ss_ready.sem, 1)


def norm_diag(k, dve, ch, layer, n):
    dve.wait_ge(k.ss_ready.sem, k.ss_ready.at(layer, TT * (n + 1)))
    dve.tensor_scalar(k.var[:, 0:TT], k.ss[:, 0:TT], 1.0 / DM, EPS, ALU.mult, ALU.add).then_inc(ch.sem, ch.one())
    dve.wait_ge(ch.sem, ch.at(layer))
    rsqrt(dve, ch, layer, k.rstd[:, 0:TT], k.var[:, 0:TT], k.tmp[:, 0:TT])
    dve.tensor_scalar(k.diag[:, 0, :], k.ident, k.rstd[:, 0:1], None, ALU.mult).then_inc(ch.sem, ch.one())
    dve.wait_ge(ch.sem, ch.at(layer))
    dve.tensor_scalar(k.diag[:, 1, :], k.ident, k.rstd[:, 1:2], None, ALU.mult).then_inc(k.diag_ready.sem, 1)


def norm_transpose(k, pe, layer, n):
    pe.wait_ge(k.diag_ready.sem, k.diag_ready.at(layer, n + 1))
    for b in range(4):
        for kk in range(2):
            for tt in range(TT):
                kt = 2 * b + kk
                ins = pe.matmul(k.ps[:, 4 + b, kk * SEQ + tt * P:kk * SEQ + (tt + 1) * P],
                                k.x[:, tt, kt * P:(kt + 1) * P], k.diag[:, tt, :], start=True, stop=True)
        ins.then_inc(k.nT_done.sem, 1)


def norm_high(k, act, layer, n, gain):
    for b in range(4):
        act.wait_ge(k.nT_done.sem, k.nT_done.at(layer, 4 * n + b + 1))
        for kk in range(2):
            kt = 2 * b + kk
            ins = act.activation(k.aH[:, kt, :], k.ps[:, 4 + b, kk * SEQ:(kk + 1) * SEQ], ACT.Copy,
                                 scale=gain[:, kt:kt + 1])
        ins.then_inc(k.aH_ready.sem, 1)


def norm_low(k, dve, layer, n, gain):
    for b in range(4):
        dve.wait_ge(k.aH_ready.sem, k.aH_ready.at(layer, 4 * n + b + 1))
        for kk in range(2):
            kt = 2 * b + kk
            ins = dve.scalar_tensor_tensor(k.aL[:, kt, :], k.ps[:, 4 + b, kk * SEQ:(kk + 1) * SEQ],
                                           gain[:, kt:kt + 1], k.aH[:, kt, :].bitcast(F32),
                                           ALU.mult, ALU.subtract)
        ins.then_inc(k.a_ready.sem, 1)


def residual(k, dve):
    for tt in range(TT):
        ins = dve.tensor_tensor(k.x[:, tt, :].rearrange("p (a b) -> p a b", a=2),
                                k.x[:, tt, :].rearrange("p (a b) -> p a b", a=2),
                                k.ps[:, 4 + 2 * tt:6 + 2 * tt, :], ALU.add)
    ins.then_inc(k.x_new.sem, 1)


def head_slot(h):
    return h // 2, h % 2


def first_block(nc, k, d, sems):
    with ExitStack() as ctx:
        def sb(name, shape, dt=F32):
            return ctx.enter_context(nc.sbuf_tensor(name, shape, dt))

        def sig(name, per, start=0):
            return Signal(sems.enter_context(nc.semaphore("a_" + name)), per, start)

        st = Stream(0, CA)
        consts = sb("a_consts", [P, int(KA_END)])
        k.ident = consts[:, KA_ID:KA_ADD]
        att_add = consts[:, KA_ADD:KA_MULT]
        att_mult = consts[:, KA_MULT:KA_CAUS]
        ml_add = consts[:, KA_CAUS:KA_SEL]
        sel = consts[0:MH, KA_SEL:KA_FREQ].rearrange("p (h n) -> p h n", h=MH)
        freq = consts[:, KA_FREQ:KA_END]
        par = sb("a_par", [P, int(PA_END)])
        rows = sb("a_rows", [P, ROWS_A])
        pos_i = sb("pos_i", [P, TT], I32)
        pos_f = sb("pos_f", [P, TT])
        angle = sb("angle", [P, 4, TT, RH])
        cos, sin = sb("cos", [P, TT, RH]), sb("sin", [P, TT, RH])
        R1 = sb("R1", [P, 8 * 3 * P])
        R2 = sb("R2", [P, 8 * 3 * P])
        R3 = sb("R3", [P, 8 * (SEQ + CONV - 1)])
        qk_tok = R1[:, 0:TT * 2 * AH * AD].rearrange("p (t h d) -> p t h d", t=TT, h=2 * AH)
        logit = [R1[:, 0:AH * P].rearrange("p (h n) -> p h n", h=AH),
                 R1[:, AH * P:3 * AH * P].rearrange("p (h n) -> p h n", h=AH)]
        qkF = R2[:, 0:8 * SEQ].rearrange("p (f n) -> p f n", f=8)
        pT = R2[:, :].rearrange("p (h b n) -> p h b n", h=AH, b=3)
        z_pad = R3[:, :].rearrange("p (f n) -> p f n", f=8)
        ml_w = [R3[:, 0:MH * SEQ].rearrange("p (h n) -> p h n", h=MH),
                R3[:, MH * SEQ:MH * (SEQ + P)].rearrange("p (h n) -> p h n", h=MH)]
        v_tok = sb("v_tok", [P, TT, AH, AD + 1])
        mv_tok = sb("mv_tok", [P, TT, MH, MD])
        mqk = sb("mqk", [P, 8, SEQ])
        gates = sb("a_gates", [P, 16, SEQ])
        mo = sb("mo", [P, MH, SEQ])
        hn = sb("hn", [P, TT * MH * MD])
        ya = sb("ya", [P, TT * AH * AD])
        hn_v = hn[:, :].rearrange("p (t h d) -> p (t h) d", t=TT, h=MH)
        ya_v = ya[:, :].rearrange("p (t j e d) -> p t j e d", t=TT, j=4, e=2)
        g_rows = hn[0:MH, :].rearrange("p (a n) -> p a n", a=4)
        ones = sb("ones", [P, SEQ])
        g_tok = sb("g_tok", [P, TT, 2 * MH])
        g_tmp = sb("g_tmp", [P, 2, TT, MH])
        ml_cols = sb("ml_cols", [P, 2, TT, MH])
        exp_m = sb("exp_m", [P, TT, MH])
        small = sb("small", [P, 6, TT * MH])
        rmax = sb("rmax", [P, TT, AH])
        rsum = sb("rsum", [P, TT, AH])
        mixed = R2[:, 0:1024].rearrange("p (a n) -> p a n", a=2)
        mix_t = R2[:, 1024:1536]
        hid_r = R1[:, 0:3 * 512].rearrange("p (s n) -> p s n", s=3)
        yH = k.mixH[:, :].rearrange("p (f n) -> p f n", f=8)
        yL = k.mixL[:, :].rearrange("p (f n) -> p f n", f=8)
        hidH = k.mixH[:, 0:3 * 512].rearrange("p (s n) -> p s n", s=3)
        hidL = k.mixL[:, 0:3 * 512].rearrange("p (s n) -> p s n", s=3)

        const_loaded, par_loaded, row_loaded = sig("const_loaded", 0), sig("par_loaded", 16), sig("row_loaded", 16)
        k.x_new, k.ss_ready, k.diag_ready = sig("x_new", 2, 1), sig("ss_ready", 4), sig("diag_ready", 2)
        k.nT_done, k.aH_ready, k.a_ready = sig("nT_done", 8), sig("aH_ready", 8), sig("a_ready", 8)
        rope_ready, angle_ready, trig_ready = sig("rope_ready", 1), sig("angle_ready", 0), sig("trig_ready", 0)
        half_ready = sig("half_ready", 1)
        t_evicted, f_evicted = sig("t_evicted", 4), sig("f_evicted", 14)
        qkT_done, qkF_ready = sig("qkT_done", 4), sig("qkF_ready", 4)
        conv_ready, convt_ready, mqk_ready = sig("conv_ready", 2), sig("convt_ready", 2), sig("mqk_ready", 2)
        gate_ready, gexp_ready, lf_ready = sig("gate_ready", 1), sig("gexp_ready", 2), sig("lf_ready", 1)
        sc_done, max_ready, exp_ready, p_ready = sig("sc_done", 2), sig("max_ready", 2), sig("exp_ready", 2), sig("p_ready", 2)
        gr_done, rows_ready, nm_done, epre_ready, et_ready = (
            sig("gr_done", 1), sig("rows_ready", 1), sig("nm_done", 1), sig("epre_ready", 1), sig("et_ready", 1))
        s_done, wt_ready, num_done, num_copied = sig("s_done", 1), sig("wt_ready", 1), sig("num_done", 1), sig("num_copied", 1)
        hn_ready, hnT_done, yb_ready, ybH_ready, yb_split = (
            sig("hn_ready", 1), sig("hnT_done", 1), sig("yb_ready", 1), sig("ybH_ready", 1), sig("yb_split", 1))
        pT_done, pT_ready, pv_done, ya_ready = sig("pT_done", 3), sig("pT_ready", 3), sig("pv_done", 1), sig("ya_ready", 1)
        yaT_done, yaH_ready, ya_split = sig("yaT_done", 1), sig("yaH_ready", 1), sig("ya_split", 1)
        mix_ready, mixH_ready, mix_split = sig("mix_ready", 4), sig("mixH_ready", 4), sig("mix_split", 4)
        relu_ready, sq_ready, hidH_ready, hid_ready = (
            sig("relu_ready", FF_A), sig("sq_ready", FF_A), sig("hidH_ready", FF_A), sig("hid_ready", FF_A))
        dve_chain = sig("dve_chain", DVE_A)
        fin = sig("fin", 0)
        block = ctx.enter_context(nc.Block())

        FFC = CA - 2 * FF_A
        GF = [8, 9, 10, 11] + [13, 14] + list(range(15, 23))

        def up_chunk(j):
            return FFC + (j if j < 2 else 2 * j - 2)

        def down_chunk(j):
            return FFC + (3 + 2 * j if j < FF_A - 2 else 2 * FF_A - 2 + j - (FF_A - 2))

        @block.gpsimd
        def _(pool):
            pool.dma_start(consts[:, :], d.consts_a).then_inc(const_loaded.sem, 16)
            pool.dma_start(pos_i[:, :], d.positions).then_inc(const_loaded.sem, 16)
            pool.dma_start(rows[:, :], d.rows_a[0:1, :].rearrange("a n -> (a n)").partition_broadcast(P))\
                .then_inc(row_loaded.sem, 16)
            pool.dma_start(par[:, :], d.par_a[0:P, :]).then_inc(par_loaded.sem, 16)
            for l in range(1, DEPTH):
                pool.wait_ge(t_evicted.sem, t_evicted.at(l - 1, 4))
                pool.wait_ge(gate_ready.sem, gate_ready.at(l - 1, 1))
                pool.dma_start(rows[:, :], d.rows_a[l:l + 1, :].rearrange("a n -> (a n)").partition_broadcast(P))\
                    .then_inc(row_loaded.sem, 16)
                pool.wait_ge(k.a_ready.sem, k.a_ready.at(l - 1, 8))
                pool.dma_start(par[:, :], d.par_a[l * P:(l + 1) * P, :]).then_inc(par_loaded.sem, 16)
            pool.wait_ge(t_evicted.sem, t_evicted.at(DEPTH - 1, 4))
            pool.wait_ge(gate_ready.sem, gate_ready.at(DEPTH - 1, 1))
            pool.dma_start(rows[:, 0:DM], d.final_norm_w.partition_broadcast(P)).then_inc(row_loaded.sem, 16)

        @block.sync
        def _(sp):
            for tt in range(TT):
                sp.dma_start(k.x[:, tt, :], d.x[tt * P:(tt + 1) * P, :]).then_inc(k.x_loaded, 16)
            for s in range(SLOTS):
                sp.dma_start(k.raw[:, s, :], d.w_a[s]).then_inc(k.raw_loaded[s], 16)
            with sp.Fori(1, DEPTH * CA // SLOTS) as g:
                for s in range(SLOTS):
                    sp.wait_ge(k.lo_ready, g * SLOTS + (s - SLOTS + 1))
                    sp.dma_start(k.raw[:, s, :], d.w_a[g * SLOTS + s]).then_inc(k.raw_loaded[s], 16)

        @block.scalar
        def _(act):
            act.wait_ge(k.x_loaded, 16 * TT)
            act.wait_ge(angle_ready.sem, angle_ready.at(0, 1))
            act.activation(sin[:, :, :], angle[:, 0], ACT.Sin).then_inc(trig_ready.sem, 1)
            act.activation(cos[:, :, :], angle[:, 1], ACT.Sin).then_inc(trig_ready.sem, 1)
            with act.Fori(0, DEPTH) as l:
                high = Splitter(split_high, k, act, st, l)
                norm_stats(k, act, l, 0)
                high.upto(1)
                act.wait_ge(par_loaded.sem, par_loaded.at(l, 16))
                norm_high(k, act, l, 0, par[:, PA_NORM:PA_MLP])
                act.wait_ge(half_ready.sem, half_ready.at(l, 1))

                high.upto(8)
                for b in range(4):
                    act.wait_ge(qkT_done.sem, qkT_done.at(l, b + 1))
                    act.activation(qkF[:, 2 * b:2 * b + 2, :].rearrange("p f n -> p (f n)"), k.ps[:, 4 + b, :],
                                   ACT.Copy).then_inc(qkF_ready.sem, 1)

                def conv_in(i):
                    high.upto(10 + i)
                    act.wait_ge(k.chunk_done, st.results(l, 8 + i))
                    for n in range(2):
                        f = 2 * i + n
                        ins = act.activation(z_pad[:, f, CONV - 1:], k.ps[:, i % 2, n * SEQ:(n + 1) * SEQ],
                                             ACT.Identity, bias=par[:, PA_BQK + f:PA_BQK + f + 1])
                    ins.then_inc(f_evicted.sem, 1)

                def conv_tanh(j):
                    act.wait_ge(conv_ready.sem, conv_ready.at(l, j + 1))
                    act.activation((hn, ya)[j][:, :], mqk[:, 4 * j:4 * j + 4, :].rearrange("p f n -> p (f n)"),
                                   ACT.Tanh, scale=0.5).then_inc(convt_ready.sem, 1)

                conv_in(0)
                conv_in(1)
                conv_in(2)
                conv_tanh(0)
                conv_in(3)
                high.upto(14)
                act.wait_ge(gate_ready.sem, gate_ready.at(l, 1))
                act.activation(g_tmp[:, 1], g_tmp[:, 0], ACT.Exp, scale=-1.0).then_inc(gexp_ready.sem, 1)
                act.wait_ge(gexp_ready.sem, gexp_ready.at(l, 1))
                act.activation(g_tmp[:, 1], g_tmp[:, 1], ACT.Ln, bias=1.0).then_inc(gexp_ready.sem, 1)
                conv_tanh(1)

                def soft(qt):
                    act.wait_ge(max_ready.sem, max_ready.at(l, 2 - qt))
                    for h in range(AH):
                        ins = act.activation(logit[qt][:, h, :], logit[qt][:, h, :], ACT.Exp,
                                             bias=rmax[:, qt, h:h + 1], scale=AD ** -0.5)
                    ins.then_inc(exp_ready.sem, 1)

                def gate_in(i):
                    c = 13 + i
                    act.wait_ge(k.chunk_done, st.results(l, c))
                    for n in range(2):
                        f = 2 * i + n
                        out = mo[:, f, :] if i < 2 else gates[:, f - 4, :]
                        ins = act.activation(out, k.ps[:, i % 2, n * SEQ:(n + 1) * SEQ], ACT.Tanh,
                                             bias=par[:, PA_BMO + f:PA_BMO + f + 1], scale=0.5)
                    ins.then_inc(f_evicted.sem, 1)
                    high.upto(c + 3)

                soft(1)
                high.upto(15)
                soft(0)
                gate_in(0)
                gate_in(1)
                act.wait_ge(epre_ready.sem, epre_ready.at(l, 1))
                for s in range(TT):
                    for h in range(MH):
                        act.activation(ml_w[s][:, h, :], ml_w[s][:, h, :], ACT.Exp, bias=ml_cols[:, 0, s, h:h + 1])
                act.activation(exp_m[:, :, :], ml_cols[:, 1], ACT.Exp, scale=-1.0).then_inc(et_ready.sem, 1)
                gate_in(2)
                gate_in(3)
                act.wait_ge(num_done.sem, num_done.at(l, 1))
                for tt in range(TT):
                    ins = act.activation(hn[:, tt * 512:(tt + 1) * 512], k.ps[:, 2 + tt, :], ACT.Copy)
                ins.then_inc(num_copied.sem, 1)
                gate_in(4)

                def weights_T(i):
                    act.wait_ge(pT_done.sem, pT_done.at(l, i + 1))
                    for n, b in enumerate(((4, 5), (6, 7), (4, 5))[i]):
                        src = k.ps[:, b, :]
                        if i < 2:
                            dst = pT[:, 4 * i + 2 * n:4 * i + 2 * n + 2, 1:3, :]
                            src = src.rearrange("p (h b n) -> p h b n", h=2, b=2)
                        else:
                            dst = pT[:, 4 * n:4 * n + 4, 0, :]
                            src = src.rearrange("p (h n) -> p h n", h=4)
                        ins = act.activation(dst, src, ACT.Copy)
                    ins.then_inc(pT_ready.sem, 1)

                weights_T(0)
                weights_T(1)
                gate_in(5)
                weights_T(2)
                gate_in(6)
                gate_in(7)
                act.wait_ge(yb_ready.sem, yb_ready.at(l, 1))
                act.activation(yH[:, 4:8, :].rearrange("p f n -> p (f n)"), hn[:, :], ACT.Copy).then_inc(ybH_ready.sem, 1)
                gate_in(8)
                act.wait_ge(yaT_done.sem, yaT_done.at(l, 1))
                for b in range(2):
                    ins = act.activation(yH[:, 2 * b:2 * b + 2, :].rearrange("p f n -> p (f n)"), k.ps[:, 4 + b, :], ACT.Copy)
                ins.then_inc(yaH_ready.sem, 1)
                gate_in(9)
                for i in range(4):
                    high.upto(26 + i)
                    act.wait_ge(mix_ready.sem, mix_ready.at(l, i + 1))
                    act.activation(k.aH[:, 2 * i:2 * i + 2, :].rearrange("p f n -> p (f n)"), mixed[:, i % 2, :],
                                   ACT.Copy, scale=0.5).then_inc(mixH_ready.sem, 1)
                high.upto(FFC + 1)
                norm_stats(k, act, l, 1)
                norm_high(k, act, l, 1, par[:, PA_MLP:PA_BQK])
                high.upto(FFC + 2)

                def unit(j, c_up, highs, trips=0, q=0):
                    act.wait_ge(k.chunk_done, st.results(l, c_up, trips))
                    if j >= 3:
                        act.wait_ge(hid_ready.sem, l * FF_A + q + (j - 2))
                    act.activation(hid_r[:, j % 3, :], k.ps[:, j % 3, :], ACT.Relu).then_inc(relu_ready.sem, 1)
                    if highs:
                        split_high(k, act, st, l, highs[0], trips)
                    act.wait_ge(sq_ready.sem, l * FF_A + q + (j + 1))
                    act.activation(hidH[:, j % 3, :], hid_r[:, j % 3, :], ACT.Copy).then_inc(hidH_ready.sem, 1)
                    for c in highs[1:]:
                        split_high(k, act, st, l, c, trips)

                unit(0, up_chunk(0), [FFC + 3])
                unit(1, up_chunk(1), [FFC + 4])
                unit(2, up_chunk(2), [FFC + 5, FFC + 6])
                with act.Fori(0, 4) as q:
                    for j in range(3, 6):
                        unit(j, up_chunk(j), [up_chunk(j) + 3, up_chunk(j) + 4], q * 2, q * 3)
                unit(15, up_chunk(15), [up_chunk(15) + 3])
            norm_stats(k, act, DEPTH, 0)

        @block.vector
        def _(dve):
            ch = Chain(k.pre_chain, 0)
            dve.memset(ones[:, :], 1.0).then_inc(k.pre_chain, 1)
            ch.n = 1
            dve.memset(v_tok[:, :, :, AD:AD + 1], 1.0).then_inc(ch.sem, ch.one())
            dve.wait_ge(const_loaded.sem, const_loaded.at(0, 32))
            dve.tensor_copy(pos_f[:, :], pos_i[:, :]).then_inc(ch.sem, ch.one())
            dve.wait_ge(ch.sem, ch.at(0))
            dve.tensor_tensor(angle[:, 0], last(pos_f[:, :], RH), mid(freq, TT), ALU.mult).then_inc(ch.sem, ch.one())
            dve.wait_ge(ch.sem, ch.at(0))
            magic = 12582912.0
            dve.tensor_scalar(angle[:, 2], angle[:, 0], 1.0 / (2 * math.pi), magic, ALU.mult, ALU.add).then_inc(ch.sem, ch.one())
            dve.wait_ge(ch.sem, ch.at(0))
            dve.tensor_scalar(angle[:, 2], angle[:, 2], -magic, None, ALU.add).then_inc(ch.sem, ch.one())
            two_pi = 2 * math.pi
            c1 = 6.28125
            c2 = float(np.float32(np.round((two_pi - c1) * 2 ** 21) / 2 ** 21))
            c3 = float(np.float32(two_pi - c1 - c2))
            for part in (c1, c2, c3):
                dve.wait_ge(ch.sem, ch.at(0))
                dve.scalar_tensor_tensor(angle[:, 0], angle[:, 2], -part, angle[:, 0], ALU.mult, ALU.add).then_inc(ch.sem, ch.one())
            dve.wait_ge(ch.sem, ch.at(0))
            pi = float(np.nextafter(np.float32(math.pi), np.float32(0)))
            dve.tensor_scalar(angle[:, 1], angle[:, 0], math.pi / 2, None, ALU.add).then_inc(ch.sem, ch.one())
            dve.wait_ge(ch.sem, ch.at(0))
            dve.tensor_scalar(angle[:, 3], angle[:, 1], pi, -two_pi, ALU.is_gt, ALU.mult).then_inc(ch.sem, ch.one())
            dve.wait_ge(ch.sem, ch.at(0))
            dve.tensor_tensor(angle[:, 1], angle[:, 1], angle[:, 3], ALU.add).then_inc(ch.sem, ch.one())
            dve.wait_ge(ch.sem, ch.at(0))
            dve.tensor_scalar(angle[:, 0:2], angle[:, 0:2], pi, -pi, ALU.min, ALU.max).then_inc(angle_ready.sem, 1)
            dve.wait_ge(k.x_loaded, 16 * TT)
            dve.sem_inc(k.x_new.sem, 1)

            with dve.Fori(0, DEPTH) as l:
                low = Splitter(split_low, k, dve, st, l)
                ch = Chain(dve_chain.sem, DVE_A)

                def bias_rows(n, width=512):
                    return rows[:, n * 512:n * 512 + width]

                norm_diag(k, dve, ch, l, 0)
                low.upto(1)
                dve.wait_ge(par_loaded.sem, par_loaded.at(l, 16))
                dve.memset(z_pad[:, :, 0:CONV - 1], 0.0).then_inc(ch.sem, ch.one())
                dve.tensor_scalar(par[:, PA_BMO:PA_CW], par[:, PA_BMO:PA_CW], 0.5, None, ALU.mult).then_inc(half_ready.sem, 1)
                norm_low(k, dve, l, 0, par[:, PA_NORM:PA_MLP])
                dve.wait_ge(row_loaded.sem, row_loaded.at(l, 16))
                low.upto(3)
                for n in range(4):
                    dve.wait_ge(k.chunk_done, st.results(l, 2 * n + 1))
                    for tt in range(TT):
                        src = k.ps[:, 2 * (n % 2) + tt, :]
                        if n < 2:
                            dst, src = qk_tok[:, tt, 8 * n:8 * n + 8, :], src.rearrange("p (h d) -> p h d", h=8)
                            b = bias_rows(n).rearrange("p (h d) -> p h d", h=8)
                        elif n == 2:
                            dst, src = v_tok[:, tt, :, 0:AD], src.rearrange("p (h d) -> p h d", h=8)
                            b = bias_rows(n).rearrange("p (h d) -> p h d", h=8)
                        else:
                            dst, src = mv_tok[:, tt], src.rearrange("p (h d) -> p h d", h=4)
                            b = bias_rows(n).rearrange("p (h d) -> p h d", h=4)
                        ins = dve.tensor_tensor(dst, src, b, ALU.add)
                    ins.then_inc(t_evicted.sem, 1)
                    if n == 1:
                        dve.wait_ge(trig_ready.sem, trig_ready.at(0, 2))
                        dve.wait_ge(t_evicted.sem, t_evicted.at(l, 2))
                        tmp = hn[:, :].rearrange("p (a t h r) -> p a t h r", a=4, t=TT, h=2 * AH)
                        for tt in range(TT):
                            q1, q2 = qk_tok[:, tt, :, 0:RH], qk_tok[:, tt, :, RH:2 * RH]
                            cs, sn = mid(cos[:, tt, :], 2 * AH), mid(sin[:, tt, :], 2 * AH)
                            for i, (a, b) in enumerate(((q1, cs), (q2, sn), (q2, cs), (q1, sn))):
                                dve.tensor_tensor(tmp[:, i, tt], a, b, ALU.mult).then_inc(ch.sem, ch.one())
                            dve.wait_ge(ch.sem, ch.at(l))
                            dve.tensor_tensor(q1, tmp[:, 0, tt], tmp[:, 1, tt], ALU.subtract).then_inc(ch.sem, ch.one())
                            ins = dve.tensor_tensor(q2, tmp[:, 2, tt], tmp[:, 3, tt], ALU.add)
                            if tt == 0:
                                ins.then_inc(ch.sem, ch.one())
                        ins.then_inc(rope_ready.sem, 1)
                    low.upto(2 * n + 5)

                def conv(j):
                    dve.wait_ge(f_evicted.sem, f_evicted.at(l, 2 * j + 2))
                    dve.wait_ge(ch.sem, ch.at(l))
                    for t in range(CONV):
                        for f in range(4 * j, 4 * j + 4):
                            w = par[:, PA_CW + 8 * t + f:PA_CW + 8 * t + f + 1]
                            z = z_pad[:, f, t:t + SEQ]
                            if t == 0:
                                ins = dve.tensor_scalar(mqk[:, f, :], z, w, par[:, PA_CB + f:PA_CB + f + 1],
                                                        ALU.mult, ALU.add)
                            else:
                                ins = dve.scalar_tensor_tensor(mqk[:, f, :], z, w, mqk[:, f, :], ALU.mult, ALU.add)
                            if t < CONV - 1 or f < 4 * j + 3:
                                ins.then_inc(ch.sem, ch.one())
                        if t < CONV - 1:
                            dve.wait_ge(ch.sem, ch.at(l))
                    ins.then_inc(conv_ready.sem, 1)

                def conv_silu(j):
                    dve.wait_ge(convt_ready.sem, convt_ready.at(l, j + 1))
                    v = mqk[:, 4 * j:4 * j + 4, :].rearrange("p f n -> p (f n)")
                    dve.scalar_tensor_tensor(v, (hn, ya)[j][:, :], 1.0, v, ALU.add, ALU.mult).then_inc(mqk_ready.sem, 1)

                conv(0)
                low.upto(12)
                conv_silu(0)
                conv(1)
                low.upto(13)
                dve.wait_ge(k.chunk_done, st.results(l, 12))
                dve.tensor_tensor(g_tok[:, :, :], k.ps[:, 2, 0:TT * 2 * MH].rearrange("p (t n) -> p t n", t=TT),
                                        mid(bias_rows(4, 2 * MH), TT), ALU.add).then_inc(ch.sem, ch.one())
                dve.wait_ge(ch.sem, ch.at(l))
                forget = g_tok[:, :, MH:2 * MH]
                dve.scalar_tensor_tensor(g_tmp[:, 0], forget, -1.0, forget, ALU.mult, ALU.max).then_inc(gate_ready.sem, 1)
                low.upto(14)
                conv_silu(1)
                dve.wait_ge(gexp_ready.sem, gexp_ready.at(l, 2))
                dve.scalar_tensor_tensor(forget, forget, 0.0, g_tmp[:, 1], ALU.min, ALU.subtract).then_inc(lf_ready.sem, 1)

                def masked_max(qt):
                    dve.wait_ge(sc_done.sem, sc_done.at(l, 2 - qt))
                    n = (qt + 1) * P
                    lo, banks = (0, slice(2, 4)) if qt == 0 else (P, slice(4, 8))
                    src = k.ps[:, banks, :].rearrange("p b (h n) -> p (b h) n", n=n)
                    dve.tensor_tensor(logit[qt], src, mid(att_add[:, lo:lo + n], AH), ALU.add).then_inc(ch.sem, ch.one())
                    dve.wait_ge(ch.sem, ch.at(l))
                    dve.tensor_reduce(rmax[:, qt, :], logit[qt], AX.X, ALU.max).then_inc(ch.sem, ch.one())
                    dve.wait_ge(ch.sem, ch.at(l))
                    dve.tensor_scalar(rmax[:, qt, :], rmax[:, qt, :], -(AD ** -0.5), None, ALU.mult).then_inc(max_ready.sem, 1)

                def patterns(qt):
                    dve.wait_ge(exp_ready.sem, exp_ready.at(l, 2 - qt))
                    lo, n = (0, P) if qt == 0 else (P, 2 * P)
                    dve.tensor_tensor(logit[qt], logit[qt], mid(att_mult[:, lo:lo + n], AH), ALU.mult).then_inc(p_ready.sem, 1)

                masked_max(1)
                masked_max(0)
                low.upto(15)
                dve.wait_ge(gr_done.sem, gr_done.at(l, 1))
                b_row, a_row, negM, m_row = (g_rows[:, i, :] for i in range(4))
                one4 = ones[0:MH, :]
                dve.tensor_tensor_scan(b_row, one4, k.ps[0:MH, 2, SEQ:2 * SEQ], 0.0, ALU.mult, ALU.add).then_inc(ch.sem, ch.one())
                dve.wait_ge(ch.sem, ch.at(l))
                dve.tensor_tensor(a_row, k.ps[0:MH, 2, 0:SEQ], b_row, ALU.subtract).then_inc(ch.sem, ch.one())
                dve.wait_ge(ch.sem, ch.at(l))
                dve.tensor_tensor_scan(m_row, a_row, a_row, 0.0, ALU.max, ALU.max).then_inc(ch.sem, ch.one())
                dve.wait_ge(ch.sem, ch.at(l))
                dve.tensor_scalar(negM, m_row, -1.0, None, ALU.mult).then_inc(ch.sem, ch.one())
                dve.wait_ge(ch.sem, ch.at(l))
                dve.tensor_tensor(m_row, m_row, b_row, ALU.add).then_inc(rows_ready.sem, 1)
                patterns(1)
                low.upto(16)
                dve.wait_ge(nm_done.sem, nm_done.at(l, 1))
                src = k.ps[:, 4:6, :].rearrange("p b (h n) -> p (b h) n", n=SEQ)
                dve.tensor_copy(ml_cols[:, :, :, :].rearrange("p a t h -> p (a t h)"), k.ps[:, 6, 0:2 * TT * MH]).then_inc(ch.sem, ch.one())
                dve.tensor_tensor(ml_w[0], src, mid(ml_add[:, 0:SEQ], MH), ALU.add).then_inc(ch.sem, ch.one())
                dve.tensor_tensor(ml_w[1], src[:, :, P:SEQ], mid(ml_add[:, SEQ:SEQ + P], MH), ALU.add).then_inc(epre_ready.sem, 1)
                patterns(0)
                low.upto(17)
                dve.wait_ge(s_done.sem, s_done.at(l, 1))
                dve.wait_ge(et_ready.sem, et_ready.at(l, 1))
                scale = MD ** -0.5 / 4
                dve.scalar_tensor_tensor(ml_w[0], k.ps[:, 2:4, :].rearrange("p b (h n) -> p (b h) n", n=SEQ),
                                               scale, ml_w[0], ALU.mult, ALU.mult).then_inc(ch.sem, ch.one())
                dve.scalar_tensor_tensor(ml_w[1], k.ps[:, 7, :].rearrange("p (h n) -> p h n", n=P),
                                         scale, ml_w[1], ALU.mult, ALU.mult).then_inc(wt_ready.sem, 1)
                low.upto(18)
                dve.wait_ge(num_done.sem, num_done.at(l, 1))
                den, r, q_, v_, s_, y_ = (small[:, i, :] for i in range(6))
                dve.tensor_copy(den, k.ps[:, 6, 64:64 + TT * MH]).then_inc(ch.sem, ch.one())
                dve.wait_ge(ch.sem, ch.at(l))
                dve.scalar_tensor_tensor(den, den, -1.0, den, ALU.mult, ALU.max).then_inc(ch.sem, ch.one())
                dve.wait_ge(ch.sem, ch.at(l))
                dve.tensor_tensor(den, den, exp_m[:, :, :].rearrange("p t h -> p (t h)"), ALU.max).then_inc(ch.sem, ch.one())
                dve.wait_ge(ch.sem, ch.at(l))
                dve.reciprocal(r, den).then_inc(ch.sem, ch.one())
                dve.wait_ge(num_copied.sem, num_copied.at(l, 1))
                sq = R3[:, 0:TT * MH * MD].rearrange("p (g d) -> p g d", d=MD)
                dve.tensor_tensor(sq, hn_v, hn_v, ALU.mult).then_inc(ch.sem, ch.one())
                dve.wait_ge(ch.sem, ch.at(l))
                dve.tensor_reduce(s_, sq, AX.X, ALU.add).then_inc(ch.sem, ch.one())
                dve.tensor_tensor(q_, r, r, ALU.mult).then_inc(ch.sem, ch.one())
                dve.wait_ge(ch.sem, ch.at(l))
                dve.tensor_tensor(v_, q_, s_, ALU.mult).then_inc(ch.sem, ch.one())
                dve.wait_ge(ch.sem, ch.at(l))
                dve.tensor_scalar(v_, v_, 1.0 / MD, EPS, ALU.mult, ALU.add).then_inc(ch.sem, ch.one())
                dve.wait_ge(ch.sem, ch.at(l))
                rsqrt(dve, ch, l, y_, v_, s_)
                dve.tensor_tensor(y_, y_, r, ALU.mult).then_inc(ch.sem, ch.one())
                dve.wait_ge(ch.sem, ch.at(l))
                dve.tensor_tensor(hn_v, hn_v, last(y_, MD), ALU.mult).then_inc(hn_ready.sem, 1)
                low.upto(19)
                dve.wait_ge(f_evicted.sem, f_evicted.at(l, 6))
                dve.tensor_scalar(mo[:, :, :], mo[:, :, :], 0.5, 0.5, ALU.mult, ALU.add).then_inc(ch.sem, ch.one())
                dve.wait_ge(ch.sem, ch.at(l))
                low.upto(20)
                dve.wait_ge(hnT_done.sem, hnT_done.at(l, 1))
                for h in range(MH):
                    ins = dve.scalar_tensor_tensor(hn[:, h * SEQ:(h + 1) * SEQ], k.ps[:, 2 + h // 2, (h % 2) * SEQ:(h % 2 + 1) * SEQ],
                                                   par[:, PA_MN + h:PA_MN + h + 1], mo[:, h, :], ALU.mult, ALU.mult)
                ins.then_inc(yb_ready.sem, 1)
                low.upto(21)
                dve.wait_ge(pv_done.sem, pv_done.at(l, 1))
                for qt in range(TT):
                    for par_ in range(2):
                        src = k.ps[:, 4 + 2 * qt + par_, 0:4 * (AD + 1)].rearrange("p (j d) -> p j d", j=4)
                        dve.reciprocal(rsum[:, qt, 4 * par_:4 * par_ + 4], src[:, :, AD]).then_inc(ch.sem, ch.one())
                dve.wait_ge(ch.sem, ch.at(l))
                for qt in range(TT):
                    for par_ in range(2):
                        src = k.ps[:, 4 + 2 * qt + par_, 0:4 * (AD + 1)].rearrange("p (j d) -> p j d", j=4)
                        ins = dve.tensor_tensor(ya_v[:, qt, :, par_, :], src[:, :, 0:AD],
                                                last(rsum[:, qt, 4 * par_:4 * par_ + 4], AD), ALU.mult)
                ins.then_inc(ya_ready.sem, 1)
                low.upto(22)
                dve.wait_ge(ybH_ready.sem, ybH_ready.at(l, 1))
                dve.tensor_tensor(yL[:, 4:8, :].rearrange("p f n -> p (f n)"), hn[:, :],
                                  yH[:, 4:8, :].rearrange("p f n -> p (f n)").bitcast(F32), ALU.subtract).then_inc(yb_split.sem, 1)
                low.upto(23)
                dve.wait_ge(yaH_ready.sem, yaH_ready.at(l, 1))
                dve.tensor_tensor(yL[:, 0:4, :].rearrange("p f n -> p (f n)"),
                                  k.ps[:, 4:6, :].rearrange("p b n -> p (b n)"),
                                  yH[:, 0:4, :].rearrange("p f n -> p (f n)").bitcast(F32), ALU.subtract).then_inc(ya_split.sem, 1)
                low.upto(24)
                dve.wait_ge(f_evicted.sem, f_evicted.at(l, 14))
                for i in range(4):
                    low.upto(min(24 + i + 1, FFC))
                    dve.wait_ge(k.chunk_done, st.results(l, 23 + i))
                    b = 2 * (i % 2)
                    dve.scalar_tensor_tensor(mix_t, gates[:, 2 * i:2 * i + 2, :].rearrange("p f n -> p (f n)"),
                                                   1.0, k.ps[:, b, :], ALU.add, ALU.mult).then_inc(ch.sem, ch.one())
                    dve.scalar_tensor_tensor(mixed[:, i % 2, :], gates[:, 8 + 2 * i:10 + 2 * i, :].rearrange("p f n -> p (f n)"),
                                                   1.0, k.ps[:, b + 1, :], ALU.add, ALU.mult).then_inc(ch.sem, ch.one())
                    dve.wait_ge(ch.sem, ch.at(l))
                    dve.tensor_tensor(mixed[:, i % 2, :], mixed[:, i % 2, :], mix_t, ALU.add).then_inc(mix_ready.sem, 1)
                    dve.wait_ge(mixH_ready.sem, mixH_ready.at(l, i + 1))
                    dve.scalar_tensor_tensor(k.aL[:, 2 * i:2 * i + 2, :].rearrange("p f n -> p (f n)"), mixed[:, i % 2, :], 0.5,
                                             k.aH[:, 2 * i:2 * i + 2, :].rearrange("p f n -> p (f n)").bitcast(F32),
                                             ALU.mult, ALU.subtract).then_inc(mix_split.sem, 1)
                for c in range(28, FFC):
                    low.upto(c)
                dve.wait_ge(k.chunk_done, st.results(l, FFC - 1))
                residual(k, dve)
                low.upto(FFC + 1)
                norm_diag(k, dve, ch, l, 1)
                norm_low(k, dve, l, 1, par[:, PA_MLP:PA_BQK])
                low.upto(FFC + 2)

                def unit(j, lows, trips=0, q=0):
                    dve.wait_ge(relu_ready.sem, l * FF_A + q + (j + 1))
                    r = hid_r[:, j % 3, :]
                    dve.tensor_tensor(r, r, r, ALU.mult).then_inc(sq_ready.sem, 1)
                    if lows:
                        split_low(k, dve, st, l, lows[0], trips)
                    dve.wait_ge(hidH_ready.sem, l * FF_A + q + (j + 1))
                    dve.tensor_tensor(hidL[:, j % 3, :], r, hidH[:, j % 3, :].bitcast(F32), ALU.subtract)\
                        .then_inc(hid_ready.sem, 1)
                    for c in lows[1:]:
                        split_low(k, dve, st, l, c, trips)

                unit(0, [FFC + 3])
                unit(1, [FFC + 4])
                unit(2, [FFC + 5, FFC + 6])
                with dve.Fori(0, 4) as q:
                    for j in range(3, 6):
                        unit(j, [up_chunk(j) + 3, up_chunk(j) + 4], q * 2, q * 3)
                unit(15, [up_chunk(15) + 3])
                dve.wait_ge(k.chunk_done, st.results(l, CA - 1))
                residual(k, dve)
                assert ch.n == DVE_A, ch.n
            dve.wait_ge(k.ss_ready.sem, k.ss_ready.at(DEPTH, TT))
            ch = Chain(fin.sem, 0)
            dve.tensor_scalar(k.var[:, 0:TT], k.ss[:, 0:TT], 1.0 / DM, EPS, ALU.mult, ALU.add).then_inc(ch.sem, ch.one())
            dve.wait_ge(ch.sem, ch.at(0))
            rsqrt(dve, ch, 0, k.rstd[:, 0:TT], k.var[:, 0:TT], k.tmp[:, 0:TT])
            dve.wait_ge(row_loaded.sem, row_loaded.at(DEPTH, 16))
            for tt in range(TT):
                dve.scalar_tensor_tensor(k.x[:, tt, :], k.x[:, tt, :], k.rstd[:, tt:tt + 1], rows[:, 0:DM],
                                               ALU.mult, ALU.mult).then_inc(ch.sem, ch.one())
            dve.wait_ge(ch.sem, ch.at(0))

        @block.tensor
        def _(pe):
            aop = lambda kt: (k.aH[:, kt, :], k.aL[:, kt, :])
            yop = lambda kt: (yH[:, kt, :], yL[:, kt, :])
            pe.wait_ge(k.x_loaded, 16 * TT)
            pe.sem_inc(k.chunk_done, SLOTS)
            with pe.Fori(0, DEPTH) as l:
                norm_transpose(k, pe, l, 0)
                pe.wait_ge(k.a_ready.sem, k.a_ready.at(l, 4))
                for n in range(4):
                    for half in range(2):
                        c = 2 * n + half
                        pe.wait_ge(k.lo_ready, st.count(l, c))
                        if half == 0 and n >= 2:
                            pe.wait_ge(t_evicted.sem, t_evicted.at(l, n - 1))
                        t_chunk(k, pe, c, range(4 * half, 4 * half + 4), 512, aop,
                                lambda tt, h: k.ps[:, 2 * (n % 2) + tt, :], half == 0, half == 1)
                pe.wait_ge(rope_ready.sem, rope_ready.at(l, 1))
                for b in range(4):
                    for n in range(2):
                        for tt in range(TT):
                            f = 2 * b + n
                            ins = pe.matmul(k.ps[:, 4 + b, n * SEQ + tt * P:n * SEQ + (tt + 1) * P],
                                            qk_tok[:, tt, 2 * f:2 * f + 2, :].rearrange("p h d -> p (h d)"), k.ident,
                                            start=True, stop=True)
                    ins.then_inc(qkT_done.sem, 1)

                def feature(i, c):
                    pe.wait_ge(k.lo_ready, st.count(l, c))
                    if i >= 2:
                        pe.wait_ge(f_evicted.sem, f_evicted.at(l, i - 1))
                    else:
                        pe.wait_ge(t_evicted.sem, t_evicted.at(l, 3))
                    f_chunk(k, pe, c, [i % 2], [range(8)], aop)

                for i in range(4):
                    feature(i, GF[i])
                pe.wait_ge(k.lo_ready, st.count(l, 12))
                pe.wait_ge(t_evicted.sem, t_evicted.at(l, 4))
                t_gate = lambda tt, h: k.ps[:, 2, tt * 2 * MH:(tt + 1) * 2 * MH]
                t_chunk(k, pe, 12, range(8), 2 * MH, aop, t_gate, True, True)

                pe.wait_ge(qkF_ready.sem, qkF_ready.at(l, 4))
                pe.wait_ge(gate_ready.sem, gate_ready.at(l, 1))
                for qt in (1, 0):
                    n = (qt + 1) * P
                    for h in range(AH):
                        j, e = head_slot(h)
                        if qt == 0:
                            out = k.ps[:, 2 + e, j * P:(j + 1) * P]
                        else:
                            out = k.ps[:, 4 + 2 * e + j // 2, (j % 2) * SEQ:(j % 2 + 1) * SEQ]
                        rows_ = slice(e * AD, (e + 1) * AD)
                        ins = pe.matmul(out, qkF[rows_, j, qt * P:(qt + 1) * P], qkF[rows_, 4 + j, 0:n],
                                        start=True, stop=True)
                    ins.then_inc(sc_done.sem, 1)
                feature(4, 13)
                pe.wait_ge(lf_ready.sem, lf_ready.at(l, 1))
                pe.wait_ge(max_ready.sem, max_ready.at(l, 2))
                for g in range(2):
                    for tt in range(TT):
                        ins = pe.matmul(k.ps[0:MH, 2, g * SEQ + tt * P:g * SEQ + (tt + 1) * P],
                                        g_tok[:, tt, g * MH:(g + 1) * MH], k.ident, start=True, stop=True)
                ins.then_inc(gr_done.sem, 1)
                feature(5, 14)
                pe.wait_ge(rows_ready.sem, rows_ready.at(l, 1))
                for h in range(MH):
                    pe.matmul(k.ps[:, 4 + h // 2, (h % 2) * SEQ:(h % 2 + 1) * SEQ], sel[:, h, :], g_rows[:, 2, :],
                              start=True, stop=True)
                for i, row in enumerate((1, 3)):
                    for tt in range(TT):
                        ins = pe.matmul(k.ps[:, 6, (2 * i + tt) * MH:(2 * i + tt + 1) * MH],
                                        g_rows[:, row, tt * P:(tt + 1) * P], k.ident[0:MH, 0:MH], start=True, stop=True)
                ins.then_inc(nm_done.sem, 1)
                feature(6, 15)
                pe.wait_ge(mqk_ready.sem, mqk_ready.at(l, 2))
                for h in range(MH):
                    pe.matmul(k.ps[:, 2 + h // 2, (h % 2) * SEQ:(h % 2 + 1) * SEQ], mqk[:, 4 + h, 0:P], mqk[:, h, :],
                              start=True, stop=True)
                for h in range(MH):
                    ins = pe.matmul(k.ps[:, 7, h * P:(h + 1) * P], mqk[:, 4 + h, P:SEQ], mqk[:, h, P:SEQ],
                                    start=True, stop=True)
                ins.then_inc(s_done.sem, 1)
                feature(7, 16)
                pe.wait_ge(wt_ready.sem, wt_ready.at(l, 1))
                for h in range(MH):
                    pe.matmul(k.ps[:, 2, h * P:(h + 1) * P], ml_w[0][:, h, 0:P], mv_tok[:, 0, h, :], start=True, stop=True)
                    pe.matmul(k.ps[:, 3, h * P:(h + 1) * P], ml_w[0][:, h, P:SEQ], mv_tok[:, 0, h, :], start=True, stop=False)
                    pe.matmul(k.ps[:, 3, h * P:(h + 1) * P], ml_w[1][:, h, :], mv_tok[:, 1, h, :], start=False, stop=True)
                for h in range(MH):
                    d0, d1 = (k.ps[:, 6, 64 + tt * MH + h:65 + tt * MH + h] for tt in range(TT))
                    pe.matmul(d0, ml_w[0][:, h, 0:P], ones[:, 0:1], start=True, stop=True)
                    pe.matmul(d1, ml_w[0][:, h, P:SEQ], ones[:, 0:1], start=True, stop=False)
                    ins = pe.matmul(d1, ml_w[1][:, h, :], ones[:, 0:1], start=False, stop=True)
                ins.then_inc(num_done.sem, 1)
                feature(8, 17)

                def weights_T(i):
                    for n, b in enumerate(((4, 5), (6, 7), (4, 5))[i]):
                        for s in range(4):
                            if i < 2:
                                h, kb = 4 * i + 2 * n + s // 2, s % 2
                                src = logit[1][:, h, kb * P:(kb + 1) * P]
                            else:
                                src = logit[0][:, 4 * n + s, :]
                            ins = pe.matmul(k.ps[:, b, s * P:(s + 1) * P], src, k.ident, start=True, stop=True)
                    ins.then_inc(pT_done.sem, 1)

                pe.wait_ge(p_ready.sem, p_ready.at(l, 1))
                weights_T(0)
                pe.wait_ge(hn_ready.sem, hn_ready.at(l, 1))
                weights_T(1)
                for h in range(MH):
                    for tt in range(TT):
                        ins = pe.matmul(k.ps[:, 2 + h // 2, (h % 2) * SEQ + tt * P:(h % 2) * SEQ + (tt + 1) * P],
                                        hn_v[:, tt * MH + h, :], k.ident, start=True, stop=True)
                ins.then_inc(hnT_done.sem, 1)
                feature(9, 18)
                pe.wait_ge(p_ready.sem, p_ready.at(l, 2))
                pe.wait_ge(pT_ready.sem, pT_ready.at(l, 1))
                weights_T(2)
                feature(10, 19)
                feature(11, 20)
                pe.wait_ge(pT_ready.sem, pT_ready.at(l, 3))
                for qt in range(TT):
                    for h in range(AH):
                        j, e = head_slot(h)
                        out = k.ps[:, 4 + 2 * qt + e, j * (AD + 1):(j + 1) * (AD + 1)]
                        for s in range(qt + 1):
                            ins = pe.matmul(out, pT[:, 4 * e + j, s + qt, :], v_tok[:, s, h, :], start=s == 0, stop=s == qt)
                ins.then_inc(pv_done.sem, 1)
                feature(12, 21)
                pe.wait_ge(ya_ready.sem, ya_ready.at(l, 1))
                for f in range(4):
                    for tt in range(TT):
                        ins = pe.matmul(k.ps[:, 4 + f // 2, (f % 2) * SEQ + tt * P:(f % 2) * SEQ + (tt + 1) * P],
                                        ya[:, tt * 512 + f * P:tt * 512 + (f + 1) * P], k.ident, start=True, stop=True)
                ins.then_inc(yaT_done.sem, 1)
                feature(13, 22)
                for i in range(4):
                    c = 23 + i
                    pe.wait_ge(k.lo_ready, st.count(l, c))
                    if i == 0:
                        pe.wait_ge(yb_split.sem, yb_split.at(l, 1))
                        pe.wait_ge(ya_split.sem, ya_split.at(l, 1))
                        pe.wait_ge(f_evicted.sem, f_evicted.at(l, 14))
                    if i >= 2:
                        pe.wait_ge(mix_ready.sem, mix_ready.at(l, i - 1))
                    b = 2 * (i % 2)
                    f_chunk(k, pe, c, [b, b + 1], [range(4), range(4, 8)], yop)
                t_out = lambda tt, h: k.ps[:, 4 + 2 * tt + h, :]
                for i in range(4):
                    c = 27 + i
                    pe.wait_ge(k.lo_ready, st.count(l, c))
                    pe.wait_ge(mix_split.sem, mix_split.at(l, i + 1))
                    t_chunk(k, pe, c, range(2 * i, 2 * i + 2), DM, aop, t_out, i == 0, i == 3)
                norm_transpose(k, pe, l, 1)

                def up(j, c, trips=0, q=0):
                    pe.wait_ge(k.lo_ready, st.count(l, c, trips))
                    if j >= 3:
                        pe.wait_ge(relu_ready.sem, l * FF_A + q + (j - 2))
                    f_chunk(k, pe, c, [j % 3], [range(8)], aop)

                def down(j, c, trips=0, q=0):
                    pe.wait_ge(k.lo_ready, st.count(l, c, trips))
                    pe.wait_ge(hid_ready.sem, l * FF_A + q + (j + 1))
                    hid = lambda kt: [x[:, j % 3, kt * SEQ:(kt + 1) * SEQ] for x in (hidH, hidL)]
                    t_chunk(k, pe, c, range(2), DM, hid, t_out, j == 0, j == FF_A - 1)

                pe.wait_ge(k.a_ready.sem, k.a_ready.at(l, 8))
                up(0, up_chunk(0))
                up(1, up_chunk(1))
                up(2, up_chunk(2))
                down(0, down_chunk(0))
                with pe.Fori(0, 4) as q:
                    for j in range(1, 4):
                        up(j + 2, up_chunk(j + 2), q * 2, q * 3)
                        down(j, down_chunk(j), q * 2, q * 3)
                up(15, up_chunk(15))
                for j in range(13, 16):
                    down(j, down_chunk(j))


(PB_N1, PB_NM, PB_N2, PB_DW, PB_CB, PB_LG, PB_LB, PB_PS, PB_GB, PB_WI, PB_WS, PB_PW, PB_VG, PB_END) = np.cumsum(
    [0, 8, 8, 8, 2 * TAPS, 2, 2, 2, 2, 4, 8 * IH, 4 * P, 2 * 64, 0])
KB_ID, KB_ADD, KB_CNT, KB_TRI, KB_HOT, KB_END = np.cumsum([0, P, 3 * P, 2 * SEQ, P, 2 * SEQ])
POOL_PAD = 16
CONV_PAD = TAPS - 1
POOL_TAPS = 16
OUT_OF_REACH = -3e38
TAKEN = float(np.float32(-3.3e38))
DVE_B = 218
POOL_B = 55


def second_block(nc, k, d, sems):
    with ExitStack() as ctx:
        def sb(name, shape, dt=F32):
            return ctx.enter_context(nc.sbuf_tensor(name, shape, dt))

        def sig(name, per, start=0):
            return Signal(sems.enter_context(nc.semaphore("b_" + name)), per, start)

        st = Stream(DEPTH * CA, CB)
        consts = sb("b_consts", [P, int(KB_HOT)])
        k.ident = consts[:, KB_ID:KB_ADD]
        reach = consts[:, KB_ADD:KB_CNT]
        inv_count = consts[:, KB_CNT:KB_TRI].rearrange("p (f n) -> p f n", f=2)
        tri = consts[:, KB_TRI:KB_HOT]
        par = sb("b_par", [P, int(PB_END)])
        wi = par[:, PB_WI:PB_WS].rearrange("p (k n) -> p k n", k=KT)
        ws = par[:, PB_WS:PB_PW].rearrange("p (g n) -> p g n", g=4)
        pw = par[:, PB_PW:PB_VG].rearrange("p (j n) -> p j n", j=2)
        v_gain = sb("v_gain", [P, BW])
        gain_row = sb("gain_row", [P, DM])
        bias = sb("bias", [P, BH, 3 * P])
        gates = sb("b_gates", [P, NBR * 8, SEQ])
        GU = sb("GU", [P, TT * 3 * BW])
        uv = GU[:, 0:TT * 2 * BW].rearrange("p (t n) -> p t n", t=TT)
        vn = GU[:, TT * 2 * BW:].rearrange("p (t n) -> p t n", t=TT)
        pT = GU[:, :].rearrange("p (h b n) -> p h b n", h=BH, b=3)
        hid_r = GU[:, 0:2 * 512].rearrange("p (s n) -> p s n", s=2)
        y0 = sb("y0", [P, TT, BW])
        xc = y0
        qkF = sb("b_qkF", [P, 4, SEQ])
        v_tok = sb("b_v_tok", [P, TT, BH, BD + 1])
        idxF = sb("idxF", [P, 2, SEQ])
        RL = sb("RL", [P, IH * 3 * P])
        rel = RL[:, :].rearrange("p (h n) -> p h n", h=IH)
        logit = rel
        mixed = RL[:, 0:1024].rearrange("p (a n) -> p a n", a=2)
        mix_t = RL[:, 1024:1536]
        post_t = RL[:, 0:DM]
        score = sb("score", [P, 3 * P])
        keep = sb("keep", [P, 3 * P])
        top8 = sb("top8", [P, TT, 8])
        w_idx = sb("w_idx", [P, TT, IH])
        rmax = sb("b_rmax", [P, TT, BH])
        rsum = sb("b_rsum", [P, TT, BH])
        yb2 = sb("yb2", [P, TT, BW])
        pz = sb("pz", [P, 2, POOL_PAD + SEQ])
        sum2 = sb("sum2", [P, 2, POOL_PAD + SEQ])
        sum4 = sb("sum4", [P, 2, POOL_PAD + SEQ])
        sum8 = sb("sum8", [P, 1, POOL_PAD + SEQ])
        pooled = sb("pooled", [P, 2, SEQ])
        conv_x = sb("conv_x", [P, 2, CONV_PAD + SEQ])
        conv_y = sb("conv_y", [P, 2, SEQ])
        conv_p = sum4[:, :, 0:SEQ]
        weighed = [pooled[:, :, :], sum2[:, :, 0:SEQ]]
        cstat = sb("cstat", [P, 4, TT])
        vstat = sb("vstat", [P, 4, TT])
        pss = sb("pss", [P, 4, TT])
        yH = k.mixH[:, :].rearrange("p (f n) -> p f n", f=8)
        yL = k.mixL[:, :].rearrange("p (f n) -> p f n", f=8)
        hidH = k.mixH[:, 0:2 * 512].rearrange("p (s n) -> p s n", s=2)
        hidL = k.mixL[:, 0:2 * 512].rearrange("p (s n) -> p s n", s=2)
        flat = lambda v: v.rearrange("p f n -> p (f n)")
        hot = flat(gates[0:32, 0:2, :])
        rel_rep = flat(gates[0:32, 2:4, :]).rearrange("p (h n) -> p h n", h=BH)
        rel_sb = gates[0:32, 4, 0:BH]
        line = gates[:, 8:16, :].rearrange("p (h a) n -> p h (a n)", h=BH)

        const_loaded, par_loaded, row_loaded, bias_moved = (
            sig("const_loaded", 48), sig("par_loaded", 32), sig("row_loaded", 48), sig("bias_moved", 0))
        k.x_new, k.ss_ready, k.diag_ready = sig("x_new", 3, 1), sig("ss_ready", 6), sig("diag_ready", 3)
        k.nT_done, k.aH_ready, k.a_ready = sig("nT_done", 12), sig("aH_ready", 12), sig("a_ready", 12)
        pss_ready = sig("pss_ready", 6)
        rel_rep_ready, line_done, line_ready = sig("rel_rep_ready", 0), sig("line_done", 0), sig("line_ready", 0)
        silu_ready, gated_ready, hidH_ready, hid_ready = (
            sig(n, 2 * FF_B) for n in ("silu_ready", "gated_ready", "hidH_ready", "hid_ready"))
        gelu_ready, vss_ready, vn_ready, gm_done, y0_ready, y0T_done, y0H_ready, y0_split = (
            sig(n, p) for n, p in (("gelu_ready", 2), ("vss_ready", 2), ("vn_ready", 1), ("gm_done", 1), ("y0_ready", 1),
                                   ("y0T_done", 1), ("y0H_ready", 1), ("y0_split", 1)))
        wi_done, wi_ready, rel_done, rel_ready = (sig(n, 1) for n in ("wi_done", "wi_ready", "rel_done", "rel_ready"))
        f_evicted, hc_ready, conv_done, pool_ready, taps_ready, conv_rest = (
            sig("f_evicted", 22), sig("hc_ready", 1), sig("conv_done", 1), sig("pool_ready", 1),
            sig("taps_ready", 1), sig("conv_rest", 1))
        ct_done, xc_ready, css_ready, cdiag_ready, lnT_done, ln_ready, lt_ready, y3_ready, y3H_ready, y3_split = (
            sig(n, 2 if n == "css_ready" else 1) for n in (
                "ct_done", "xc_ready", "css_ready", "cdiag_ready", "lnT_done", "ln_ready", "lt_ready", "y3_ready",
                "y3H_ready", "y3_split"))
        sc_done, l_ready, max_ready, exp_ready = sig("sc_done", 2), sig("l_ready", 2), sig("max_ready", 2), sig("exp_ready", 2)
        pT_done, pT_ready, pv_done, y2_ready, y2T_done, y2H_ready, y2_split = (
            sig(n, p) for n, p in (("pT_done", 2), ("pT_ready", 2), ("pv_done", 1), ("y2_ready", 1), ("y2T_done", 1),
                                   ("y2H_ready", 1), ("y2_split", 1)))
        pmm_done, y1H_ready, y1_split = (sig(n, 1) for n in ("pmm_done", "y1H_ready", "y1_split"))
        mix_ready, mixH_ready, mix_split = (sig(n, 4) for n in ("mix_ready", "mixH_ready", "mix_split"))
        dve_chain, pool_chain, pool_pre = sig("dve_chain", DVE_B), sig("pool_chain", POOL_B), sig("pool_pre", 0)
        block = ctx.enter_context(nc.Block())

        F0 = (0, CB - 3 * FF_B)
        M0 = 3 * FF_B
        G0 = M0 + 9
        BR = M0 + 25
        WO = BR + 4

        def a_chunk(f, j):
            return F0[f] + (3 * j - 1 if j else 0)

        def b_chunk(f, j):
            return F0[f] + (3 * j if j else 1)

        def down_chunk(f, j):
            return F0[f] + (3 * j + 4 if j < FF_B - 1 else 3 * FF_B - 1)

        @block.gpsimd
        def _(pool):
            pool.dma_start(hot, d.consts_b[0:32, KB_HOT:KB_END]).then_inc(const_loaded.sem, 16)
            pool.dma_start(rel_sb, d.rel_bias).then_inc(const_loaded.sem, 16)
            pool.dma_start(consts[:, :], d.consts_b[:, 0:KB_HOT]).then_inc(const_loaded.sem, 16)
            pool.dma_start(par[:, :], d.par_b[0:P, :]).then_inc(par_loaded.sem, 16)
            pool.dma_start(v_gain[:, :], d.v_gain[0].partition_broadcast(P)).then_inc(par_loaded.sem, 16)
            pool.dma_start(gain_row[:, :], d.post_gains[0].partition_broadcast(P)).then_inc(row_loaded.sem, 16)
            pool.wait_ge(const_loaded.sem, const_loaded.at(0, 48))
            pool.wait_ge(line_ready.sem, line_ready.at(0, 1))
            pool.dma_start(d.bias_line, line).then_inc(bias_moved.sem, 16)
            pool.wait_ge(bias_moved.sem, bias_moved.at(0, 16))
            for h in range(BH):
                j, e = head_slot(h)
                for qt in range(TT):
                    n = (qt + 1) * P
                    lo = 0 if qt == 0 else P
                    skew = bass.AP(tensor=d.bias_line.tensor, offset=h * 2 * SEQ + SEQ - 1 - qt * P,
                                   ap=[[BH * 2 * SEQ - 1, P], [1, n]])
                    pool.dma_start(bias[:, 2 * e + j, lo:lo + n], skew).then_inc(bias_moved.sem, 16)
            zc = Chain(pool_pre.sem, 0)
            pool.memset(pz[:, :, 0:POOL_PAD], 0.0).then_inc(zc.sem, zc.one())
            pool.wait_ge(zc.sem, zc.at(0))
            pool.memset(conv_x[:, :, 0:CONV_PAD], 0.0).then_inc(zc.sem, zc.one())
            pool.wait_ge(zc.sem, zc.at(0))
            with pool.Fori(0, DEPTH) as l:
                ch = Chain(pool_chain.sem, POOL_B)
                value = held(pool, par_loaded.at(l, 32))
                pool.wait_ge(const_loaded.sem, 48)
                pool.wait_ge(par_loaded.sem, value)
                taps = par[:, PB_DW:PB_CB]
                pool.tensor_scalar(taps, taps, 0.5, None, ALU.mult).then_inc(taps_ready.sem, 1)
                pool.wait_ge(taps_ready.sem, taps_ready.at(l, 1))
                pool.wait_ge(k.x_new.sem, k.x_new.at(l, 1))
                pool.dma_start(gain_row[:, :], d.post_gains[l * 3 + 1].partition_broadcast(P)).then_inc(row_loaded.sem, 16)
                value = held(pool, hc_ready.at(l, 1))
                pool.wait_ge(const_loaded.sem, 48)
                pool.wait_ge(hc_ready.sem, value)

                def weigh(t):
                    for f in range(2):
                        w = par[:, PB_DW + 2 * t + f:PB_DW + 2 * t + f + 1]
                        value = held(pool, ch.at(l, f))
                        pool.wait_ge(const_loaded.sem, 48)
                        pool.wait_ge(ch.sem, value)
                        if t == 0:
                            pool.tensor_scalar(conv_p[:, f, :], conv_x[:, f, 0:SEQ], w, par[:, PB_CB + f:PB_CB + f + 1],
                                                     ALU.mult, ALU.add).then_inc(ch.sem, ch.one())
                        else:
                            pool.tensor_scalar(weighed[t % 2][:, f, :], conv_x[:, f, t:t + SEQ], w, None, ALU.mult).then_inc(ch.sem, ch.one())

                weigh(0)
                weigh(1)
                for t in range(1, POOL_TAPS):
                    if t + 1 < POOL_TAPS:
                        weigh(t + 1)
                        pool.wait_ge(ch.sem, ch.at(l, 2))
                    else:
                        pool.wait_ge(ch.sem, ch.at(l))
                    pool.tensor_tensor(conv_p, conv_p, weighed[t % 2], ALU.add).then_inc(ch.sem, ch.one())
                pool.wait_ge(ch.sem, ch.at(l))
                pool.wait_ge(conv_rest.sem, conv_rest.at(l, 1))
                pool.tensor_tensor(conv_y[:, :, :], conv_y[:, :, :], conv_p, ALU.add).then_inc(conv_done.sem, 1)
                pool.wait_ge(conv_done.sem, conv_done.at(l, 1))
                pool.wait_ge(f_evicted.sem, f_evicted.at(l, 3))
                N = POOL_PAD + SEQ
                add = lambda o, a, s, lo: pool.tensor_tensor(o[:, :, lo:N], a[:, :, lo:N], a[:, :, lo - s:N - s], ALU.add).then_inc(ch.sem, ch.one())
                add(sum2, pz, 1, 1)
                pool.wait_ge(ch.sem, ch.at(l))
                add(sum4, sum2, 2, 3)
                pool.wait_ge(ch.sem, ch.at(l))
                pool.tensor_tensor(pooled[0:64, 0, :], sum2[0:64, 0, POOL_PAD:], inv_count[0:64, 0, :], ALU.mult).then_inc(ch.sem, ch.one())
                pool.wait_ge(ch.sem, ch.at(l))
                add(sum8, sum4[:, 1:2, :], 4, 7)
                pool.wait_ge(ch.sem, ch.at(l))
                pool.tensor_tensor(pooled[64:P, 0, :], sum4[64:P, 0, POOL_PAD:], inv_count[64:P, 0, :], ALU.mult).then_inc(ch.sem, ch.one())
                pool.wait_ge(ch.sem, ch.at(l))
                add(sum2[:, 1:2, :], sum8, 8, 15)
                pool.wait_ge(ch.sem, ch.at(l))
                pool.tensor_tensor(pooled[0:64, 1, :], sum8[0:64, 0, POOL_PAD:], inv_count[0:64, 1, :], ALU.mult).then_inc(ch.sem, ch.one())
                pool.wait_ge(ch.sem, ch.at(l))
                pool.tensor_tensor(pooled[64:P, 1, :], sum2[64:P, 1, POOL_PAD:], inv_count[64:P, 1, :], ALU.mult).then_inc(ch.sem, ch.one())
                pool.wait_ge(ch.sem, ch.at(l))
                pool.tensor_tensor(pooled[:, :, :], pooled[:, :, :], pz[:, :, POOL_PAD:], ALU.subtract).then_inc(pool_ready.sem, 1)
                pool.wait_ge(k.x_new.sem, k.x_new.at(l, 2))
                pool.dma_start(gain_row[:, :], d.post_gains[l * 3 + 2].partition_broadcast(P)).then_inc(row_loaded.sem, 16)
                pool.wait_ge(k.a_ready.sem, k.a_ready.at(l, 12))
                pool.dma_start(par[:, :], d.par_b[bass.ds((l + 1) * P, P), :]).then_inc(par_loaded.sem, 16)
                pool.dma_start(v_gain[:, :], d.v_gain[l + 1].partition_broadcast(P)).then_inc(par_loaded.sem, 16)
                pool.wait_ge(k.x_new.sem, k.x_new.at(l, 3))
                pool.dma_start(gain_row[:, :], d.post_gains[l * 3 + 3].partition_broadcast(P)).then_inc(row_loaded.sem, 16)
                assert ch.n == POOL_B, ("pool", ch.n)
            pool.wait_ge(par_loaded.sem, par_loaded.at(DEPTH, 32))
            pool.wait_ge(row_loaded.sem, row_loaded.at(DEPTH, 16))

        @block.sync
        def _(sp):
            with sp.Fori(0, DEPTH * CB // SLOTS) as g:
                for s in range(SLOTS):
                    sp.wait_ge(k.lo_ready, g * SLOTS + (DEPTH * CA + s - SLOTS + 1))
                    sp.dma_start(k.raw[:, s, :], d.w_b[g * SLOTS + s]).then_inc(k.raw_loaded[s], 16)
            sp.wait_ge(k.x_new.sem, k.x_new.at(DEPTH, 0))
            for tt in range(TT):
                sp.dma_start(d.out[tt * P:(tt + 1) * P, :], k.x[:, tt, :]).then_inc(k.stored, 16)
            sp.wait_ge(k.stored, 16 * TT)

        @block.scalar
        def _(act):
            act.wait_ge(const_loaded.sem, const_loaded.at(0, 48))
            act.wait_ge(line_done.sem, line_done.at(0, 1))
            for h in range(BH):
                ins = act.activation(line[:, h, :], k.ps[:, h, :], ACT.Copy)
            ins.then_inc(line_ready.sem, 1)

            def mlp(l, high, f):
                def unit(j, highs, trips=0, q=0):
                    act.wait_ge(k.chunk_done, st.results(l, a_chunk(f, j), trips))
                    if j >= 2:
                        act.wait_ge(hid_ready.sem, (l * 2 + f) * FF_B + q + (j - 1))
                    act.activation(hid_r[:, j % 2, :], k.ps[:, 2 * (j % 2), :], ACT.Silu).then_inc(silu_ready.sem, 1)
                    for c in highs[:2]:
                        split_high(k, act, st, l, c, trips)
                    act.wait_ge(gated_ready.sem, (l * 2 + f) * FF_B + q + (j + 1))
                    act.activation(hidH[:, j % 2, :], hid_r[:, j % 2, :], ACT.Copy).then_inc(hidH_ready.sem, 1)
                    for c in highs[2:]:
                        split_high(k, act, st, l, c, trips)

                first = F0[f]
                unit(0, [first + 3, first + 4])
                with act.Fori(0, 4) as q:
                    for j in (1, 2):
                        unit(j, [first + 3 * j + i for i in (2, 3, 4)], q * 2, q * 2)
                unit(9, [first + 3 * 9 + i for i in (2, 3, 4)])
                unit(10, [first + 3 * 10 + 2])

            def post_stats(l, n, c):
                act.wait_ge(k.chunk_done, st.results(l, c))
                for tt in range(TT):
                    act.activation(k.aL[:, 4 * tt:4 * tt + 4, :].rearrange("p (b a) n -> p b (a n)", b=2),
                                   k.ps[:, 4 + 2 * tt:6 + 2 * tt, :], ACT.Square, accum_out=pss[:, 0, tt:tt + 1])\
                       .then_inc(pss_ready.sem, 1)

            with act.Fori(0, DEPTH) as l:
                high = Splitter(split_high, k, act, st, l)
                norm_stats(k, act, l, 0)
                high.upto(1)
                act.wait_ge(par_loaded.sem, par_loaded.at(l, 32))
                norm_high(k, act, l, 0, par[:, PB_N1:PB_NM])
                high.upto(F0[0] + 2)
                mlp(l, high, 0)
                high.next = M0
                post_stats(l, 0, M0 - 1)
                norm_stats(k, act, l, 1)
                high.upto(M0 + 1)
                norm_high(k, act, l, 1, par[:, PB_NM:PB_N2])
                high.upto(M0 + 3)
                act.wait_ge(k.chunk_done, st.results(l, M0 + 1))
                for tt in range(TT):
                    act.activation(uv[:, tt, :], k.ps[:, 2 + tt, :], ACT.Gelu_apprx_tanh).then_inc(gelu_ready.sem, 1)
                act.wait_ge(gelu_ready.sem, gelu_ready.at(l, 2))
                for tt in range(TT):
                    act.activation(conv_y[:, tt, :], uv[:, tt, BW:], ACT.Square, accum_out=vstat[:, 0, tt:tt + 1])\
                       .then_inc(vss_ready.sem, 1)
                high.upto(M0 + 4)
                act.wait_ge(k.chunk_done, st.results(l, M0 + 2))
                act.activation(v_tok[:, :, :, 0:BD], k.ps[:, 0, :].rearrange("p (t h n) -> p t h n", t=TT, h=BH), ACT.Copy)\
                   .then_inc(f_evicted.sem, 1)
                high.upto(M0 + 6)
                act.wait_ge(k.chunk_done, st.results(l, M0 + 4))
                act.activation(flat(conv_y[:, :, :]), k.ps[:, 0, :], ACT.Tanh, scale=0.5).then_inc(f_evicted.sem, 1)
                high.upto(M0 + 7)
                act.wait_ge(k.chunk_done, st.results(l, M0 + 5))
                act.activation(pz[:, :, POOL_PAD:], k.ps[:, 1, :].rearrange("p (f n) -> p f n", f=2), ACT.Copy)\
                   .then_inc(f_evicted.sem, 1)
                high.upto(M0 + 8)
                act.wait_ge(k.chunk_done, st.results(l, M0 + 6))
                act.activation(flat(idxF[:, :, :]), k.ps[:, 0, :], ACT.Copy).then_inc(f_evicted.sem, 1)
                act.wait_ge(y0T_done.sem, y0T_done.at(l, 1))
                act.activation(flat(yH[:, 0:2, :]), k.ps[:, 3, :], ACT.Copy).then_inc(y0H_ready.sem, 1)
                high.upto(M0 + 9)
                for i in range(2):
                    act.wait_ge(k.chunk_done, st.results(l, M0 + 7 + i))
                    act.activation(flat(qkF[:, 2 * i:2 * i + 2, :]), k.ps[:, 1 - i, :], ACT.Copy).then_inc(f_evicted.sem, 1)
                    if i == 0:
                        act.wait_ge(rel_done.sem, rel_done.at(l, 1))
                        for h in range(IH):
                            ins = act.activation(rel[:, h, :], k.ps[:, 4 + h, 0:3 * P], ACT.Relu, scale=ID ** -0.5)
                        ins.then_inc(rel_ready.sem, 1)
                    high.upto(M0 + 10 + i)
                act.wait_ge(bias_moved.sem, bias_moved.at(0, 16 * (1 + 2 * BH)))

                def gate_in(i):
                    act.wait_ge(k.chunk_done, st.results(l, G0 + i))
                    act.activation(flat(gates[:, 2 * i:2 * i + 2, :]), k.ps[:, (i + 1) % 2, :], ACT.Tanh, scale=0.5)\
                       .then_inc(f_evicted.sem, 1)
                    high.upto(G0 + i + 3)

                def soft(qt):
                    act.wait_ge(max_ready.sem, max_ready.at(l, 2 - qt))
                    n, lo = (P, 0) if qt == 0 else (2 * P, P)
                    for h in range(BH):
                        ins = act.activation(logit[:, h, lo:lo + n], logit[:, h, lo:lo + n], ACT.Exp,
                                             bias=rmax[:, qt, h:h + 1])
                    ins.then_inc(exp_ready.sem, 1)

                for i in range(5):
                    gate_in(i)
                soft(1)
                soft(0)
                gate_in(5)
                act.wait_ge(pT_done.sem, pT_done.at(l, 1))
                for n in range(2):
                    ins = act.activation(pT[:, 2 * n:2 * n + 2, 1:3, :],
                                         k.ps[:, 2 + n, :].rearrange("p (h b n) -> p h b n", h=2, b=2), ACT.Copy)
                ins.then_inc(pT_ready.sem, 1)
                act.wait_ge(pT_done.sem, pT_done.at(l, 2))
                act.activation(pT[:, :, 0, :], k.ps[:, 4, :].rearrange("p (h n) -> p h n", h=BH), ACT.Copy)\
                   .then_inc(pT_ready.sem, 1)
                gate_in(6)
                gate_in(7)
                gate_in(8)
                act.wait_ge(y2T_done.sem, y2T_done.at(l, 1))
                act.activation(flat(yH[:, 4:6, :]), k.ps[:, 3, :], ACT.Copy).then_inc(y2H_ready.sem, 1)
                for i in range(9, 12):
                    gate_in(i)
                act.wait_ge(xc_ready.sem, xc_ready.at(l, 1))
                for tt in range(TT):
                    act.activation(conv_y[:, tt, :], xc[:, tt, :], ACT.Square, accum_out=cstat[:, 1, tt:tt + 1])\
                       .then_inc(css_ready.sem, 1)
                gate_in(12)
                act.wait_ge(lnT_done.sem, lnT_done.at(l, 1))
                for f in range(2):
                    ins = act.activation(conv_y[:, f, :], k.ps[:, 7, f * SEQ:(f + 1) * SEQ], ACT.Identity,
                                         scale=par[:, PB_LG + f:PB_LG + f + 1], bias=par[:, PB_LB + f:PB_LB + f + 1])
                ins.then_inc(ln_ready.sem, 1)
                act.wait_ge(ln_ready.sem, ln_ready.at(l, 1))
                act.activation(flat(xc[:, :, :]), flat(conv_y[:, :, :]), ACT.Tanh, scale=0.5).then_inc(lt_ready.sem, 1)
                gate_in(13)
                act.wait_ge(y3_ready.sem, y3_ready.at(l, 1))
                act.activation(flat(yH[:, 6:8, :]), flat(conv_y[:, :, :]), ACT.Copy, scale=0.5).then_inc(y3H_ready.sem, 1)
                act.wait_ge(pmm_done.sem, pmm_done.at(l, 1))
                for g in range(4):
                    j, e = g // 2, g % 2
                    half = slice(e * 64, (e + 1) * 64)
                    ins = act.activation(yH[half, 2 + j, :], k.ps[half, 4 + 2 * e, j * SEQ:(j + 1) * SEQ], ACT.Copy,
                                         scale=par[half, PB_PS + j:PB_PS + j + 1])
                ins.then_inc(y1H_ready.sem, 1)
                gate_in(14)
                gate_in(15)
                for i in range(4):
                    high.upto(BR + 3 + i)
                    act.wait_ge(mix_ready.sem, mix_ready.at(l, i + 1))
                    act.activation(flat(k.aH[:, 2 * i:2 * i + 2, :]), mixed[:, i % 2, :], ACT.Copy, scale=0.5)\
                       .then_inc(mixH_ready.sem, 1)
                high.upto(F0[1] - 1)
                post_stats(l, 1, F0[1] - 1)
                norm_stats(k, act, l, 2)
                high.upto(F0[1] + 1)
                norm_high(k, act, l, 2, par[:, PB_N2:PB_DW])
                high.upto(F0[1] + 2)
                mlp(l, high, 1)
                post_stats(l, 2, CB - 1)

        @block.vector
        def _(dve):
            dve.wait_ge(const_loaded.sem, const_loaded.at(0, 48))
            dve.tensor_copy(rel_rep, last(rel_sb, P)).then_inc(rel_rep_ready.sem, 1)
            dve.memset(v_tok[:, :, :, BD:BD + 1], 1.0).then_inc(k.x_new.sem, 1)

            def mlp(l, low, f):
                def unit(j, lows, trips=0, q=0):
                    n = (l * 2 + f) * FF_B + q + (j + 1)
                    for c in lows[:1]:
                        split_low(k, dve, st, l, c, trips)
                    dve.wait_ge(silu_ready.sem, n)
                    dve.wait_ge(k.chunk_done, st.results(l, b_chunk(f, j), trips))
                    r = hid_r[:, j % 2, :]
                    dve.tensor_tensor(r, r, k.ps[:, 2 * (j % 2) + 1, :], ALU.mult).then_inc(gated_ready.sem, 1)
                    for c in lows[1:2]:
                        split_low(k, dve, st, l, c, trips)
                    dve.wait_ge(hidH_ready.sem, n)
                    dve.tensor_tensor(hidL[:, j % 2, :], r, hidH[:, j % 2, :].bitcast(F32), ALU.subtract)\
                       .then_inc(hid_ready.sem, 1)
                    for c in lows[2:]:
                        split_low(k, dve, st, l, c, trips)

                first = F0[f]
                unit(0, [first + 3, first + 4])
                with dve.Fori(0, 4) as q:
                    for j in (1, 2):
                        unit(j, [first + 3 * j + i for i in (2, 3, 4)], q * 2, q * 2)
                unit(9, [first + 3 * 9 + i for i in (2, 3, 4)])
                unit(10, [first + 3 * 10 + 2])

            def post(l, ch, n, half):
                dve.wait_ge(pss_ready.sem, pss_ready.at(l, TT * (n + 1)))
                dve.tensor_scalar(pss[:, 1, :], pss[:, 0, :], 1.0 / DM, EPS, ALU.mult, ALU.add).then_inc(ch.sem, ch.one())
                dve.wait_ge(ch.sem, ch.at(l))
                rsqrt(dve, ch, l, pss[:, 2, :], pss[:, 1, :], pss[:, 3, :])
                if half:
                    dve.tensor_scalar(pss[:, 2, :], pss[:, 2, :], 0.5, None, ALU.mult).then_inc(ch.sem, ch.one())
                    dve.wait_ge(ch.sem, ch.at(l))
                dve.wait_ge(row_loaded.sem, row_loaded.at(l, 16 * (n + 1)))
                for tt in range(TT):
                    dve.scalar_tensor_tensor(post_t.rearrange("p (b n) -> p b n", b=2), k.ps[:, 4 + 2 * tt:6 + 2 * tt, :],
                                                   pss[:, 2, tt:tt + 1], gain_row[:, :].rearrange("p (b n) -> p b n", b=2),
                                                   ALU.mult, ALU.mult).then_inc(ch.sem, ch.one())
                    dve.wait_ge(ch.sem, ch.at(l))
                    ins = dve.tensor_tensor(k.x[:, tt, :], k.x[:, tt, :], post_t, ALU.add)
                    if tt == 0:
                        ins.then_inc(ch.sem, ch.one())
                        dve.wait_ge(ch.sem, ch.at(l))
                ins.then_inc(k.x_new.sem, 1)

            with dve.Fori(0, DEPTH) as l:
                low = Splitter(split_low, k, dve, st, l)
                ch = Chain(dve_chain.sem, DVE_B)
                norm_diag(k, dve, ch, l, 0)
                low.upto(1)
                dve.wait_ge(par_loaded.sem, par_loaded.at(l, 32))
                norm_low(k, dve, l, 0, par[:, PB_N1:PB_NM])
                low.upto(2)
                mlp(l, low, 0)
                low.next = M0
                post(l, ch, 0, True)
                norm_diag(k, dve, ch, l, 1)
                low.upto(M0 + 1)
                dve.tensor_tensor(ws, ws, mid(tri, 4), ALU.mult).then_inc(ch.sem, ch.one())
                norm_low(k, dve, l, 1, par[:, PB_NM:PB_N2])
                low.upto(M0 + 2)
                dve.wait_ge(vss_ready.sem, vss_ready.at(l, 2))
                dve.tensor_scalar(vstat[:, 1, :], vstat[:, 0, :], 1.0 / BW, EPS, ALU.mult, ALU.add).then_inc(ch.sem, ch.one())
                dve.wait_ge(ch.sem, ch.at(l))
                rsqrt(dve, ch, l, vstat[:, 2, :], vstat[:, 1, :], vstat[:, 3, :])
                for tt in range(TT):
                    ins = dve.scalar_tensor_tensor(vn[:, tt, :], uv[:, tt, BW:], vstat[:, 2, tt:tt + 1], v_gain[:, :],
                                                   ALU.mult, ALU.mult)
                    if tt == 0:
                        ins.then_inc(ch.sem, ch.one())
                ins.then_inc(vn_ready.sem, 1)
                low.upto(M0 + 4)
                dve.wait_ge(wi_done.sem, wi_done.at(l, 1))
                dve.tensor_scalar(w_idx[:, :, :], k.ps[:, 6, 0:TT * IH].rearrange("p (t h) -> p t h", t=TT), IH ** -0.5, None,
                                  ALU.mult).then_inc(wi_ready.sem, 1)
                low.upto(M0 + 6)
                dve.wait_ge(f_evicted.sem, f_evicted.at(l, 2))
                dve.scalar_tensor_tensor(conv_x[:, :, CONV_PAD:], conv_y[:, :, :], 1.0,
                                         k.ps[:, 1, :].rearrange("p (f n) -> p f n", f=2), ALU.add, ALU.mult)\
                   .then_inc(hc_ready.sem, 1)
                dve.wait_ge(gm_done.sem, gm_done.at(l, 1))
                for g in range(4):
                    cols = slice(g * 64, (g + 1) * 64)
                    ins = dve.scalar_tensor_tensor(y0[:, :, cols], k.ps[:, 2, :].rearrange("p (t n) -> p t n", t=TT)[:, :, cols],
                                                   par[:, PB_GB + g:PB_GB + g + 1], uv[:, :, cols], ALU.add, ALU.mult)
                ins.then_inc(y0_ready.sem, 1)
                low.upto(M0 + 8)
                dve.wait_ge(y0H_ready.sem, y0H_ready.at(l, 1))
                dve.tensor_tensor(flat(yL[:, 0:2, :]), k.ps[:, 3, :], flat(yH[:, 0:2, :]).bitcast(F32), ALU.subtract)\
                   .then_inc(y0_split.sem, 1)
                low.upto(M0 + 9)

                def conv_taps(n):
                    for t in range(conv_taps.next, min(conv_taps.next + n, TAPS)):
                        for f in range(2):
                            w = par[:, PB_DW + 2 * t + f:PB_DW + 2 * t + f + 1]
                            src = conv_x[:, f, t:t + SEQ]
                            if t == POOL_TAPS:
                                ins = dve.tensor_scalar(conv_y[:, f, :], src, w, None, ALU.mult)
                            else:
                                dve.wait_ge(ch.sem, ch.at(l, 1))
                                ins = dve.scalar_tensor_tensor(conv_y[:, f, :], src, w, conv_y[:, f, :], ALU.mult, ALU.add)
                            if (t, f) == (TAPS - 1, 1):
                                ins.then_inc(conv_rest.sem, 1)
                            else:
                                ins.then_inc(ch.sem, ch.one())
                    conv_taps.next += n

                conv_taps.next = POOL_TAPS
                dve.wait_ge(taps_ready.sem, taps_ready.at(l, 1))
                dve.wait_ge(hc_ready.sem, hc_ready.at(l, 1))
                conv_taps(3)
                dve.wait_ge(rel_ready.sem, rel_ready.at(l, 1))
                tiles = ((0, slice(0, P)), (1, slice(P, 3 * P)))
                for h in range(IH):
                    for qt, cols in tiles:
                        w = w_idx[:, qt, h:h + 1]
                        if h == 0:
                            dve.tensor_scalar(score[:, cols], rel[:, h, cols], w, None, ALU.mult).then_inc(ch.sem, ch.one())
                        else:
                            dve.scalar_tensor_tensor(score[:, cols], rel[:, h, cols], w, score[:, cols], ALU.mult, ALU.add).then_inc(ch.sem, ch.one())
                    dve.wait_ge(ch.sem, ch.at(l))
                dve.tensor_tensor(score[:, :], score[:, :], reach, ALU.add).then_inc(ch.sem, ch.one())
                dve.wait_ge(ch.sem, ch.at(l))
                low.upto(M0 + 10)

                def logits(qt):
                    dve.wait_ge(sc_done.sem, sc_done.at(l, 2 - qt))
                    if qt == 1:
                        out, src, b = logit[:, :, P:3 * P], k.ps[:, 2:4, :].rearrange("p b (h n) -> p (b h) n", h=2), bias[:, :, P:3 * P]
                    else:
                        out, b = (v[:, :, 0:P].rearrange("p (b h) n -> p b h n", b=2) for v in (logit, bias))
                        src = k.ps[:, 4:6, 0:SEQ].rearrange("p b (h n) -> p b h n", h=2)
                    dve.scalar_tensor_tensor(out, src, BD ** -0.5, b, ALU.mult, ALU.add).then_inc(l_ready.sem, 1)

                dve.wait_ge(bias_moved.sem, bias_moved.at(0, 16 * (1 + 2 * BH)))
                for r in range(TOPK // 8):
                    value = held(dve, ch.at(l))
                    dve.wait_ge(const_loaded.sem, 48)
                    dve.wait_ge(ch.sem, value)
                    for qt, cols in tiles:
                        dve.max(top8[:, qt, :], score[:, cols]).then_inc(ch.sem, ch.one())
                    value = held(dve, ch.at(l))
                    dve.wait_ge(const_loaded.sem, 48)
                    dve.wait_ge(ch.sem, value)
                    for qt, cols in tiles:
                        dve.match_replace(score[:, cols], top8[:, qt, :], score[:, cols], TAKEN).then_inc(ch.sem, ch.one())
                    if r == 1:
                        logits(1)
                        low.upto(M0 + 11)
                        conv_taps(3)
                    if r == 3:
                        logits(0)
                        low.upto(M0 + 12)
                        conv_taps(3)
                    if r == 6:
                        low.upto(M0 + 13)
                        conv_taps(3)
                dve.wait_ge(ch.sem, ch.at(l))
                dve.tensor_scalar(keep[:, :], score[:, :], TAKEN, -NEG, ALU.is_equal, ALU.mult).then_inc(ch.sem, ch.one())
                dve.wait_ge(ch.sem, ch.at(l))
                dve.scalar_tensor_tensor(keep[:, :], keep[:, :], NEG, reach, ALU.add, ALU.add).then_inc(ch.sem, ch.one())
                dve.wait_ge(ch.sem, ch.at(l))
                dve.wait_ge(l_ready.sem, l_ready.at(l, 2))
                for qt, cols in ((1, slice(P, 3 * P)), (0, slice(0, P))):
                    v = logit[:, :, cols]
                    dve.tensor_tensor(v, v, mid(keep[:, cols], BH), ALU.add).then_inc(ch.sem, ch.one())
                    dve.wait_ge(ch.sem, ch.at(l))
                    dve.tensor_reduce(rmax[:, qt, :], v, AX.X, ALU.max).then_inc(ch.sem, ch.one())
                    dve.wait_ge(ch.sem, ch.at(l))
                    dve.tensor_scalar(rmax[:, qt, :], rmax[:, qt, :], -1.0, None, ALU.mult).then_inc(max_ready.sem, 1)
                low.upto(M0 + 14)
                conv_taps(3)
                low.upto(M0 + 16)
                dve.wait_ge(pv_done.sem, pv_done.at(l, 1))
                y2v = yb2[:, :, :].rearrange("p t (j e n) -> p t j e n", j=2, e=2)
                outs = [k.ps[:, (5, 2)[qt], 0:BH * (BD + 1)].rearrange("p (e j n) -> p e j n", e=2, j=2) for qt in range(TT)]
                for qt in range(TT):
                    dve.reciprocal(rsum[:, qt, :].rearrange("p (e j) -> p e j", e=2), outs[qt][:, :, :, BD]).then_inc(ch.sem, ch.one())
                dve.wait_ge(ch.sem, ch.at(l))
                for qt in range(TT):
                    for e in range(2):
                        ins = dve.tensor_tensor(y2v[:, qt, :, e, :], outs[qt][:, e, :, 0:BD],
                                                last(rsum[:, qt, 2 * e:2 * e + 2], BD), ALU.mult)
                ins.then_inc(y2_ready.sem, 1)
                low.upto(M0 + 18)
                dve.wait_ge(y2H_ready.sem, y2H_ready.at(l, 1))
                dve.tensor_tensor(flat(yL[:, 4:6, :]), k.ps[:, 3, :], flat(yH[:, 4:6, :]).bitcast(F32), ALU.subtract)\
                   .then_inc(y2_split.sem, 1)
                low.upto(M0 + 20)
                dve.wait_ge(ct_done.sem, ct_done.at(l, 1))
                byt = k.ps[:, 6, :].rearrange("p (t n) -> p t n", t=TT)
                dve.tensor_reduce(cstat[:, 0, :], byt, AX.X, ALU.add).then_inc(ch.sem, ch.one())
                dve.wait_ge(ch.sem, ch.at(l))
                dve.tensor_scalar(cstat[:, 0, :], cstat[:, 0, :], -1.0 / BW, None, ALU.mult).then_inc(ch.sem, ch.one())
                dve.wait_ge(ch.sem, ch.at(l))
                for tt in range(TT):
                    ins = dve.tensor_scalar(xc[:, tt, :], byt[:, tt, :], cstat[:, 0, tt:tt + 1], None, ALU.add)
                    if tt == 0:
                        ins.then_inc(ch.sem, ch.one())
                ins.then_inc(xc_ready.sem, 1)
                low.upto(M0 + 21)
                dve.wait_ge(css_ready.sem, css_ready.at(l, 2))
                dve.tensor_scalar(cstat[:, 1, :], cstat[:, 1, :], 1.0 / BW, EPS, ALU.mult, ALU.add).then_inc(ch.sem, ch.one())
                dve.wait_ge(ch.sem, ch.at(l))
                rsqrt(dve, ch, l, cstat[:, 2, :], cstat[:, 1, :], cstat[:, 3, :])
                for tt in range(TT):
                    ins = dve.tensor_scalar(k.diag[:, tt, :], k.ident, cstat[:, 2, tt:tt + 1], None, ALU.mult)
                    if tt == 0:
                        ins.then_inc(ch.sem, ch.one())
                ins.then_inc(cdiag_ready.sem, 1)
                low.upto(M0 + 22)
                dve.wait_ge(lt_ready.sem, lt_ready.at(l, 1))
                dve.scalar_tensor_tensor(flat(conv_y[:, :, :]), flat(xc[:, :, :]), 1.0, flat(conv_y[:, :, :]), ALU.add, ALU.mult)\
                   .then_inc(y3_ready.sem, 1)
                low.upto(M0 + 23)
                dve.wait_ge(y3H_ready.sem, y3H_ready.at(l, 1))
                dve.scalar_tensor_tensor(flat(yL[:, 6:8, :]), flat(conv_y[:, :, :]), 0.5, flat(yH[:, 6:8, :]).bitcast(F32),
                                         ALU.mult, ALU.subtract).then_inc(y3_split.sem, 1)
                dve.wait_ge(y1H_ready.sem, y1H_ready.at(l, 1))
                for g in range(4):
                    j, e = g // 2, g % 2
                    half = slice(e * 64, (e + 1) * 64)
                    ins = dve.scalar_tensor_tensor(yL[half, 2 + j, :], k.ps[half, 4 + 2 * e, j * SEQ:(j + 1) * SEQ],
                                                   par[half, PB_PS + j:PB_PS + j + 1], yH[half, 2 + j, :].bitcast(F32),
                                                   ALU.mult, ALU.subtract)
                ins.then_inc(y1_split.sem, 1)
                low.upto(BR + 1)
                dve.wait_ge(f_evicted.sem, f_evicted.at(l, 22))
                for i in range(4):
                    low.upto(BR + 1 + i)
                    dve.wait_ge(k.chunk_done, st.results(l, BR + i))
                    for n in range(NBR):
                        g = flat(gates[:, 8 * n + 2 * i:8 * n + 2 * i + 2, :])
                        out = mixed[:, i % 2, :] if n == 0 else mix_t
                        dve.scalar_tensor_tensor(out, g, 1.0, k.ps[:, 4 * (i % 2) + n, :], ALU.add, ALU.mult).then_inc(ch.sem, ch.one())
                        dve.wait_ge(ch.sem, ch.at(l))
                        if n:
                            ins = dve.tensor_tensor(mixed[:, i % 2, :], mixed[:, i % 2, :], mix_t, ALU.add)
                            if n < NBR - 1:
                                ins.then_inc(ch.sem, ch.one())
                                dve.wait_ge(ch.sem, ch.at(l))
                    ins.then_inc(mix_ready.sem, 1)
                    dve.wait_ge(mixH_ready.sem, mixH_ready.at(l, i + 1))
                    dve.scalar_tensor_tensor(flat(k.aL[:, 2 * i:2 * i + 2, :]), mixed[:, i % 2, :], 0.5,
                                             flat(k.aH[:, 2 * i:2 * i + 2, :]).bitcast(F32), ALU.mult, ALU.subtract)\
                       .then_inc(mix_split.sem, 1)
                low.upto(F0[1] - 1)
                post(l, ch, 1, False)
                norm_diag(k, dve, ch, l, 2)
                low.upto(F0[1] + 1)
                norm_low(k, dve, l, 2, par[:, PB_N2:PB_DW])
                low.upto(F0[1] + 2)
                mlp(l, low, 1)
                post(l, ch, 2, True)
                assert ch.n == DVE_B, ("dve", ch.n)

        @block.tensor
        def _(pe):
            aop = lambda kt: (k.aH[:, kt, :], k.aL[:, kt, :])
            yop = lambda kt: (yH[:, kt, :], yL[:, kt, :])
            t_out = lambda tt, h: k.ps[:, 4 + 2 * tt + h, :]
            pe.wait_ge(rel_rep_ready.sem, rel_rep_ready.at(0, 1))
            pe.wait_ge(const_loaded.sem, const_loaded.at(0, 48))
            for h in range(BH):
                ins = pe.matmul(k.ps[:, h, :], rel_rep[:, h, :], hot, start=True, stop=True)
            ins.then_inc(line_done.sem, 1)

            def mlp(l, f):
                def up(j, trips=0, q=0):
                    base = (l * 2 + f) * FF_B + q
                    pe.wait_ge(k.lo_ready, st.count(l, a_chunk(f, j), trips))
                    if j >= 2:
                        pe.wait_ge(silu_ready.sem, base + (j - 1))
                    f_chunk(k, pe, a_chunk(f, j), [2 * (j % 2)], [range(8)], aop)
                    pe.wait_ge(k.lo_ready, st.count(l, b_chunk(f, j), trips))
                    if j >= 2:
                        pe.wait_ge(gated_ready.sem, base + (j - 1))
                    f_chunk(k, pe, b_chunk(f, j), [2 * (j % 2) + 1], [range(8)], aop)

                def down(j, trips=0, q=0):
                    pe.wait_ge(k.lo_ready, st.count(l, down_chunk(f, j), trips))
                    pe.wait_ge(hid_ready.sem, (l * 2 + f) * FF_B + q + (j + 1))
                    hid = lambda kt: [x[:, j % 2, kt * SEQ:(kt + 1) * SEQ] for x in (hidH, hidL)]
                    t_chunk(k, pe, down_chunk(f, j), range(2), DM, hid, t_out, j == 0, j == FF_B - 1)

                up(0)
                up(1)
                down(0)
                with pe.Fori(0, 4) as q:
                    for j in (1, 2):
                        up(j + 1, q * 2, q * 2)
                        down(j, q * 2, q * 2)
                up(10)
                down(9)
                down(10)

            pe.wait_ge(line_ready.sem, line_ready.at(0, 1))
            with pe.Fori(0, DEPTH) as l:
                norm_transpose(k, pe, l, 0)
                pe.wait_ge(k.a_ready.sem, k.a_ready.at(l, 4))
                mlp(l, 0)
                norm_transpose(k, pe, l, 1)
                pe.wait_ge(k.a_ready.sem, k.a_ready.at(l, 8))
                for half in range(2):
                    pe.wait_ge(k.lo_ready, st.count(l, M0 + half))
                    t_chunk(k, pe, M0 + half, range(4 * half, 4 * half + 4), 512, aop,
                            lambda tt, h: k.ps[:, 2 + tt, :], half == 0, half == 1)
                pe.wait_ge(k.lo_ready, st.count(l, M0 + 2))
                t_chunk(k, pe, M0 + 2, range(8), 256, aop, lambda tt, h: k.ps[:, 0, tt * BW:(tt + 1) * BW], True, True)
                pe.wait_ge(par_loaded.sem, par_loaded.at(l, 32))
                for tt in range(TT):
                    for kt in range(KT):
                        for i, a in enumerate((k.aH, k.aL)):
                            ins = pe.matmul(k.ps[:, 6, tt * IH:(tt + 1) * IH], a[:, kt, tt * P:(tt + 1) * P].bitcast(F32),
                                            wi[:, kt, :], start=kt == 0 and i == 0, stop=kt == KT - 1 and i == 1)
                ins.then_inc(wi_done.sem, 1)

                def feature(i):
                    pe.wait_ge(k.lo_ready, st.count(l, M0 + i))
                    if i == 5:
                        pe.wait_ge(hc_ready.sem, hc_ready.at(l, 1))
                    elif i == 4:
                        pe.wait_ge(f_evicted.sem, f_evicted.at(l, 1))
                    elif i >= 6:
                        pe.wait_ge(f_evicted.sem, f_evicted.at(l, i - 4))
                    f_chunk(k, pe, M0 + i, [i % 2], [range(8)], aop)

                for i in (3, 4, 5):
                    feature(i)
                pe.wait_ge(vn_ready.sem, vn_ready.at(l, 1))
                for tt in range(TT):
                    for g in range(4):
                        ins = pe.matmul(k.ps[:, 2, tt * BW + g * 64:tt * BW + (g + 1) * 64], ws[:, g, :],
                                        vn[:, tt, g * 64:(g + 1) * 64], start=True, stop=True)
                ins.then_inc(gm_done.sem, 1)
                feature(6)

                def to_features(bank, src, by=None):
                    for f in range(2):
                        for tt in range(TT):
                            ins = pe.matmul(k.ps[:, bank, f * SEQ + tt * P:f * SEQ + (tt + 1) * P], src[:, tt, f * P:(f + 1) * P],
                                            k.ident if by is None else by[:, tt, :], start=True, stop=True)
                    return ins

                pe.wait_ge(y0_ready.sem, y0_ready.at(l, 1))
                to_features(3, y0).then_inc(y0T_done.sem, 1)
                feature(7)
                pe.wait_ge(f_evicted.sem, f_evicted.at(l, 4))
                pe.wait_ge(wi_ready.sem, wi_ready.at(l, 1))
                for h in range(IH):
                    rows_ = slice(h * ID, (h + 1) * ID)
                    pe.matmul(k.ps[:, 4 + h, 0:P], idxF[rows_, 0, 0:P], idxF[rows_, 1, 0:P], start=True, stop=True)
                    ins = pe.matmul(k.ps[:, 4 + h, P:3 * P], idxF[rows_, 0, P:SEQ], idxF[rows_, 1, :], start=True, stop=True)
                ins.then_inc(rel_done.sem, 1)
                feature(8)
                feature(9)

                def scores(qt):
                    n = (qt + 1) * P
                    for h in range(BH):
                        j, e = head_slot(h)
                        rows_ = slice(e * BD, (e + 1) * BD)
                        ins = pe.matmul(k.ps[:, (4, 2)[qt] + e, j * n:(j + 1) * n], qkF[rows_, j, qt * P:(qt + 1) * P],
                                        qkF[rows_, 2 + j, 0:n], start=True, stop=True)
                    ins.then_inc(sc_done.sem, 1)

                pe.wait_ge(f_evicted.sem, f_evicted.at(l, 6))
                pe.wait_ge(y0_split.sem, y0_split.at(l, 1))
                scores(1)
                feature(10)
                pe.wait_ge(rel_ready.sem, rel_ready.at(l, 1))
                scores(0)
                for i in (11, 12, 13, 14):
                    feature(i)
                pe.wait_ge(exp_ready.sem, exp_ready.at(l, 2))
                for h in range(BH):
                    for kb in range(2):
                        ins = pe.matmul(k.ps[:, 2 + h // 2, (h % 2) * SEQ + kb * P:(h % 2) * SEQ + (kb + 1) * P],
                                        logit[:, h, (1 + kb) * P:(2 + kb) * P], k.ident, start=True, stop=True)
                ins.then_inc(pT_done.sem, 1)
                for h in range(BH):
                    ins = pe.matmul(k.ps[:, 4, h * P:(h + 1) * P], logit[:, h, 0:P], k.ident, start=True, stop=True)
                ins.then_inc(pT_done.sem, 1)
                feature(15)
                pe.wait_ge(pT_ready.sem, pT_ready.at(l, 2))
                for qt in range(TT):
                    for h in range(BH):
                        j, e = head_slot(h)
                        out = k.ps[:, (5, 2)[qt], (2 * e + j) * (BD + 1):(2 * e + j + 1) * (BD + 1)]
                        for s in range(qt + 1):
                            ins = pe.matmul(out, pT[:, 2 * e + j, s + qt, :], v_tok[:, s, h, :], start=s == 0, stop=s == qt)
                ins.then_inc(pv_done.sem, 1)
                feature(16)
                pe.wait_ge(y2_ready.sem, y2_ready.at(l, 1))
                to_features(3, yb2).then_inc(y2T_done.sem, 1)
                for i in (17, 18, 19):
                    feature(i)
                pe.wait_ge(conv_done.sem, conv_done.at(l, 1))
                for tt in range(TT):
                    for f in range(2):
                        ins = pe.matmul(k.ps[:, 6, tt * BW + f * P:tt * BW + (f + 1) * P], conv_y[:, f, tt * P:(tt + 1) * P],
                                        k.ident, start=True, stop=True)
                ins.then_inc(ct_done.sem, 1)
                feature(20)
                pe.wait_ge(cdiag_ready.sem, cdiag_ready.at(l, 1))
                to_features(7, xc, k.diag).then_inc(lnT_done.sem, 1)
                feature(21)
                feature(22)
                pe.wait_ge(const_loaded.sem, const_loaded.at(0, 48))
                pe.wait_ge(pool_ready.sem, pool_ready.at(l, 1))
                pe.wait_ge(y2_split.sem, y2_split.at(l, 1))
                for g in range(4):
                    j, e = g // 2, g % 2
                    half = slice(e * 64, (e + 1) * 64)
                    ins = pe.matmul(k.ps[half, 4 + 2 * e, j * SEQ:(j + 1) * SEQ], pw[half, j, :], pooled[half, j, :],
                                    start=True, stop=True)
                ins.then_inc(pmm_done.sem, 1)
                feature(23)
                feature(24)
                for i in range(4):
                    pe.wait_ge(k.lo_ready, st.count(l, BR + i))
                    if i == 0:
                        pe.wait_ge(y0_split.sem, y0_split.at(l, 1))
                        pe.wait_ge(y2_split.sem, y2_split.at(l, 1))
                        pe.wait_ge(y3_split.sem, y3_split.at(l, 1))
                        pe.wait_ge(y1_split.sem, y1_split.at(l, 1))
                        pe.wait_ge(f_evicted.sem, f_evicted.at(l, 22))
                    if i >= 2:
                        pe.wait_ge(mix_ready.sem, mix_ready.at(l, i - 1))
                    f_chunk(k, pe, BR + i, [4 * (i % 2) + n for n in range(NBR)], [(2 * n, 2 * n + 1) for n in range(NBR)], yop)
                pe.wait_ge(mix_ready.sem, mix_ready.at(l, 4))
                for i in range(4):
                    pe.wait_ge(k.lo_ready, st.count(l, WO + i))
                    pe.wait_ge(mix_split.sem, mix_split.at(l, i + 1))
                    t_chunk(k, pe, WO + i, range(2 * i, 2 * i + 2), DM, aop, t_out, i == 0, i == 3)
                norm_transpose(k, pe, l, 2)
                pe.wait_ge(k.a_ready.sem, k.a_ready.at(l, 12))
                mlp(l, 1)


class Names:
    pass


def tensors(nc, k, ctx):
    def sb(name, shape, dt=F32):
        return ctx.enter_context(nc.sbuf_tensor(name, shape, dt))

    k.ps = ctx.enter_context(nc.psum_tensor("ps", [P, 8, 512], F32))
    k.raw = sb("raw", [P, SLOTS, CH])
    k.w_hi, k.w_lo = sb("w_hi", [P, SLOTS, CH], F32R), sb("w_lo", [P, SLOTS, CH], F32R)
    k.x = sb("x", [P, TT, DM])
    k.aH, k.aL = sb("aH", [P, KT, SEQ], F32R), sb("aL", [P, KT, SEQ], F32R)
    k.mixH, k.mixL = sb("mixH", [P, 8 * SEQ], F32R), sb("mixL", [P, 8 * SEQ], F32R)
    k.diag = sb("diag", [P, TT, P])
    k.ss, k.var, k.rstd, k.tmp = (sb(n, [P, 8]) for n in ("ss", "var", "rstd", "tmp"))
    k.x_loaded = ctx.enter_context(nc.semaphore("x_loaded"))
    k.pre_chain = ctx.enter_context(nc.semaphore("pre_chain"))
    k.raw_loaded = [ctx.enter_context(nc.semaphore(f"raw_loaded{s}")) for s in range(SLOTS)]
    k.hi_ready, k.lo_ready, k.chunk_done, k.stored = (
        ctx.enter_context(nc.semaphore(n)) for n in ("hi_ready", "lo_ready", "chunk_done", "stored"))


def constants_a():
    c = np.zeros((P, KA_END), np.float32)
    t, s = np.arange(SEQ)[:, None], np.arange(SEQ)[None, :]
    dist = t - s
    mult = sum(((dist >= 0) & (dist % r == 0) & (dist // r <= w // r)).astype(np.float32)
               for w, r in ((128, 1), (512, 4), (2048, 16)))
    add = np.where(mult > 0, 0.0, NEG).astype(np.float32)
    c[:, KA_ID:KA_ADD] = np.eye(P)
    for lo, m in ((KA_ADD, add), (KA_MULT, mult)):
        c[:, lo:lo + P], c[:, lo + P:lo + 3 * P] = m[:P, :P], m[P:]
    causal = np.where(dist >= 0, 0.0, NEG).astype(np.float32).T
    c[:, KA_CAUS:KA_CAUS + SEQ], c[:, KA_CAUS + SEQ:KA_SEL] = causal[:P], causal[P:, P:]
    for h in range(MH):
        c[h, KA_SEL + h * P:KA_SEL + (h + 1) * P] = 1.0
    c[:, KA_FREQ:KA_END] = (np.float64(500000.0) ** (-np.arange(0, 2 * RH, 2) / (2 * RH))).astype(np.float32)
    return c


def f_pack(w):
    return [w[:, i:i + 256].reshape(8, P, 256).transpose(1, 0, 2).reshape(P, CH) for i in range(0, w.shape[1], 256)]


def t_pack(w, width):
    n = CH // width
    return [w[i:i + n * P].reshape(n, P, width).transpose(1, 0, 2).reshape(P, CH) for i in range(0, w.shape[0], n * P)]


def columns(*vs):
    return np.concatenate([np.asarray(v).reshape(-1, P).T for v in vs], axis=1)


def pack_first(a, l):
    w, b = a["w_in"][l], a["b_in"][l]
    chunks = []
    for lo in (0, 512, 1024, 2560):
        chunks += t_pack(w[:, lo:lo + 512], 512)
    chunks += f_pack(w[:, 1536:2560])
    gate = np.zeros((P, CH), np.float32)
    gate.reshape(P, 8, 256)[:, :, 0:8] = w[:, 3584:3592].reshape(8, P, 8).transpose(1, 0, 2)
    chunks.append(gate)
    chunks += f_pack(w[:, 3072:3584]) + f_pack(w[:, 3592:5640])
    chunks += f_pack(np.concatenate([a["w_proj_att"][l], a["w_proj_mlstm"][l]]))
    chunks += t_pack(a["w_out"][l], DM)
    up, down = f_pack(a["w_ff1"][l]), t_pack(a["w_ff2"][l], DM)
    chunks += [up[0], up[1]]
    for j in range(FF_A):
        chunks += up[j + 2:j + 3] + down[j:j + 1]
    par = columns(a["norm_mix_w"][l], a["norm_mlp_w"][l], b[1536:2560], b[3072:3584], b[3592:5640],
                  a["conv_w"][l].reshape(-1), a["conv_b"][l], a["mlstm_norm_w"][l])
    rows = np.concatenate([b[0:1536], b[2560:3072], b[3584:3592]])
    return chunks, par, rows


def constants_b():
    c = np.zeros((P, KB_END), np.float32)
    c[:, KB_ID:KB_ADD] = np.eye(P)
    dist = np.arange(SEQ)[:, None] - np.arange(SEQ)[None, :]
    reach = np.where(dist >= 0, 0.0, OUT_OF_REACH).astype(np.float32)
    c[:, KB_ADD:KB_ADD + P], c[:, KB_ADD + P:KB_CNT] = reach[:P, :P], reach[P:]
    count = c[:, KB_CNT:KB_TRI].reshape(P, 2, SEQ)
    for g, w in enumerate((2, 4, 8, 16)):
        count[64 * (g % 2):64 * (g % 2) + 64, g // 2] = 1.0 / np.minimum(np.arange(1, SEQ + 1), w)
    c[:, KB_CNT:KB_TRI] = count.reshape(P, -1)
    c[:, KB_TRI:KB_HOT] = np.triu(np.ones((P, P)))
    n = np.arange(SEQ)
    large = 16 + (np.log(np.maximum(n, 1) / 16) / math.log(8) * 16).astype(np.int64)
    bucket = np.where(n < 16, n, np.minimum(large, 31))
    c[bucket[::-1], KB_HOT + np.arange(SEQ)] = 1.0
    return c


def mlp_pack(gu, down):
    a, b, dn = f_pack(gu[:, :256 * FF_B]), f_pack(gu[:, 256 * FF_B:]), t_pack(down, DM)
    chunks = [a[0], b[0]]
    for j in range(FF_B):
        chunks += a[j + 1:j + 2] + b[j + 1:j + 2] + dn[j:j + 1]
    return chunks


def pack_second(a, l):
    w = a["w_in_2"][l]
    chunks = mlp_pack(a["ffn1_w_gu_2"][l], a["ffn1_w_down_2"][l])
    chunks += t_pack(w[:, 0:512], 512)
    chunks += f_pack(w[:, 1280:1536])
    chunks += f_pack(w[:, 1700:2212])
    chunks += f_pack(w[:, 512:768])
    chunks += f_pack(np.concatenate([w[:, 1536:1664]] + [w[:, 1664:1696]] * IH, axis=1))
    chunks += f_pack(w[:, 768:1280])
    chunks += f_pack(w[:, 2212:6308])
    chunks += f_pack(a["w_branch_2"][l].reshape(NBR * BW, DM))
    chunks += t_pack(a["w_out_2"][l], DM)
    chunks += mlp_pack(a["ffn2_w_gu_2"][l], a["ffn2_w_down_2"][l])
    par = np.concatenate([
        columns(a["ffn1_pre_g_2"][l], a["mix_pre_g_2"][l], a["ffn2_pre_g_2"][l], a["conv_dw_2"][l].reshape(-1),
                a["conv_b_2"][l], a["conv_ln_g_2"][l], a["conv_ln_b_2"][l], a["pool_scale_2"][l], a["gm_b_2"][l]),
        w[:, 1696:1700].reshape(KT, P, IH).transpose(1, 0, 2).reshape(P, -1),
        a["gm_ws_2"][l].transpose(2, 0, 1).reshape(P, -1),
        a["pool_w_2"][l].reshape(2, 2, 64, 64).transpose(1, 2, 0, 3).reshape(P, -1)], axis=1)
    return chunks, par


def pack(inputs):
    a = {n: np.asarray(v) for n, v in inputs.items()}
    first = [pack_first(a, l) for l in range(DEPTH)]
    second = [pack_second(a, l) for l in range(DEPTH)]
    gains = [a[n][l] for l in range(DEPTH) for n in ("ffn1_post_g_2", "mix_post_g_2", "ffn2_post_g_2")]
    arrays = {
        "x": a["x"][0],
        "positions": a["positions"].reshape(TT, P).T,
        "w_a": np.stack([c for chunks, _, _ in first for c in chunks]),
        "par_a": np.concatenate([par for _, par, _ in first]),
        "rows_a": np.stack([rows for _, _, rows in first]),
        "final_norm_w": a["final_norm_w"],
        "consts_a": constants_a(),
        "w_b": np.stack([c for chunks, _ in second for c in chunks]),
        "par_b": np.concatenate([par for _, par in second + second[-1:]]),
        "v_gain": np.stack([a["gm_v_g_2"][l] for l in (*range(DEPTH), DEPTH - 1)]),
        "post_gains": np.stack(gains + gains[-1:]),
        "rel_bias": a["rel_bias_2"],
        "consts_b": constants_b(),
    }
    return {n: np.ascontiguousarray(v) for n, v in arrays.items()}


def program(nc, d):
    k = Names()
    with ExitStack() as ctx:
        tensors(nc, k, ctx)
        first_block(nc, k, d, ctx)
        second_block(nc, k, d, ctx)


def kernel(**inputs):
    import concourse.bacc as bacc
    from concourse.bass_utils import run_bass_kernel_spmd

    nc = bacc.Bacc("TRN2", target_bir_lowering=False, num_devices=1)
    arrays = pack(inputs)
    d = Names()
    for name, a in arrays.items():
        vars(d)[name] = nc.dram_tensor("in_" + name, a.shape, mybir.dt.from_np(a.dtype), kind="ExternalInput").ap()
    d.bias_line = nc.dram_tensor("bias_line", (P, BH, 2 * SEQ), F32, kind="Internal").ap()
    d.out = nc.dram_tensor("out", (SEQ, DM), F32, kind="ExternalOutput").ap()
    program(nc, d)
    r = run_bass_kernel_spmd(nc, [{"in_" + n: a for n, a in arrays.items()}], core_ids=[0])
    return r.results[0]["out"].reshape(1, SEQ, DM)
```

```python
import math
from contextlib import ExitStack

import numpy as np
import concourse.bass as bass
from concourse import mybir
from concourse.alu_op_type import AluOpType as ALU

F32, F32R, I32 = mybir.dt.float32, mybir.dt.float32r, mybir.dt.int32
ACT = mybir.ActivationFunctionType
AX = mybir.AxisListType

P = 128
SEQ, DM, DEPTH = 256, 1024, 2
TT = SEQ // P
KT = DM // P
CH = 2048
SLOTS = 3
EPS = 1e-6
NEG = -1e30

AH, AD = 8, 64
MH, MD = 4, 128
RH = 8
CONV = 4
CA = 63
FF_A = 16
BW, BH, BD = 256, 4, 64
IH, ID = 4, 32
TOPK = 64
TAPS = 31
CB = 99
FF_B = 11
NBR = 4

PA_NORM, PA_MLP, PA_BQK, PA_BMO, PA_BG, PA_CW, PA_CB, PA_MN, PA_MG, PA_END = np.cumsum([0, 8, 8, 8, 4, 16, 32, 8, 4, 1])
ROWS_A = 4 * 512 + 8

KA_ID, KA_FREQ, KA_ADD, KA_MULT, KA_CAUS, KA_SEL, KA_END = np.cumsum([0, P, RH, 3 * P, 3 * P, 3 * P, MH * P])

KB_ID, KB_ADD, KB_CNT, KB_TRI, KB_END = np.cumsum([0, P, 3 * P, 2 * SEQ, P])

AHEAD_HIGH, AHEAD_LOW = 2, 1

DVE_A = 112


class Signal:

    def __init__(self, sem, per, start=0):
        self.sem, self.per, self.start = sem, per, start

    def at(self, layer, n):
        return layer * self.per + (self.start + n)


def held(eng, value):
    return eng.snap(eng.to_reg(value))


class Chain:

    def __init__(self, sem, per):
        self.sem, self.per, self.n = sem, per, 0

    def one(self):
        self.n += 1
        return 1

    def at(self, layer, later=0):
        return layer * self.per + (self.n - later)


class Stream:

    def __init__(self, base, per):
        assert base % SLOTS == 0 and per % SLOTS == 0
        self.base, self.per = base, per

    def count(self, layer, c, trips=0):
        return (layer * (self.per // SLOTS) + trips) * SLOTS + (self.base + c + 1)

    def results(self, layer, c, trips=0):
        return self.count(layer, c, trips) + SLOTS

    def loads(self, layer, c, trips=0):
        return (layer * (self.per // SLOTS) + trips) * 16 + 16 * (self.base // SLOTS + c // SLOTS + 1)


def mid(ap, n):
    return ap.unsqueeze(1).broadcast_to([ap.shape[0], n, ap.shape[1]])


def last(ap, n):
    return ap.unsqueeze(len(ap.shape)).broadcast_to([*ap.shape, n])


def rsqrt(dve, ch, layer, y, v, t, done=None):
    dve.tensor_single_scalar(t.bitcast(I32), v.bitcast(I32), 1, ALU.arith_shift_right).then_inc(ch.sem, ch.one())
    dve.wait_ge(ch.sem, ch.at(layer))
    dve.tensor_scalar(y.bitcast(I32), t.bitcast(I32), -1.0, float(0x5F3759DF - 2 ** 22 - 2 ** 31), ALU.mult, ALU.add)\
        .then_inc(ch.sem, ch.one())
    dve.wait_ge(ch.sem, ch.at(layer))
    for step in range(3):
        if y.shape[-1] <= 2:
            for i in range(y.shape[-1]):
                c = slice(i, i + 1)
                dve.scalar_tensor_tensor(t[:, c], y[:, c], y[:, c], v[:, c], ALU.mult, ALU.mult).then_inc(ch.sem, ch.one())
        else:
            dve.tensor_tensor(t, y, y, ALU.mult).then_inc(ch.sem, ch.one())
            dve.wait_ge(ch.sem, ch.at(layer))
            dve.tensor_tensor(t, t, v, ALU.mult).then_inc(ch.sem, ch.one())
        dve.wait_ge(ch.sem, ch.at(layer))
        ins = dve.scalar_tensor_tensor(y, t, -1.5, y, ALU.add, ALU.mult)
        if step == 2 and done is not None:
            ins.then_inc(done, 1)
        else:
            ins.then_inc(ch.sem, ch.one())
            dve.wait_ge(ch.sem, ch.at(layer))



def split_high(k, act, st, layer, c, trips=0):
    s = c % SLOTS
    act.wait_ge(k.raw_loaded[s], st.loads(layer, c, trips))
    act.wait_ge(k.chunk_done, st.count(layer, c, trips))
    act.activation(k.w_hi[:, s, :], k.raw[:, s, :], ACT.Copy).then_inc(k.hi_ready, 1)


def split_low(k, dve, st, layer, c, trips=0):
    s = c % SLOTS
    dve.wait_ge(k.hi_ready, st.count(layer, c, trips))
    dve.tensor_tensor(k.w_lo[:, s, :], k.raw[:, s, :], k.w_hi[:, s, :].bitcast(F32),
                      ALU.subtract).then_inc(k.lo_ready, 1)


def split_ahead(split, k, eng, st, layer, n):
    for c in range(n):
        split(k, eng, st, layer, c)


class Splitter:

    def __init__(self, split, k, eng, st, layer, first):
        self.args, self.split, self.next = (k, eng, st, layer), split, first

    def upto(self, c):
        while self.next <= c:
            self.split(*self.args, self.next)
            self.next += 1


def product(pe, out, a, b, first, end):
    pe.matmul(out, a[0], b[0], start=first, stop=False)
    pe.matmul(out, a[0], b[1], start=False, stop=False)
    return pe.matmul(out, a[1], b[0], start=False, stop=end)


def f_chunk(k, pe, c, banks, rows, act, pairs_ready=None, tiles=2):
    s = c % SLOTS
    hi = k.w_hi[:, s, :].rearrange("p (k n) -> p k n", k=8)
    lo = k.w_lo[:, s, :].rearrange("p (k n) -> p k n", k=8)
    for bank, kts in zip(banks, rows):
        for n in range(tiles):
            out = k.ps[:, bank, n * SEQ:(n + 1) * SEQ]
            for i, kt in enumerate(kts):
                if pairs_ready is not None and n == 0 and kt % 2 == 0:
                    pe.wait_ge(k.a_ready.sem, pairs_ready(kt // 2))
                cols = slice(n * P, (n + 1) * P)
                end = product(pe, out, (hi[:, kt, cols], lo[:, kt, cols]), act(kt), i == 0, i == len(kts) - 1)
    end.then_inc(k.chunk_done, 1)


def t_last(k, pe, chunks, out):
    for tt in range(TT):
        for n, (c, act) in enumerate(chunks):
            s = c % SLOTS
            hi = k.w_hi[:, s, :].rearrange("p (k n) -> p k n", k=2)
            lo = k.w_lo[:, s, :].rearrange("p (k n) -> p k n", k=2)
            for h in range(2):
                for i in range(2):
                    a = [x[:, tt * P:(tt + 1) * P] for x in act(i)]
                    b = (hi[:, i, h * 512:(h + 1) * 512], lo[:, i, h * 512:(h + 1) * 512])
                    ins = product(pe, out(tt, h), a, b, False, n == len(chunks) - 1 and i == 1)
            if tt == 1:
                ins.then_inc(k.chunk_done, 1)
        if tt == 0:
            ins.then_inc(k.tile_done.sem, 1)


def t_chunk(k, pe, c, kts, cols, act, out, first, end, tile_done=None):
    s = c % SLOTS
    w = CH // len(kts)
    hi = k.w_hi[:, s, :].rearrange("p (k n) -> p k n", k=len(kts))
    lo = k.w_lo[:, s, :].rearrange("p (k n) -> p k n", k=len(kts))
    step = min(cols, 512)
    for tt in range(TT):
        for h in range(max(1, cols // 512)):
            for i, kt in enumerate(kts):
                a = [x[:, tt * P:(tt + 1) * P] for x in act(kt)]
                b = (hi[:, i, h * step:(h + 1) * step], lo[:, i, h * step:(h + 1) * step])
                ins = product(pe, out(tt, h), a, b, first and i == 0, end and i == len(kts) - 1)
        if tt == 0 and tile_done is not None:
            ins.then_inc(tile_done, 1)
    ins.then_inc(k.chunk_done, 1)


def norm_stats(k, act, layer, n):
    for tt in range(TT):
        act.wait_ge(k.x_new.sem, k.x_new.at(layer, TT * n + tt + 1))
        act.activation(k.aL[:, 4 * tt:4 * tt + 4, :], k.x[:, tt, :].rearrange("p (a b) -> p a b", a=4),
                       ACT.Square, accum_out=k.ss[:, tt:tt + 1]).then_inc(k.ss_ready.sem, 1)


def norm_rstd(k, dve, ch, layer, n):
    dve.wait_ge(k.ss_ready.sem, k.ss_ready.at(layer, TT * (n + 1)))
    dve.tensor_scalar(k.var[:, 0:TT], k.ss[:, 0:TT], 0.5 / DM, 0.5 * EPS, ALU.mult, ALU.add).then_inc(ch.sem, ch.one())
    dve.wait_ge(ch.sem, ch.at(layer))
    rsqrt(dve, ch, layer, k.rstd[:, 0:TT], k.var[:, 0:TT], k.tmp[:, 0:TT], k.rstd_ready.sem)
    dve.wait_ge(k.rstd_ready.sem, k.rstd_ready.at(layer, n + 1))
    for h in range(2):
        cols = slice(h * DM // 2, (h + 1) * DM // 2)
        dve.tensor_scalar(k.xs[:, 1, cols], k.x[:, 1, cols], k.rstd[:, 1:2], None, ALU.mult)\
           .then_inc(k.scaled1.sem, 1)


def norm_scale(k, act, layer, n):
    act.wait_ge(k.rstd_ready.sem, k.rstd_ready.at(layer, n + 1))
    for h in range(2):
        cols = slice(h * DM // 2, (h + 1) * DM // 2)
        act.activation(k.xs[:, 0, cols], k.x[:, 0, cols], ACT.Copy, scale=k.rstd[:, 0:1]).then_inc(k.scaled0.sem, 1)


def norm_transpose(k, pe, layer, n):
    for b in range(4):
        if b % 2 == 0:
            pe.wait_ge(k.scaled0.sem, k.scaled0.at(layer, 2 * n + b // 2 + 1))
            pe.wait_ge(k.scaled1.sem, k.scaled1.at(layer, 2 * n + b // 2 + 1))
        for kk in range(2):
            for tt in range(TT):
                kt = 2 * b + kk
                ins = pe.transpose(k.ps[:, 4 + b, kk * SEQ + tt * P:kk * SEQ + (tt + 1) * P],
                                   k.xs[:, tt, kt * P:(kt + 1) * P], k.ident)
        ins.then_inc(k.nT_done.sem, 1)


def norm_high(k, act, layer, n, gain):
    for b in range(4):
        act.wait_ge(k.nT_done.sem, k.nT_done.at(layer, 4 * n + b + 1))
        for kk in range(2):
            kt = 2 * b + kk
            ins = act.activation(k.aH[:, kt, :], k.ps[:, 4 + b, kk * SEQ:(kk + 1) * SEQ], ACT.Copy,
                                 scale=gain[:, kt:kt + 1])
        ins.then_inc(k.aH_ready.sem, 1)


def norm_low(k, dve, layer, n, gain):
    for b in range(4):
        dve.wait_ge(k.aH_ready.sem, k.aH_ready.at(layer, 4 * n + b + 1))
        for kk in range(2):
            kt = 2 * b + kk
            ins = dve.scalar_tensor_tensor(k.aL[:, kt, :], k.ps[:, 4 + b, kk * SEQ:(kk + 1) * SEQ],
                                           gain[:, kt:kt + 1], k.aH[:, kt, :].bitcast(F32),
                                           ALU.mult, ALU.subtract)
        ins.then_inc(k.a_ready.sem, 1)


def residual(k, dve, st, layer, c, n):
    for tt in range(TT):
        if tt == 0:
            dve.wait_ge(k.tile_done.sem, k.tile_done.at(layer, n))
        else:
            dve.wait_ge(k.chunk_done, st.results(layer, c))
        dve.tensor_tensor(k.x[:, tt, :].rearrange("p (a b) -> p a b", a=2),
                          k.x[:, tt, :].rearrange("p (a b) -> p a b", a=2),
                          k.ps[:, 4 + 2 * tt:6 + 2 * tt, :], ALU.add).then_inc(k.x_new.sem, 1)


def head_slot(h):
    return h // 2, h % 2


def first_block(nc, k, d, sems):
    with ExitStack() as ctx:
        def sb(name, shape, dt=F32):
            return ctx.enter_context(nc.sbuf_tensor(name, shape, dt))

        def sig(name, per, start=0):
            return Signal(sems.enter_context(nc.semaphore("a_" + name)), per, start)

        st = Stream(0, CA)
        consts = k.consts
        k.ident = consts[:, KA_ID:KA_FREQ]
        att_add = consts[:, KA_ADD:KA_MULT]
        att_mult = consts[:, KA_MULT:KA_CAUS]
        ml_add = consts[:, KA_CAUS:KA_SEL]
        sel = consts[0:MH, KA_SEL:KA_END].rearrange("p (h n) -> p h n", h=MH)
        freq = consts[:, KA_FREQ:KA_ADD]
        par = sb("a_par", [P, int(PA_END)])
        rows = k.rows
        pos_i = sb("pos_i", [P, TT], I32)
        pos_f = sb("pos_f", [P, TT])
        angle = sb("angle", [P, 4, TT, RH])
        cos, sin = sb("cos", [P, TT, RH]), sb("sin", [P, TT, RH])
        R1 = sb("R1", [P, 8 * 3 * P])
        R2 = sb("R2", [P, 8 * 3 * P])
        R3 = sb("R3", [P, 8 * (SEQ + CONV - 1)])
        qk_tok = R1[:, 0:TT * 2 * AH * AD].rearrange("p (t h d) -> p t h d", t=TT, h=2 * AH)
        logit = [R1[:, 0:AH * P].rearrange("p (h n) -> p h n", h=AH),
                 R1[:, AH * P:3 * AH * P].rearrange("p (h n) -> p h n", h=AH)]
        qkF = R2[:, 0:8 * SEQ].rearrange("p (f n) -> p f n", f=8)
        pT = R2[:, :].rearrange("p (h b n) -> p h b n", h=AH, b=3)
        z_pad = R3[:, :].rearrange("p (f n) -> p f n", f=8)
        ml_w = [R3[:, 0:MH * SEQ].rearrange("p (h n) -> p h n", h=MH),
                R3[:, MH * SEQ:MH * (SEQ + P)].rearrange("p (h n) -> p h n", h=MH)]
        v_tok = sb("v_tok", [P, TT, AH, AD + 1])
        mv_tok = sb("mv_tok", [P, TT, MH, MD])
        mqk = sb("mqk", [P, 8, SEQ])
        gates = sb("a_gates", [P, 16, SEQ])
        mo = sb("mo", [P, MH, SEQ])
        hn = sb("hn", [P, TT * MH * MD])
        ya = sb("ya", [P, TT * AH * AD])
        hn_v = hn[:, :].rearrange("p (t h d) -> p (t h) d", t=TT, h=MH)
        ya_v = ya[:, :].rearrange("p (t j e d) -> p t j e d", t=TT, j=4, e=2)
        g_rows = hn[0:MH, :].rearrange("p (a n) -> p a n", a=4)
        forget, fall = hn[32:32 + MH, 0:SEQ], hn[32:32 + MH, SEQ:2 * SEQ]
        ones = sb("ones", [P, SEQ])
        ml_cols = sb("ml_cols", [P, 2, TT, MH])
        exp_m = sb("exp_m", [P, TT, MH])
        small = sb("small", [P, 6, TT * MH])
        rmax = sb("rmax", [P, TT, AH])
        rsum = sb("rsum", [P, TT, AH])
        mixed = R2[:, 0:1024].rearrange("p (a n) -> p a n", a=2)
        mix_t = R2[:, 1024:1536]
        hid_r = R1[:, 0:3 * 512].rearrange("p (s n) -> p s n", s=3)
        yH = k.mixH[:, :].rearrange("p (f n) -> p f n", f=8)
        yL = k.mixL[:, :].rearrange("p (f n) -> p f n", f=8)
        hidH = k.mixH[:, 0:3 * 512].rearrange("p (s n) -> p s n", s=3)
        hidL = k.mixL[:, 0:3 * 512].rearrange("p (s n) -> p s n", s=3)

        head_loaded, const_loaded, hot_loaded = sig("head_loaded", 0), sig("const_loaded", 0), sig("hot_loaded", 0)
        par_loaded, row_loaded = sig("par_loaded", 16), sig("row_loaded", 16)
        rel_rep_ready, line_done, line_ready = sig("rel_rep_ready", 0), sig("line_done", 0), sig("line_ready", 0)
        wide = lambda v: v.rearrange("p f n -> p (f n)")
        hot = gates[0:32, 0, :]
        rel_rep = wide(gates[0:32, 2:4, :]).rearrange("p (h n) -> p h n", h=BH)
        rel_sb = gates[0:32, 4, 0:BH]
        line = gates[:, 8:16, :].rearrange("p (h a) n -> p h (a n)", h=BH)
        k.x_new, k.ss_ready, k.tile_done = sig("x_new", 4), sig("ss_ready", 4), sig("tile_done", 2)
        k.rstd_ready, k.scaled0, k.scaled1 = sig("rstd_ready", 2), sig("scaled0", 4), sig("scaled1", 4)
        k.xs = R1[:, 0:TT * DM].rearrange("p (t n) -> p t n", t=TT)
        k.nT_done, k.aH_ready, k.a_ready = sig("nT_done", 8), sig("aH_ready", 8), sig("a_ready", 8)
        rope_ready, angle_ready, trig_ready = sig("rope_ready", 1), sig("angle_ready", 0), sig("trig_ready", 0)
        half_ready = sig("half_ready", 1)
        t_evicted, f_evicted = sig("t_evicted", 4), sig("f_evicted", 14)
        qkT_done, qkF_ready = sig("qkT_done", 4), sig("qkF_ready", 4)
        conv_ready, convt_ready, mqk_ready = sig("conv_ready", 2), sig("convt_ready", 2), sig("mqk_ready", 2)
        gate_ready, gexp_ready = sig("gate_ready", 1), sig("gexp_ready", 2)
        sc_done, max_ready, exp_ready, p_ready = sig("sc_done", 2), sig("max_ready", 2), sig("exp_ready", 2), sig("p_ready", 2)
        rows_ready, nm_done, epre_ready, et_ready = (
            sig("rows_ready", 1), sig("nm_done", 1), sig("epre_ready", 1), sig("et_ready", 1))
        s_done, wt_ready, num_done, num_copied = sig("s_done", 1), sig("wt_ready", 1), sig("num_done", 1), sig("num_copied", 1)
        hn_ready, hnT_done, yb_ready, ybH_ready, yb_split = (
            sig("hn_ready", 1), sig("hnT_done", 1), sig("yb_ready", 1), sig("ybH_ready", 1), sig("yb_split", 1))
        pT_done, pT_ready, pv_done, ya_ready = sig("pT_done", 3), sig("pT_ready", 3), sig("pv_done", 1), sig("ya_ready", 1)
        yaT_done, yaH_ready, ya_split = sig("yaT_done", 1), sig("yaH_ready", 1), sig("ya_split", 1)
        mix_ready, mixH_ready, mix_split = sig("mix_ready", 4), sig("mixH_ready", 4), sig("mix_split", 4)
        relu_ready, sq_ready, hidH_ready, hid_ready = (
            sig("relu_ready", FF_A), sig("sq_ready", FF_A), sig("hidH_ready", FF_A), sig("hid_ready", FF_A))
        dve_chain = sig("dve_chain", DVE_A)
        fin = sig("fin", 0)
        block = ctx.enter_context(nc.Block())

        FFC = CA - 2 * FF_A
        GF = [8, 9, 10, 11] + [13, 14] + list(range(15, 23))

        def up_chunk(j):
            return FFC + (j if j < 2 else 2 * j - 2)

        def down_chunk(j):
            return FFC + (3 + 2 * j if j < FF_A - 2 else 2 * FF_A - 2 + j - (FF_A - 2))

        @block.gpsimd
        def _(pool):
            pool.dma_start(par[:, :], d.par_a[0:P, :]).then_inc(par_loaded.sem, 16)
            pool.wait_ge(k.raw_loaded[AHEAD_HIGH - 1], 16)
            pool.dma_start(rows[:, :], d.rows_a[0:1, :].rearrange("a n -> (a n)").partition_broadcast(P))\
                .then_inc(row_loaded.sem, 16)
            pool.dma_start(consts[:, KA_ADD:KA_END], d.consts_a[:, KA_ADD:KA_END]).then_inc(const_loaded.sem, 16)
            pool.wait_ge(line_ready.sem, 1)
            pool.dma_start(d.bias_line, line).then_inc(k.bias_moved, 16)
            for l in range(1, DEPTH):
                pool.wait_ge(t_evicted.sem, t_evicted.at(l - 1, 4))
                pool.wait_ge(gate_ready.sem, gate_ready.at(l - 1, 1))
                pool.dma_start(rows[:, :], d.rows_a[l:l + 1, :].rearrange("a n -> (a n)").partition_broadcast(P))\
                    .then_inc(row_loaded.sem, 16)
                pool.wait_ge(k.a_ready.sem, k.a_ready.at(l - 1, 8))
                pool.dma_start(par[:, :], d.par_a[l * P:(l + 1) * P, :]).then_inc(par_loaded.sem, 16)
            pool.wait_ge(t_evicted.sem, t_evicted.at(DEPTH - 1, 4))
            pool.wait_ge(gate_ready.sem, gate_ready.at(DEPTH - 1, 1))
            pool.dma_start(rows[:, 0:DM], d.final_norm_w.partition_broadcast(P)).then_inc(row_loaded.sem, 16)
            pool.dma_start(k.par_b, d.par_b[0:P, :]).then_inc(k.par_b_loaded, 16)
            pool.wait_ge(k.a_ready.sem, k.a_ready.at(DEPTH - 1, 8))
            pool.dma_start(consts[:, KB_ADD:KB_END], d.consts_b[:, KB_ADD:KB_END]).then_inc(k.consts_b_loaded, 16)

        @block.sync
        def _(sp):
            sp.dma_start(pos_i[:, :], d.positions).then_inc(head_loaded.sem, 16)
            sp.dma_start(consts[:, 0:KA_ADD], d.consts_a[:, 0:KA_ADD]).then_inc(head_loaded.sem, 16)
            sp.dma_start(hot, d.hot_b).then_inc(hot_loaded.sem, 16)
            sp.dma_start(rel_sb, d.rel_bias).then_inc(hot_loaded.sem, 16)
            for tt in range(TT):
                sp.dma_start(k.x[:, tt, :], d.x[tt * P:(tt + 1) * P, :]).then_inc(k.x_loaded, 16)
            for s in range(SLOTS):
                sp.dma_start(k.raw[:, s, :], d.w_a[s]).then_inc(k.raw_loaded[s], 16)
            with sp.Fori(1, DEPTH * CA // SLOTS) as g:
                for s in range(SLOTS):
                    sp.wait_ge(k.lo_ready, g * SLOTS + (s - SLOTS + 1))
                    sp.dma_start(k.raw[:, s, :], d.w_a[g * SLOTS + s]).then_inc(k.raw_loaded[s], 16)
            for s in range(SLOTS):
                sp.wait_ge(k.lo_ready, DEPTH * CA + s - SLOTS + 1)
                sp.dma_start(k.raw[:, s, :], d.w_b[s]).then_inc(k.raw_loaded[s], 16)

        @block.scalar
        def _(act):
            act.wait_ge(angle_ready.sem, angle_ready.at(0, 1))
            act.activation(sin[:, :, :], angle[:, 0], ACT.Sin).then_inc(trig_ready.sem, 1)
            act.activation(cos[:, :, :], angle[:, 1], ACT.Sin).then_inc(trig_ready.sem, 1)
            act.wait_ge(line_done.sem, line_done.at(0, 1))
            for b in range(2):
                ins = act.activation(line[:, 2 * b:2 * b + 2, 0:SEQ], k.ps[:, b, :].rearrange("p (h n) -> p h n", h=2), ACT.Copy)
            ins.then_inc(line_ready.sem, 1)
            split_ahead(split_high, k, act, st, 0, AHEAD_HIGH)
            with act.Fori(0, DEPTH) as l:
                high = Splitter(split_high, k, act, st, l, AHEAD_HIGH)
                norm_stats(k, act, l, 0)
                norm_scale(k, act, l, 0)
                act.wait_ge(par_loaded.sem, par_loaded.at(l, 16))
                norm_high(k, act, l, 0, par[:, PA_NORM:PA_MLP])
                act.wait_ge(half_ready.sem, half_ready.at(l, 1))

                high.upto(8)
                for b in range(4):
                    act.wait_ge(qkT_done.sem, qkT_done.at(l, b + 1))
                    act.activation(qkF[:, 2 * b:2 * b + 2, :].rearrange("p f n -> p (f n)"), k.ps[:, 4 + b, :],
                                   ACT.Copy).then_inc(qkF_ready.sem, 1)

                def conv_in(i):
                    high.upto(10 + i)
                    act.wait_ge(k.chunk_done, st.results(l, 8 + i))
                    for n in range(2):
                        f = 2 * i + n
                        ins = act.activation(z_pad[:, f, CONV - 1:], k.ps[:, i % 2, n * SEQ:(n + 1) * SEQ],
                                             ACT.Identity, bias=par[:, PA_BQK + f:PA_BQK + f + 1])
                    ins.then_inc(f_evicted.sem, 1)

                def conv_tanh(j):
                    act.wait_ge(conv_ready.sem, conv_ready.at(l, j + 1))
                    act.activation((hn, ya)[j][:, :], mqk[:, 4 * j:4 * j + 4, :].rearrange("p f n -> p (f n)"),
                                   ACT.Tanh, scale=0.5).then_inc(convt_ready.sem, 1)

                conv_in(0)
                conv_in(1)
                conv_in(2)
                conv_tanh(0)
                conv_in(3)
                high.upto(14)
                act.wait_ge(gate_ready.sem, gate_ready.at(l, 1))
                act.activation(fall, fall, ACT.Exp, scale=-1.0).then_inc(gexp_ready.sem, 1)
                act.wait_ge(gexp_ready.sem, gexp_ready.at(l, 1))
                act.activation(fall, fall, ACT.Ln, bias=1.0).then_inc(gexp_ready.sem, 1)
                conv_tanh(1)

                def soft(qt):
                    act.wait_ge(max_ready.sem, max_ready.at(l, 2 - qt))
                    for h in range(AH):
                        ins = act.activation(logit[qt][:, h, :], logit[qt][:, h, :], ACT.Exp,
                                             bias=rmax[:, qt, h:h + 1], scale=AD ** -0.5)
                    ins.then_inc(exp_ready.sem, 1)

                def gate_in(i):
                    c = 13 + i
                    act.wait_ge(k.chunk_done, st.results(l, c))
                    for n in range(2):
                        f = 2 * i + n
                        out = mo[:, f, :] if i < 2 else gates[:, f - 4, :]
                        ins = act.activation(out, k.ps[:, i % 2, n * SEQ:(n + 1) * SEQ], ACT.Tanh,
                                             bias=par[:, PA_BMO + f:PA_BMO + f + 1], scale=0.5)
                    ins.then_inc(f_evicted.sem, 1)
                    high.upto(c + 3)

                high.upto(15)
                soft(1)
                soft(0)
                gate_in(0)
                gate_in(1)
                act.wait_ge(epre_ready.sem, epre_ready.at(l, 1))
                for s in range(TT):
                    for h in range(MH):
                        act.activation(ml_w[s][:, h, :], ml_w[s][:, h, :], ACT.Exp, bias=ml_cols[:, 0, s, h:h + 1])
                act.activation(exp_m[:, :, :], ml_cols[:, 1], ACT.Exp, scale=-1.0).then_inc(et_ready.sem, 1)
                act.wait_ge(k.bias_moved, 16)
                gate_in(2)
                gate_in(3)
                act.wait_ge(num_done.sem, num_done.at(l, 1))
                for tt in range(TT):
                    ins = act.activation(hn[:, tt * 512:(tt + 1) * 512], k.ps[:, 2 + tt, :], ACT.Copy)
                ins.then_inc(num_copied.sem, 1)
                gate_in(4)

                def weights_T(i):
                    act.wait_ge(pT_done.sem, pT_done.at(l, i + 1))
                    for n, b in enumerate(((4, 5), (6, 7), (4, 5))[i]):
                        src = k.ps[:, b, :]
                        if i < 2:
                            dst = pT[:, 4 * i + 2 * n:4 * i + 2 * n + 2, 1:3, :]
                            src = src.rearrange("p (h b n) -> p h b n", h=2, b=2)
                        else:
                            dst = pT[:, 4 * n:4 * n + 4, 0, :]
                            src = src.rearrange("p (h n) -> p h n", h=4)
                        ins = act.activation(dst, src, ACT.Copy)
                    ins.then_inc(pT_ready.sem, 1)

                weights_T(0)
                weights_T(1)
                gate_in(5)
                weights_T(2)
                gate_in(6)
                gate_in(7)
                act.wait_ge(yb_ready.sem, yb_ready.at(l, 1))
                act.activation(yH[:, 4:8, :].rearrange("p f n -> p (f n)"), hn[:, :], ACT.Copy).then_inc(ybH_ready.sem, 1)
                gate_in(8)
                act.wait_ge(yaT_done.sem, yaT_done.at(l, 1))
                for b in range(2):
                    ins = act.activation(yH[:, 2 * b:2 * b + 2, :].rearrange("p f n -> p (f n)"), k.ps[:, 4 + b, :], ACT.Copy)
                ins.then_inc(yaH_ready.sem, 1)
                gate_in(9)
                for i in range(4):
                    high.upto(26 + i)
                    act.wait_ge(mix_ready.sem, mix_ready.at(l, i + 1))
                    act.activation(k.aH[:, 2 * i:2 * i + 2, :].rearrange("p f n -> p (f n)"), mixed[:, i % 2, :],
                                   ACT.Copy, scale=0.5).then_inc(mixH_ready.sem, 1)
                high.upto(FFC + 1)
                norm_stats(k, act, l, 1)
                norm_scale(k, act, l, 1)
                norm_high(k, act, l, 1, par[:, PA_MLP:PA_BQK])
                high.upto(FFC + 2)

                def unit(j, c_up, highs, trips=0, q=0):
                    act.wait_ge(k.chunk_done, st.results(l, c_up, trips))
                    if j >= 3:
                        act.wait_ge(hid_ready.sem, l * FF_A + q + (j - 2))
                    act.activation(hid_r[:, j % 3, :], k.ps[:, j % 3, :], ACT.Relu).then_inc(relu_ready.sem, 1)
                    if highs:
                        split_high(k, act, st, l, highs[0], trips)
                    act.wait_ge(sq_ready.sem, l * FF_A + q + (j + 1))
                    act.activation(hidH[:, j % 3, :], hid_r[:, j % 3, :], ACT.Copy).then_inc(hidH_ready.sem, 1)
                    for c in highs[1:]:
                        split_high(k, act, st, l, c, trips)

                unit(0, up_chunk(0), [FFC + 3])
                unit(1, up_chunk(1), [FFC + 4])
                unit(2, up_chunk(2), [FFC + 5, FFC + 6])
                with act.Fori(0, 4) as q:
                    for j in range(3, 6):
                        unit(j, up_chunk(j), [up_chunk(j) + 3, up_chunk(j) + 4], q * 2, q * 3)
                unit(15, up_chunk(15), [up_chunk(15) + 3])
                split_ahead(split_high, k, act, st, l + 1, AHEAD_HIGH)
            norm_stats(k, act, DEPTH, 0)

        @block.vector
        def _(dve):
            ch = Chain(k.pre_chain, 0)
            dve.memset(ones[:, :], 1.0).then_inc(k.pre_chain, 1)
            ch.n = 1
            dve.memset(v_tok[:, :, :, AD:AD + 1], 1.0).then_inc(ch.sem, ch.one())
            dve.memset(line[:, :, SEQ:2 * SEQ], 0.0).then_inc(ch.sem, ch.one())
            dve.wait_ge(hot_loaded.sem, hot_loaded.at(0, 32))
            dve.wait_ge(ch.sem, ch.at(0))
            dve.tensor_copy(rel_rep, last(rel_sb, P)).then_inc(rel_rep_ready.sem, 1)
            dve.wait_ge(head_loaded.sem, head_loaded.at(0, 32))
            dve.tensor_copy(pos_f[:, :], pos_i[:, :]).then_inc(ch.sem, ch.one())
            dve.wait_ge(ch.sem, ch.at(0))
            dve.tensor_tensor(angle[:, 0], last(pos_f[:, :], RH), mid(freq, TT), ALU.mult).then_inc(ch.sem, ch.one())
            dve.wait_ge(ch.sem, ch.at(0))
            magic = 12582912.0
            dve.tensor_scalar(angle[:, 2], angle[:, 0], 1.0 / (2 * math.pi), magic, ALU.mult, ALU.add).then_inc(ch.sem, ch.one())
            dve.wait_ge(ch.sem, ch.at(0))
            dve.tensor_scalar(angle[:, 2], angle[:, 2], -magic, None, ALU.add).then_inc(ch.sem, ch.one())
            two_pi = 2 * math.pi
            c1 = 6.28125
            c2 = float(np.float32(np.round((two_pi - c1) * 2 ** 21) / 2 ** 21))
            c3 = float(np.float32(two_pi - c1 - c2))
            for part in (c1, c2, c3):
                dve.wait_ge(ch.sem, ch.at(0))
                dve.scalar_tensor_tensor(angle[:, 0], angle[:, 2], -part, angle[:, 0], ALU.mult, ALU.add).then_inc(ch.sem, ch.one())
            dve.wait_ge(ch.sem, ch.at(0))
            pi = float(np.nextafter(np.float32(math.pi), np.float32(0)))
            dve.tensor_scalar(angle[:, 1], angle[:, 0], math.pi / 2, None, ALU.add).then_inc(ch.sem, ch.one())
            dve.wait_ge(ch.sem, ch.at(0))
            dve.tensor_scalar(angle[:, 3], angle[:, 1], pi, -two_pi, ALU.is_gt, ALU.mult).then_inc(ch.sem, ch.one())
            dve.wait_ge(ch.sem, ch.at(0))
            dve.tensor_tensor(angle[:, 1], angle[:, 1], angle[:, 3], ALU.add).then_inc(ch.sem, ch.one())
            dve.wait_ge(ch.sem, ch.at(0))
            dve.tensor_scalar(angle[:, 0:2], angle[:, 0:2], pi, -pi, ALU.min, ALU.max).then_inc(angle_ready.sem, 1)
            dve.wait_ge(k.x_loaded, 16 * TT)
            dve.sem_inc(k.x_new.sem, TT)
            split_ahead(split_low, k, dve, st, 0, AHEAD_LOW)

            with dve.Fori(0, DEPTH) as l:
                low = Splitter(split_low, k, dve, st, l, AHEAD_LOW)
                ch = Chain(dve_chain.sem, DVE_A)

                def bias_rows(n, width=512):
                    return rows[:, n * 512:n * 512 + width]

                norm_rstd(k, dve, ch, l, 0)
                low.upto(1)
                dve.wait_ge(par_loaded.sem, par_loaded.at(l, 16))
                dve.memset(z_pad[:, :, 0:CONV - 1], 0.0).then_inc(ch.sem, ch.one())
                dve.tensor_scalar(par[:, PA_BMO:PA_CW], par[:, PA_BMO:PA_CW], 0.5, None, ALU.mult).then_inc(half_ready.sem, 1)
                norm_low(k, dve, l, 0, par[:, PA_NORM:PA_MLP])
                dve.wait_ge(row_loaded.sem, row_loaded.at(l, 16))
                low.upto(3)
                for n in range(4):
                    dve.wait_ge(k.chunk_done, st.results(l, 2 * n + 1))
                    for tt in range(TT):
                        src = k.ps[:, 2 * (n % 2) + tt, :]
                        if n < 2:
                            dst, src = qk_tok[:, tt, 8 * n:8 * n + 8, :], src.rearrange("p (h d) -> p h d", h=8)
                            b = bias_rows(n).rearrange("p (h d) -> p h d", h=8)
                        elif n == 2:
                            dst, src = v_tok[:, tt, :, 0:AD], src.rearrange("p (h d) -> p h d", h=8)
                            b = bias_rows(n).rearrange("p (h d) -> p h d", h=8)
                        else:
                            dst, src = mv_tok[:, tt], src.rearrange("p (h d) -> p h d", h=4)
                            b = bias_rows(n).rearrange("p (h d) -> p h d", h=4)
                        ins = dve.tensor_tensor(dst, src, b, ALU.add)
                    ins.then_inc(t_evicted.sem, 1)
                    if n == 1:
                        dve.wait_ge(trig_ready.sem, trig_ready.at(0, 2))
                        dve.wait_ge(t_evicted.sem, t_evicted.at(l, 2))
                        tmp = hn[:, :].rearrange("p (a t h r) -> p a t h r", a=4, t=TT, h=2 * AH)
                        for tt in range(TT):
                            q1, q2 = qk_tok[:, tt, :, 0:RH], qk_tok[:, tt, :, RH:2 * RH]
                            cs, sn = mid(cos[:, tt, :], 2 * AH), mid(sin[:, tt, :], 2 * AH)
                            for i, (a, b) in enumerate(((q1, cs), (q2, sn), (q2, cs), (q1, sn))):
                                dve.tensor_tensor(tmp[:, i, tt], a, b, ALU.mult).then_inc(ch.sem, ch.one())
                            dve.wait_ge(ch.sem, ch.at(l))
                            dve.tensor_tensor(q1, tmp[:, 0, tt], tmp[:, 1, tt], ALU.subtract).then_inc(ch.sem, ch.one())
                            ins = dve.tensor_tensor(q2, tmp[:, 2, tt], tmp[:, 3, tt], ALU.add)
                            if tt == 0:
                                ins.then_inc(ch.sem, ch.one())
                        ins.then_inc(rope_ready.sem, 1)
                    low.upto(2 * n + 5)

                def conv(j):
                    dve.wait_ge(f_evicted.sem, f_evicted.at(l, 2 * j + 2))
                    dve.wait_ge(ch.sem, ch.at(l))
                    for t in range(CONV):
                        for f in range(4 * j, 4 * j + 4):
                            w = par[:, PA_CW + 8 * t + f:PA_CW + 8 * t + f + 1]
                            z = z_pad[:, f, t:t + SEQ]
                            if t == 0:
                                ins = dve.tensor_scalar(mqk[:, f, :], z, w, par[:, PA_CB + f:PA_CB + f + 1],
                                                        ALU.mult, ALU.add)
                            else:
                                ins = dve.scalar_tensor_tensor(mqk[:, f, :], z, w, mqk[:, f, :], ALU.mult, ALU.add)
                            if t < CONV - 1 or f < 4 * j + 3:
                                ins.then_inc(ch.sem, ch.one())
                        if t < CONV - 1:
                            dve.wait_ge(ch.sem, ch.at(l))
                    ins.then_inc(conv_ready.sem, 1)

                def conv_silu(j):
                    dve.wait_ge(convt_ready.sem, convt_ready.at(l, j + 1))
                    v = mqk[:, 4 * j:4 * j + 4, :].rearrange("p f n -> p (f n)")
                    dve.scalar_tensor_tensor(v, (hn, ya)[j][:, :], 1.0, v, ALU.add, ALU.mult).then_inc(mqk_ready.sem, 1)

                conv(0)
                low.upto(12)
                conv_silu(0)
                low.upto(13)
                b_row, a_row, negM, m_row = (g_rows[:, i, :] for i in range(4))
                dve.wait_ge(mqk_ready.sem, mqk_ready.at(l, 1))
                dve.wait_ge(k.chunk_done, st.results(l, 12))
                dve.tensor_scalar(a_row, k.ps[0:MH, 2, 0:SEQ], par[0:MH, PA_MG:PA_END], None, ALU.add).then_inc(ch.sem, ch.one())
                dve.tensor_scalar(forget, k.ps[32:32 + MH, 2, 0:SEQ], par[32:32 + MH, PA_MG:PA_END], None, ALU.add)\
                   .then_inc(ch.sem, ch.one())
                dve.wait_ge(ch.sem, ch.at(l))
                dve.scalar_tensor_tensor(fall, forget, -1.0, forget, ALU.mult, ALU.max).then_inc(gate_ready.sem, 1)
                conv(1)
                low.upto(14)
                conv_silu(1)
                dve.wait_ge(gexp_ready.sem, gexp_ready.at(l, 2))
                dve.scalar_tensor_tensor(b_row, forget, 0.0, fall, ALU.min, ALU.subtract).then_inc(ch.sem, ch.one())

                def masked_max(qt):
                    dve.wait_ge(sc_done.sem, sc_done.at(l, 2 - qt))
                    n = (qt + 1) * P
                    lo, banks = (0, slice(2, 4)) if qt == 0 else (P, slice(4, 8))
                    src = k.ps[:, banks, :].rearrange("p b (h n) -> p (b h) n", n=n)
                    dve.tensor_tensor(logit[qt], src, mid(att_add[:, lo:lo + n], AH), ALU.add).then_inc(ch.sem, ch.one())
                    dve.wait_ge(ch.sem, ch.at(l))
                    dve.tensor_reduce(rmax[:, qt, :], logit[qt], AX.X, ALU.max).then_inc(ch.sem, ch.one())
                    dve.wait_ge(ch.sem, ch.at(l))
                    dve.tensor_scalar(rmax[:, qt, :], rmax[:, qt, :], -(AD ** -0.5), None, ALU.mult).then_inc(max_ready.sem, 1)

                def patterns(qt):
                    dve.wait_ge(exp_ready.sem, exp_ready.at(l, 2 - qt))
                    lo, n = (0, P) if qt == 0 else (P, 2 * P)
                    dve.tensor_tensor(logit[qt], logit[qt], mid(att_mult[:, lo:lo + n], AH), ALU.mult).then_inc(p_ready.sem, 1)

                dve.wait_ge(const_loaded.sem, const_loaded.at(0, 16))
                masked_max(1)
                low.upto(15)
                one4 = ones[0:MH, :]
                dve.tensor_tensor_scan(b_row, one4, b_row, 0.0, ALU.mult, ALU.add).then_inc(ch.sem, ch.one())
                dve.wait_ge(ch.sem, ch.at(l))
                dve.tensor_tensor(a_row, a_row, b_row, ALU.subtract).then_inc(ch.sem, ch.one())
                dve.wait_ge(ch.sem, ch.at(l))
                dve.tensor_tensor_scan(m_row, a_row, a_row, 0.0, ALU.max, ALU.max).then_inc(ch.sem, ch.one())
                dve.wait_ge(ch.sem, ch.at(l))
                dve.tensor_scalar(negM, m_row, -1.0, None, ALU.mult).then_inc(ch.sem, ch.one())
                dve.wait_ge(ch.sem, ch.at(l))
                dve.tensor_tensor(m_row, m_row, b_row, ALU.add).then_inc(rows_ready.sem, 1)
                masked_max(0)
                patterns(1)
                low.upto(16)
                dve.wait_ge(nm_done.sem, nm_done.at(l, 1))
                src = k.ps[:, 4:6, :].rearrange("p b (h n) -> p (b h) n", n=SEQ)
                dve.tensor_copy(ml_cols[:, :, :, :].rearrange("p a t h -> p (a t h)"), k.ps[:, 6, 0:2 * TT * MH]).then_inc(ch.sem, ch.one())
                dve.tensor_tensor(ml_w[0], src, mid(ml_add[:, 0:SEQ], MH), ALU.add).then_inc(ch.sem, ch.one())
                dve.tensor_tensor(ml_w[1], src[:, :, P:SEQ], mid(ml_add[:, SEQ:SEQ + P], MH), ALU.add).then_inc(epre_ready.sem, 1)
                patterns(0)
                low.upto(17)
                dve.wait_ge(s_done.sem, s_done.at(l, 1))
                dve.wait_ge(et_ready.sem, et_ready.at(l, 1))
                scale = MD ** -0.5 / 4
                dve.scalar_tensor_tensor(ml_w[0], k.ps[:, 2:4, :].rearrange("p b (h n) -> p (b h) n", n=SEQ),
                                               scale, ml_w[0], ALU.mult, ALU.mult).then_inc(ch.sem, ch.one())
                dve.scalar_tensor_tensor(ml_w[1], k.ps[:, 7, :].rearrange("p (h n) -> p h n", n=P),
                                         scale, ml_w[1], ALU.mult, ALU.mult).then_inc(wt_ready.sem, 1)
                low.upto(18)
                dve.wait_ge(num_done.sem, num_done.at(l, 1))
                den, r, q_, v_, s_, y_ = (small[:, i, :] for i in range(6))
                dve.tensor_copy(den, k.ps[:, 6, 64:64 + TT * MH]).then_inc(ch.sem, ch.one())
                dve.wait_ge(ch.sem, ch.at(l))
                dve.scalar_tensor_tensor(den, den, -1.0, den, ALU.mult, ALU.max).then_inc(ch.sem, ch.one())
                dve.wait_ge(ch.sem, ch.at(l))
                dve.tensor_tensor(den, den, exp_m[:, :, :].rearrange("p t h -> p (t h)"), ALU.max).then_inc(ch.sem, ch.one())
                dve.wait_ge(ch.sem, ch.at(l))
                dve.reciprocal(r, den).then_inc(ch.sem, ch.one())
                dve.wait_ge(num_copied.sem, num_copied.at(l, 1))
                sq = R3[:, 0:TT * MH * MD].rearrange("p (g d) -> p g d", d=MD)
                dve.tensor_tensor(sq, hn_v, hn_v, ALU.mult).then_inc(ch.sem, ch.one())
                dve.wait_ge(ch.sem, ch.at(l))
                dve.tensor_reduce(s_, sq, AX.X, ALU.add).then_inc(ch.sem, ch.one())
                dve.tensor_tensor(q_, r, r, ALU.mult).then_inc(ch.sem, ch.one())
                dve.wait_ge(ch.sem, ch.at(l))
                dve.tensor_tensor(v_, q_, s_, ALU.mult).then_inc(ch.sem, ch.one())
                dve.wait_ge(ch.sem, ch.at(l))
                dve.tensor_scalar(v_, v_, 0.5 / MD, 0.5 * EPS, ALU.mult, ALU.add).then_inc(ch.sem, ch.one())
                dve.wait_ge(ch.sem, ch.at(l))
                rsqrt(dve, ch, l, y_, v_, s_)
                dve.tensor_tensor(y_, y_, r, ALU.mult).then_inc(ch.sem, ch.one())
                dve.wait_ge(ch.sem, ch.at(l))
                dve.tensor_tensor(hn_v, hn_v, last(y_, MD), ALU.mult).then_inc(hn_ready.sem, 1)
                low.upto(19)
                dve.wait_ge(f_evicted.sem, f_evicted.at(l, 6))
                dve.tensor_scalar(mo[:, :, :], mo[:, :, :], 0.5, 0.5, ALU.mult, ALU.add).then_inc(ch.sem, ch.one())
                dve.wait_ge(ch.sem, ch.at(l))
                low.upto(20)
                dve.wait_ge(hnT_done.sem, hnT_done.at(l, 1))
                for h in range(MH):
                    ins = dve.scalar_tensor_tensor(hn[:, h * SEQ:(h + 1) * SEQ], k.ps[:, 2 + h // 2, (h % 2) * SEQ:(h % 2 + 1) * SEQ],
                                                   par[:, PA_MN + h:PA_MN + h + 1], mo[:, h, :], ALU.mult, ALU.mult)
                ins.then_inc(yb_ready.sem, 1)
                low.upto(21)
                dve.wait_ge(pv_done.sem, pv_done.at(l, 1))
                for qt in range(TT):
                    for par_ in range(2):
                        src = k.ps[:, 4 + 2 * qt + par_, 0:4 * (AD + 1)].rearrange("p (j d) -> p j d", j=4)
                        dve.reciprocal(rsum[:, qt, 4 * par_:4 * par_ + 4], src[:, :, AD]).then_inc(ch.sem, ch.one())
                dve.wait_ge(ch.sem, ch.at(l))
                for qt in range(TT):
                    for par_ in range(2):
                        src = k.ps[:, 4 + 2 * qt + par_, 0:4 * (AD + 1)].rearrange("p (j d) -> p j d", j=4)
                        ins = dve.tensor_tensor(ya_v[:, qt, :, par_, :], src[:, :, 0:AD],
                                                last(rsum[:, qt, 4 * par_:4 * par_ + 4], AD), ALU.mult)
                ins.then_inc(ya_ready.sem, 1)
                low.upto(22)
                dve.wait_ge(ybH_ready.sem, ybH_ready.at(l, 1))
                dve.tensor_tensor(yL[:, 4:8, :].rearrange("p f n -> p (f n)"), hn[:, :],
                                  yH[:, 4:8, :].rearrange("p f n -> p (f n)").bitcast(F32), ALU.subtract).then_inc(yb_split.sem, 1)
                low.upto(23)
                dve.wait_ge(yaH_ready.sem, yaH_ready.at(l, 1))
                dve.tensor_tensor(yL[:, 0:4, :].rearrange("p f n -> p (f n)"),
                                  k.ps[:, 4:6, :].rearrange("p b n -> p (b n)"),
                                  yH[:, 0:4, :].rearrange("p f n -> p (f n)").bitcast(F32), ALU.subtract).then_inc(ya_split.sem, 1)
                low.upto(24)
                dve.wait_ge(f_evicted.sem, f_evicted.at(l, 14))
                for i in range(4):
                    low.upto(min(24 + i + 1, FFC))
                    dve.wait_ge(k.chunk_done, st.results(l, 23 + i))
                    b = 2 * (i % 2)
                    dve.scalar_tensor_tensor(mix_t, gates[:, 2 * i:2 * i + 2, :].rearrange("p f n -> p (f n)"),
                                                   1.0, k.ps[:, b, :], ALU.add, ALU.mult).then_inc(ch.sem, ch.one())
                    dve.scalar_tensor_tensor(mixed[:, i % 2, :], gates[:, 8 + 2 * i:10 + 2 * i, :].rearrange("p f n -> p (f n)"),
                                                   1.0, k.ps[:, b + 1, :], ALU.add, ALU.mult).then_inc(ch.sem, ch.one())
                    dve.wait_ge(ch.sem, ch.at(l))
                    dve.tensor_tensor(mixed[:, i % 2, :], mixed[:, i % 2, :], mix_t, ALU.add).then_inc(mix_ready.sem, 1)
                    dve.wait_ge(mixH_ready.sem, mixH_ready.at(l, i + 1))
                    dve.scalar_tensor_tensor(k.aL[:, 2 * i:2 * i + 2, :].rearrange("p f n -> p (f n)"), mixed[:, i % 2, :], 0.5,
                                             k.aH[:, 2 * i:2 * i + 2, :].rearrange("p f n -> p (f n)").bitcast(F32),
                                             ALU.mult, ALU.subtract).then_inc(mix_split.sem, 1)
                for c in range(28, FFC):
                    low.upto(c)
                low.upto(FFC)
                residual(k, dve, st, l, FFC - 1, 1)
                norm_rstd(k, dve, ch, l, 1)
                low.upto(FFC + 1)
                norm_low(k, dve, l, 1, par[:, PA_MLP:PA_BQK])
                low.upto(FFC + 2)

                def unit(j, lows, trips=0, q=0):
                    dve.wait_ge(relu_ready.sem, l * FF_A + q + (j + 1))
                    r = hid_r[:, j % 3, :]
                    dve.tensor_tensor(r, r, r, ALU.mult).then_inc(sq_ready.sem, 1)
                    if lows:
                        split_low(k, dve, st, l, lows[0], trips)
                    dve.wait_ge(hidH_ready.sem, l * FF_A + q + (j + 1))
                    dve.tensor_tensor(hidL[:, j % 3, :], r, hidH[:, j % 3, :].bitcast(F32), ALU.subtract)\
                        .then_inc(hid_ready.sem, 1)
                    for c in lows[1:]:
                        split_low(k, dve, st, l, c, trips)

                unit(0, [FFC + 3])
                unit(1, [FFC + 4])
                unit(2, [FFC + 5, FFC + 6])
                with dve.Fori(0, 4) as q:
                    for j in range(3, 6):
                        unit(j, [up_chunk(j) + 3, up_chunk(j) + 4], q * 2, q * 3)
                unit(15, [up_chunk(15) + 3])
                split_ahead(split_low, k, dve, st, l + 1, AHEAD_LOW)
                residual(k, dve, st, l, CA - 1, 2)
                assert ch.n == DVE_A, ch.n
            dve.wait_ge(k.ss_ready.sem, k.ss_ready.at(DEPTH, TT))
            ch = Chain(fin.sem, 0)
            dve.tensor_scalar(k.var[:, 0:TT], k.ss[:, 0:TT], 0.5 / DM, 0.5 * EPS, ALU.mult, ALU.add).then_inc(ch.sem, ch.one())
            dve.wait_ge(ch.sem, ch.at(0))
            rsqrt(dve, ch, 0, k.rstd[:, 0:TT], k.var[:, 0:TT], k.tmp[:, 0:TT])
            dve.wait_ge(row_loaded.sem, row_loaded.at(DEPTH, 16))
            for tt in range(TT):
                dve.scalar_tensor_tensor(k.x[:, tt, :], k.x[:, tt, :], k.rstd[:, tt:tt + 1], rows[:, 0:DM],
                                               ALU.mult, ALU.mult).then_inc(ch.sem, ch.one())
            dve.wait_ge(ch.sem, ch.at(0))

        @block.tensor
        def _(pe):
            aop = lambda kt: (k.aH[:, kt, :], k.aL[:, kt, :])
            yop = lambda kt: (yH[:, kt, :], yL[:, kt, :])
            pe.sem_inc(k.chunk_done, SLOTS)
            pe.wait_ge(rel_rep_ready.sem, rel_rep_ready.at(0, 1))
            for h in range(BH):
                ins = pe.matmul(k.ps[:, h // 2, (h % 2) * SEQ:(h % 2 + 1) * SEQ], rel_rep[:, h, :], hot, start=True, stop=True)
            ins.then_inc(line_done.sem, 1)
            pe.wait_ge(line_ready.sem, line_ready.at(0, 1))
            with pe.Fori(0, DEPTH) as l:
                norm_transpose(k, pe, l, 0)
                for n in range(4):
                    for half in range(2):
                        c = 2 * n + half
                        pe.wait_ge(k.lo_ready, st.count(l, c))
                        if n == 0:
                            pe.wait_ge(k.a_ready.sem, k.a_ready.at(l, 2 * half + 2))
                        if half == 0 and n >= 2:
                            pe.wait_ge(t_evicted.sem, t_evicted.at(l, n - 1))
                        t_chunk(k, pe, c, range(4 * half, 4 * half + 4), 512, aop,
                                lambda tt, h: k.ps[:, 2 * (n % 2) + tt, :], half == 0, half == 1)
                pe.wait_ge(rope_ready.sem, rope_ready.at(l, 1))
                for b in range(4):
                    for n in range(2):
                        for tt in range(TT):
                            f = 2 * b + n
                            ins = pe.transpose(k.ps[:, 4 + b, n * SEQ + tt * P:n * SEQ + (tt + 1) * P], qk_tok[:, tt, 2 * f:2 * f + 2, :].rearrange("p h d -> p (h d)"), k.ident)
                    ins.then_inc(qkT_done.sem, 1)

                def feature(i, c):
                    pe.wait_ge(k.lo_ready, st.count(l, c))
                    if i >= 2:
                        pe.wait_ge(f_evicted.sem, f_evicted.at(l, i - 1))
                    else:
                        pe.wait_ge(t_evicted.sem, t_evicted.at(l, 3))
                    f_chunk(k, pe, c, [i % 2], [range(8)], aop)

                for i in range(4):
                    feature(i, GF[i])
                pe.wait_ge(k.lo_ready, st.count(l, 12))
                pe.wait_ge(t_evicted.sem, t_evicted.at(l, 4))
                f_chunk(k, pe, 12, [2], [range(8)], aop, tiles=1)

                pe.wait_ge(qkF_ready.sem, qkF_ready.at(l, 4))
                pe.wait_ge(gate_ready.sem, gate_ready.at(l, 1))
                for qt in (1, 0):
                    n = (qt + 1) * P
                    for h in range(AH):
                        j, e = head_slot(h)
                        if qt == 0:
                            out = k.ps[:, 2 + e, j * P:(j + 1) * P]
                        else:
                            out = k.ps[:, 4 + 2 * e + j // 2, (j % 2) * SEQ:(j % 2 + 1) * SEQ]
                        rows_ = slice(e * AD, (e + 1) * AD)
                        ins = pe.matmul(out, qkF[rows_, j, qt * P:(qt + 1) * P], qkF[rows_, 4 + j, 0:n],
                                        start=True, stop=True)
                    ins.then_inc(sc_done.sem, 1)
                feature(4, 13)
                feature(5, 14)
                pe.wait_ge(rows_ready.sem, rows_ready.at(l, 1))
                pe.wait_ge(max_ready.sem, max_ready.at(l, 1))
                for h in range(MH):
                    pe.matmul(k.ps[:, 4 + h // 2, (h % 2) * SEQ:(h % 2 + 1) * SEQ], sel[:, h, :], g_rows[:, 2, :],
                              start=True, stop=True)
                for i, row in enumerate((1, 3)):
                    for tt in range(TT):
                        ins = pe.transpose(k.ps[:, 6, (2 * i + tt) * MH:(2 * i + tt + 1) * MH], g_rows[:, row, tt * P:(tt + 1) * P], k.ident[0:MH, 0:MH])
                ins.then_inc(nm_done.sem, 1)
                feature(6, 15)
                pe.wait_ge(mqk_ready.sem, mqk_ready.at(l, 2))
                pe.wait_ge(max_ready.sem, max_ready.at(l, 2))
                for h in range(MH):
                    pe.matmul(k.ps[:, 2 + h // 2, (h % 2) * SEQ:(h % 2 + 1) * SEQ], mqk[:, 4 + h, 0:P], mqk[:, h, :],
                              start=True, stop=True)
                for h in range(MH):
                    ins = pe.matmul(k.ps[:, 7, h * P:(h + 1) * P], mqk[:, 4 + h, P:SEQ], mqk[:, h, P:SEQ],
                                    start=True, stop=True)
                ins.then_inc(s_done.sem, 1)
                feature(7, 16)
                pe.wait_ge(wt_ready.sem, wt_ready.at(l, 1))
                for h in range(MH):
                    pe.matmul(k.ps[:, 2, h * P:(h + 1) * P], ml_w[0][:, h, 0:P], mv_tok[:, 0, h, :], start=True, stop=True)
                    pe.matmul(k.ps[:, 3, h * P:(h + 1) * P], ml_w[0][:, h, P:SEQ], mv_tok[:, 0, h, :], start=True, stop=False)
                    pe.matmul(k.ps[:, 3, h * P:(h + 1) * P], ml_w[1][:, h, :], mv_tok[:, 1, h, :], start=False, stop=True)
                for h in range(MH):
                    d0, d1 = (k.ps[:, 6, 64 + tt * MH + h:65 + tt * MH + h] for tt in range(TT))
                    pe.matmul(d0, ml_w[0][:, h, 0:P], ones[:, 0:1], start=True, stop=True)
                    pe.matmul(d1, ml_w[0][:, h, P:SEQ], ones[:, 0:1], start=True, stop=False)
                    ins = pe.matmul(d1, ml_w[1][:, h, :], ones[:, 0:1], start=False, stop=True)
                ins.then_inc(num_done.sem, 1)
                feature(8, 17)

                def weights_T(i):
                    for n, b in enumerate(((4, 5), (6, 7), (4, 5))[i]):
                        for s in range(4):
                            if i < 2:
                                h, kb = 4 * i + 2 * n + s // 2, s % 2
                                src = logit[1][:, h, kb * P:(kb + 1) * P]
                            else:
                                src = logit[0][:, 4 * n + s, :]
                            ins = pe.transpose(k.ps[:, b, s * P:(s + 1) * P], src, k.ident)
                    ins.then_inc(pT_done.sem, 1)

                pe.wait_ge(p_ready.sem, p_ready.at(l, 1))
                weights_T(0)
                pe.wait_ge(hn_ready.sem, hn_ready.at(l, 1))
                weights_T(1)
                for h in range(MH):
                    for tt in range(TT):
                        ins = pe.transpose(k.ps[:, 2 + h // 2, (h % 2) * SEQ + tt * P:(h % 2) * SEQ + (tt + 1) * P], hn_v[:, tt * MH + h, :], k.ident)
                ins.then_inc(hnT_done.sem, 1)
                feature(9, 18)
                pe.wait_ge(p_ready.sem, p_ready.at(l, 2))
                pe.wait_ge(pT_ready.sem, pT_ready.at(l, 1))
                weights_T(2)
                feature(10, 19)
                feature(11, 20)
                pe.wait_ge(pT_ready.sem, pT_ready.at(l, 3))
                for qt in range(TT):
                    for h in range(AH):
                        j, e = head_slot(h)
                        out = k.ps[:, 4 + 2 * qt + e, j * (AD + 1):(j + 1) * (AD + 1)]
                        for s in range(qt + 1):
                            ins = pe.matmul(out, pT[:, 4 * e + j, s + qt, :], v_tok[:, s, h, :], start=s == 0, stop=s == qt)
                ins.then_inc(pv_done.sem, 1)
                feature(12, 21)
                pe.wait_ge(ya_ready.sem, ya_ready.at(l, 1))
                for f in range(4):
                    for tt in range(TT):
                        ins = pe.transpose(k.ps[:, 4 + f // 2, (f % 2) * SEQ + tt * P:(f % 2) * SEQ + (tt + 1) * P], ya[:, tt * 512 + f * P:tt * 512 + (f + 1) * P], k.ident)
                ins.then_inc(yaT_done.sem, 1)
                feature(13, 22)
                for i in range(4):
                    c = 23 + i
                    pe.wait_ge(k.lo_ready, st.count(l, c))
                    if i == 0:
                        pe.wait_ge(yb_split.sem, yb_split.at(l, 1))
                        pe.wait_ge(ya_split.sem, ya_split.at(l, 1))
                        pe.wait_ge(f_evicted.sem, f_evicted.at(l, 14))
                    if i >= 2:
                        pe.wait_ge(mix_ready.sem, mix_ready.at(l, i - 1))
                    b = 2 * (i % 2)
                    f_chunk(k, pe, c, [b, b + 1], [range(4), range(4, 8)], yop)
                t_out = lambda tt, h: k.ps[:, 4 + 2 * tt + h, :]
                for i in range(4):
                    c = 27 + i
                    pe.wait_ge(k.lo_ready, st.count(l, c))
                    pe.wait_ge(mix_split.sem, mix_split.at(l, i + 1))
                    if i < 2:
                        t_chunk(k, pe, c, range(2 * i, 2 * i + 2), DM, aop, t_out, i == 0, False)
                t_last(k, pe, [(27 + i, lambda kt, i=i: aop(2 * i + kt)) for i in (2, 3)], t_out)
                norm_transpose(k, pe, l, 1)

                def up(j, c, trips=0, q=0):
                    pe.wait_ge(k.lo_ready, st.count(l, c, trips))
                    if j >= 3:
                        pe.wait_ge(relu_ready.sem, l * FF_A + q + (j - 2))
                    f_chunk(k, pe, c, [j % 3], [range(8)], aop,
                            (lambda i: k.a_ready.at(l, 4 + i + 1)) if j == 0 else None)

                def down(j, c, trips=0, q=0):
                    pe.wait_ge(k.lo_ready, st.count(l, c, trips))
                    pe.wait_ge(hid_ready.sem, l * FF_A + q + (j + 1))
                    hid = lambda kt: [x[:, j % 3, kt * SEQ:(kt + 1) * SEQ] for x in (hidH, hidL)]
                    t_chunk(k, pe, c, range(2), DM, hid, t_out, j == 0, j == FF_A - 1,
                            k.tile_done.sem if j == FF_A - 1 else None)

                up(0, up_chunk(0))
                up(1, up_chunk(1))
                up(2, up_chunk(2))
                down(0, down_chunk(0))
                with pe.Fori(0, 4) as q:
                    for j in range(1, 4):
                        up(j + 2, up_chunk(j + 2), q * 2, q * 3)
                        down(j, down_chunk(j), q * 2, q * 3)
                up(15, up_chunk(15))
                for j in range(13, 16):
                    down(j, down_chunk(j))


(PB_N1, PB_NM, PB_N2, PB_DW, PB_CB, PB_LG, PB_LB, PB_PS, PB_GB, PB_WI, PB_WS, PB_PW, PB_VG, PB_END) = np.cumsum(
    [0, 8, 8, 8, 2 * TAPS, 2, 2, 2, 2, 4, 8 * IH, 4 * P, 2 * 64, 0])
POOL_PAD = 16
CONV_PAD = TAPS - 1
POOL_TAPS = 16
OUT_OF_REACH = -3e38
TAKEN = float(np.float32(-3.3e38))
DVE_B = 198
POOL_B = 63


def second_block(nc, k, d, sems):
    with ExitStack() as ctx:
        def sb(name, shape, dt=F32):
            return ctx.enter_context(nc.sbuf_tensor(name, shape, dt))

        def sig(name, per, start=0):
            return Signal(sems.enter_context(nc.semaphore("b_" + name)), per, start)

        st = Stream(DEPTH * CA, CB)
        consts = k.consts
        k.ident = consts[:, KB_ID:KB_ADD]
        reach = consts[:, KB_ADD:KB_CNT]
        inv_count = consts[:, KB_CNT:KB_TRI].rearrange("p (f n) -> p f n", f=2)
        tri = consts[:, KB_TRI:KB_END]
        par = k.par_b
        wi = par[:, PB_WI:PB_WS].rearrange("p (k n) -> p k n", k=KT)
        ws = par[:, PB_WS:PB_PW].rearrange("p (g n) -> p g n", g=4)
        pw = par[:, PB_PW:PB_VG].rearrange("p (j n) -> p j n", j=2)
        v_gain = consts[:, KB_END:KB_END + BW]
        gain_row = k.rows[:, 0:DM]
        bias = sb("bias", [P, BH, 3 * P])
        gates = sb("b_gates", [P, NBR * 8, SEQ])
        GU = sb("GU", [P, TT * 3 * BW])
        uv = GU[:, 0:TT * 2 * BW].rearrange("p (t n) -> p t n", t=TT)
        vn = GU[:, TT * 2 * BW:].rearrange("p (t n) -> p t n", t=TT)
        pT = GU[:, :].rearrange("p (h b n) -> p h b n", h=BH, b=3)
        hid_r = GU[:, 0:2 * 512].rearrange("p (s n) -> p s n", s=2)
        y0 = sb("y0", [P, TT, BW])
        xc = y0
        qkF = sb("b_qkF", [P, 4, SEQ])
        v_tok = sb("b_v_tok", [P, TT, BH, BD + 1])
        idxF = sb("idxF", [P, 2, SEQ])
        RL = sb("RL", [P, IH * 3 * P])
        rel = RL[:, :].rearrange("p (h n) -> p h n", h=IH)
        logit = rel
        score = sb("score", [P, 3 * P])
        keep = sb("keep", [P, 3 * P])
        top8 = sb("top8", [P, TT, 8])
        diag = consts[:, KB_END + BW:KB_END + BW + TT * P].rearrange("p (t n) -> p t n", t=TT)
        wi_hi, wi_lo = (sb(n, [P, KT, IH], F32R) for n in ("wi_hi", "wi_lo"))
        w_idx = sb("w_idx", [P, TT, IH])
        rmax = sb("b_rmax", [P, TT, BH])
        rsum = sb("b_rsum", [P, TT, BH])
        yb2 = sb("yb2", [P, TT, BW])
        gated = [[RL[:, n * 512:(n + 1) * 512] for n in range(3)] + [y0[:, :, :].rearrange("p t n -> p (t n)")],
                 [GU[:, n * 512:(n + 1) * 512] for n in range(3)] + [yb2[:, :, :].rearrange("p t n -> p (t n)")]]
        pz = sb("pz", [P, 2, POOL_PAD + SEQ])
        sum2 = sb("sum2", [P, 2, POOL_PAD + SEQ])
        sum4 = sb("sum4", [P, 2, POOL_PAD + SEQ])
        sum8 = sb("sum8", [P, 1, POOL_PAD + SEQ])
        pooled = sb("pooled", [P, 2, SEQ])
        conv_x = sb("conv_x", [P, 2, CONV_PAD + SEQ])
        conv_y = sb("conv_y", [P, 2, SEQ])
        conv_p = sum4[:, :, 0:SEQ]
        weighed = [pooled[:, :, :], sum2[:, :, 0:SEQ]]
        cstat = sb("cstat", [P, 4, TT])
        vstat = sb("vstat", [P, 4, TT])
        pss = sb("pss", [P, 4, TT])
        yH = k.mixH[:, :].rearrange("p (f n) -> p f n", f=8)
        yL = k.mixL[:, :].rearrange("p (f n) -> p f n", f=8)
        hidH = k.mixH[:, 0:2 * 512].rearrange("p (s n) -> p s n", s=2)
        hidL = k.mixL[:, 0:2 * 512].rearrange("p (s n) -> p s n", s=2)
        flat = lambda v: v.rearrange("p f n -> p (f n)")

        const_loaded, par_loaded = Signal(k.consts_b_loaded, 16), Signal(k.par_b_loaded, 32)
        row_loaded, bias_moved = sig("row_loaded", 48), Signal(k.bias_moved, 0)
        k.x_new, k.ss_ready, k.tile_done = sig("x_new", 6), sig("ss_ready", 6), sig("tile_done", 3)
        k.rstd_ready, k.scaled0, k.scaled1 = sig("rstd_ready", 3), sig("scaled0", 6), sig("scaled1", 6)
        k.xs = gates[:, 16:24, :].rearrange("p (t a) n -> p t (a n)", t=TT)
        k.nT_done, k.aH_ready, k.a_ready = sig("nT_done", 12), sig("aH_ready", 12), sig("a_ready", 12)
        pss_ready, post_ready = sig("pss_ready", 6), sig("post_ready", 3)
        silu_ready, gated_ready, hidH_ready, hid_ready = (
            sig(n, 2 * FF_B) for n in ("silu_ready", "gated_ready", "hidH_ready", "hid_ready"))
        gelu_ready, vss_ready, vn_ready, gm_done, y0_ready, y0T_done, y0H_ready, y0_split = (
            sig(n, p) for n, p in (("gelu_ready", 2), ("vss_ready", 2), ("vn_ready", 1), ("gm_done", 1), ("y0_ready", 1),
                                   ("y0T_done", 1), ("y0H_ready", 1), ("y0_split", 1)))
        wi_high, wi_split, wi_done, wi_ready, rel_done, rel_ready = (
            sig(n, 1) for n in ("wi_high", "wi_split", "wi_done", "wi_ready", "rel_done", "rel_ready"))
        f_evicted, hc_ready, conv_done, pool_ready, taps_ready, conv_rest = (
            sig("f_evicted", 22), sig("hc_ready", 1), sig("conv_done", 1), sig("pool_ready", 1),
            sig("taps_ready", 1), sig("conv_rest", 1))
        ct_done, xc_ready, css_ready, cdiag_ready, lnT_done, ln_ready, lt_ready, y3_ready, y3H_ready, y3_split = (
            sig(n, 2 if n == "css_ready" else 1) for n in (
                "ct_done", "xc_ready", "css_ready", "cdiag_ready", "lnT_done", "ln_ready", "lt_ready", "y3_ready",
                "y3H_ready", "y3_split"))
        sc_done, l_ready, max_ready, exp_ready = sig("sc_done", 2), sig("l_ready", 2), sig("max_ready", 2), sig("exp_ready", 2)
        pT_done, pT_ready, pv_done, y2_ready, y2T_done, y2H_ready, y2_split = (
            sig(n, p) for n, p in (("pT_done", 2), ("pT_ready", 2), ("pv_done", 1), ("y2_ready", 1), ("y2T_done", 1),
                                   ("y2H_ready", 1), ("y2_split", 1)))
        pmm_done, y1H_ready, y1_split = (sig(n, 1) for n in ("pmm_done", "y1H_ready", "y1_split"))
        mix_ready, mixH_ready, mix_split = (sig(n, 4) for n in ("mix_ready", "mixH_ready", "mix_split"))
        branch_ready = sig("branch_ready", 4 * NBR)
        dve_chain, pool_chain, pool_pre = sig("dve_chain", DVE_B), sig("pool_chain", POOL_B), sig("pool_pre", 0)
        block = ctx.enter_context(nc.Block())

        F0 = (0, CB - 3 * FF_B)
        M0 = 3 * FF_B
        G0 = M0 + 9
        BR = M0 + 25
        WO = BR + 4

        def a_chunk(f, j):
            return F0[f] + (3 * j - 1 if j else 0)

        def b_chunk(f, j):
            return F0[f] + (3 * j if j else 1)

        def down_chunk(f, j):
            return F0[f] + (3 * j + 4 if j < FF_B - 1 else 3 * FF_B - 1)

        @block.gpsimd
        def _(pool):
            pool.dma_start(v_gain[:, :], d.v_gain[0].partition_broadcast(P)).then_inc(par_loaded.sem, 16)
            pool.dma_start(gain_row[:, :], d.post_gains[0].partition_broadcast(P)).then_inc(row_loaded.sem, 16)
            pool.wait_ge(bias_moved.sem, bias_moved.at(0, 16))
            for h in range(BH):
                j, e = head_slot(h)
                for qt in range(TT):
                    n = (qt + 1) * P
                    lo = 0 if qt == 0 else P
                    skew = bass.AP(tensor=d.bias_line.tensor, offset=h * 2 * SEQ + SEQ - 1 - qt * P,
                                   ap=[[BH * 2 * SEQ - 1, P], [1, n]])
                    pool.dma_start(bias[:, 2 * e + j, lo:lo + n], skew).then_inc(bias_moved.sem, 16)
            zc = Chain(pool_pre.sem, 0)
            pool.memset(pz[:, :, 0:POOL_PAD], 0.0).then_inc(zc.sem, zc.one())
            pool.wait_ge(zc.sem, zc.at(0))
            pool.memset(conv_x[:, :, 0:CONV_PAD], 0.0).then_inc(zc.sem, zc.one())
            pool.wait_ge(zc.sem, zc.at(0))
            with pool.Fori(0, DEPTH) as l:
                ch = Chain(pool_chain.sem, POOL_B)
                value = held(pool, par_loaded.at(l, 32))
                pool.wait_ge(const_loaded.sem, 16)
                pool.wait_ge(par_loaded.sem, value)
                taps = par[:, PB_DW:PB_CB]
                pool.tensor_scalar(taps, taps, 0.5, None, ALU.mult).then_inc(taps_ready.sem, 1)
                pool.wait_ge(taps_ready.sem, taps_ready.at(l, 1))
                pool.wait_ge(post_ready.sem, post_ready.at(l, 1))
                pool.tensor_tensor(k.x[:, 0, :], k.x[:, 0, :], k.xs[:, 0, :], ALU.add).then_inc(k.x_new.sem, 1)
                pool.wait_ge(k.x_new.sem, k.x_new.at(l, 4))
                pool.dma_start(gain_row[:, :], d.post_gains[l * 3 + 1].partition_broadcast(P)).then_inc(row_loaded.sem, 16)
                value = held(pool, hc_ready.at(l, 1))
                pool.wait_ge(const_loaded.sem, 16)
                pool.wait_ge(hc_ready.sem, value)

                def weigh(t):
                    for f in range(2):
                        w = par[:, PB_DW + 2 * t + f:PB_DW + 2 * t + f + 1]
                        value = held(pool, ch.at(l, f))
                        pool.wait_ge(const_loaded.sem, 16)
                        pool.wait_ge(ch.sem, value)
                        if t == 0:
                            pool.tensor_scalar(conv_p[:, f, :], conv_x[:, f, 0:SEQ], w, par[:, PB_CB + f:PB_CB + f + 1],
                                                     ALU.mult, ALU.add).then_inc(ch.sem, ch.one())
                        else:
                            pool.tensor_scalar(weighed[t % 2][:, f, :], conv_x[:, f, t:t + SEQ], w, None, ALU.mult).then_inc(ch.sem, ch.one())

                weigh(0)
                weigh(1)
                for t in range(1, POOL_TAPS):
                    if t + 1 < POOL_TAPS:
                        weigh(t + 1)
                        pool.wait_ge(ch.sem, ch.at(l, 2))
                    else:
                        pool.wait_ge(ch.sem, ch.at(l))
                    pool.tensor_tensor(conv_p, conv_p, weighed[t % 2], ALU.add).then_inc(ch.sem, ch.one())
                pool.wait_ge(ch.sem, ch.at(l))
                pool.wait_ge(conv_rest.sem, conv_rest.at(l, 1))
                pool.tensor_tensor(conv_y[:, :, :], conv_y[:, :, :], conv_p, ALU.add).then_inc(conv_done.sem, 1)
                pool.wait_ge(conv_done.sem, conv_done.at(l, 1))
                pool.wait_ge(f_evicted.sem, f_evicted.at(l, 3))
                N = POOL_PAD + SEQ
                add = lambda o, a, s, lo: pool.tensor_tensor(o[:, :, lo:N], a[:, :, lo:N], a[:, :, lo - s:N - s], ALU.add).then_inc(ch.sem, ch.one())
                add(sum2, pz, 1, 1)
                pool.wait_ge(ch.sem, ch.at(l))
                add(sum4, sum2, 2, 3)
                pool.wait_ge(ch.sem, ch.at(l))
                pool.tensor_tensor(pooled[0:64, 0, :], sum2[0:64, 0, POOL_PAD:], inv_count[0:64, 0, :], ALU.mult).then_inc(ch.sem, ch.one())
                pool.wait_ge(ch.sem, ch.at(l))
                add(sum8, sum4[:, 1:2, :], 4, 7)
                pool.wait_ge(ch.sem, ch.at(l))
                pool.tensor_tensor(pooled[64:P, 0, :], sum4[64:P, 0, POOL_PAD:], inv_count[64:P, 0, :], ALU.mult).then_inc(ch.sem, ch.one())
                pool.wait_ge(ch.sem, ch.at(l))
                add(sum2[:, 1:2, :], sum8, 8, 15)
                pool.wait_ge(ch.sem, ch.at(l))
                pool.tensor_tensor(pooled[0:64, 1, :], sum8[0:64, 0, POOL_PAD:], inv_count[0:64, 1, :], ALU.mult).then_inc(ch.sem, ch.one())
                pool.wait_ge(ch.sem, ch.at(l))
                pool.tensor_tensor(pooled[64:P, 1, :], sum2[64:P, 1, POOL_PAD:], inv_count[64:P, 1, :], ALU.mult).then_inc(ch.sem, ch.one())
                pool.wait_ge(ch.sem, ch.at(l))
                pool.tensor_tensor(pooled[:, :, :], pooled[:, :, :], pz[:, :, POOL_PAD:], ALU.subtract).then_inc(pool_ready.sem, 1)
                for i in range(4):
                    g = gated[i % 2]
                    for n in (0, 2):
                        pool.wait_ge(branch_ready.sem, branch_ready.at(l, NBR * i + n + 2))
                        pool.tensor_tensor(g[n], g[n], g[n + 1], ALU.add).then_inc(ch.sem, ch.one())
                    pool.wait_ge(ch.sem, ch.at(l))
                    pool.tensor_tensor(g[0], g[0], g[2], ALU.add).then_inc(mix_ready.sem, 1)
                pool.wait_ge(post_ready.sem, post_ready.at(l, 2))
                pool.tensor_tensor(k.x[:, 0, :], k.x[:, 0, :], k.xs[:, 0, :], ALU.add).then_inc(k.x_new.sem, 1)
                pool.wait_ge(k.x_new.sem, k.x_new.at(l, 6))
                pool.dma_start(gain_row[:, :], d.post_gains[l * 3 + 2].partition_broadcast(P)).then_inc(row_loaded.sem, 16)
                pool.wait_ge(k.a_ready.sem, k.a_ready.at(l, 12))
                pool.dma_start(par[:, :], d.par_b[bass.ds((l + 1) * P, P), :]).then_inc(par_loaded.sem, 16)
                pool.dma_start(v_gain[:, :], d.v_gain[l + 1].partition_broadcast(P)).then_inc(par_loaded.sem, 16)
                pool.wait_ge(post_ready.sem, post_ready.at(l, 3))
                pool.tensor_tensor(k.x[:, 0, :], k.x[:, 0, :], k.xs[:, 0, :], ALU.add).then_inc(k.x_new.sem, 1)
                pool.wait_ge(k.x_new.sem, k.x_new.at(l, 8))
                pool.dma_start(gain_row[:, :], d.post_gains[l * 3 + 3].partition_broadcast(P)).then_inc(row_loaded.sem, 16)
                assert ch.n == POOL_B, ("pool", ch.n)
            pool.wait_ge(par_loaded.sem, par_loaded.at(DEPTH, 32))
            pool.wait_ge(row_loaded.sem, row_loaded.at(DEPTH, 16))

        @block.sync
        def _(sp):
            with sp.Fori(1, DEPTH * CB // SLOTS) as g:
                for s in range(SLOTS):
                    sp.wait_ge(k.lo_ready, g * SLOTS + (DEPTH * CA + s - SLOTS + 1))
                    sp.dma_start(k.raw[:, s, :], d.w_b[g * SLOTS + s]).then_inc(k.raw_loaded[s], 16)
            for s in range(AHEAD_HIGH):
                sp.wait_ge(k.lo_ready, DEPTH * (CA + CB) + s - SLOTS + 1)
                sp.dma_start(k.raw[:, s, :], d.w_b[s]).then_inc(k.raw_loaded[s], 16)
            sp.wait_ge(k.x_new.sem, k.x_new.at(DEPTH, 2))
            for tt in range(TT):
                sp.dma_start(d.out[tt * P:(tt + 1) * P, :], k.x[:, tt, :]).then_inc(k.stored, 16)
            sp.wait_ge(k.stored, 16 * TT)

        @block.scalar
        def _(act):
            def mlp(l, high, f):
                def unit(j, highs, trips=0, q=0):
                    act.wait_ge(k.chunk_done, st.results(l, a_chunk(f, j), trips))
                    if j >= 2:
                        act.wait_ge(hid_ready.sem, (l * 2 + f) * FF_B + q + (j - 1))
                    act.activation(hid_r[:, j % 2, :], k.ps[:, 2 * (j % 2), :], ACT.Silu).then_inc(silu_ready.sem, 1)
                    for c in highs[:2]:
                        split_high(k, act, st, l, c, trips)
                    act.wait_ge(gated_ready.sem, (l * 2 + f) * FF_B + q + (j + 1))
                    act.activation(hidH[:, j % 2, :], hid_r[:, j % 2, :], ACT.Copy).then_inc(hidH_ready.sem, 1)
                    for c in highs[2:]:
                        split_high(k, act, st, l, c, trips)

                first = F0[f]
                unit(0, [first + 3, first + 4])
                with act.Fori(0, 4) as q:
                    for j in (1, 2):
                        unit(j, [first + 3 * j + i for i in (2, 3, 4)], q * 2, q * 2)
                unit(9, [first + 3 * 9 + i for i in (2, 3, 4)])
                unit(10, [first + 3 * 10 + 2])

            def post_stats(l, n, c, between=lambda: None):
                for tt in range(TT):
                    if tt == 0:
                        act.wait_ge(k.tile_done.sem, k.tile_done.at(l, n + 1))
                    else:
                        between()
                        act.wait_ge(k.chunk_done, st.results(l, c))
                    act.activation(k.xs[:, tt, :].rearrange("p (b n) -> p b n", b=2), k.ps[:, 4 + 2 * tt:6 + 2 * tt, :],
                                   ACT.Square, accum_out=pss[:, 0, tt:tt + 1]).then_inc(pss_ready.sem, 1)

            with act.Fori(0, DEPTH) as l:
                high = Splitter(split_high, k, act, st, l, AHEAD_HIGH)
                norm_stats(k, act, l, 0)
                norm_scale(k, act, l, 0)
                act.wait_ge(par_loaded.sem, par_loaded.at(l, 32))
                norm_high(k, act, l, 0, par[:, PB_N1:PB_NM])
                act.activation(wi_hi[:, :, :], wi, ACT.Copy).then_inc(wi_high.sem, 1)
                high.upto(F0[0] + 2)
                mlp(l, high, 0)
                high.next = M0
                high.upto(M0 + 1)
                post_stats(l, 0, M0 - 1)
                norm_stats(k, act, l, 1)
                norm_scale(k, act, l, 1)
                norm_high(k, act, l, 1, par[:, PB_NM:PB_N2])
                high.upto(M0 + 3)
                act.wait_ge(k.chunk_done, st.results(l, M0 + 1))
                for tt in range(TT):
                    act.activation(uv[:, tt, :], k.ps[:, 2 + tt, :], ACT.Gelu_apprx_tanh).then_inc(gelu_ready.sem, 1)
                act.wait_ge(gelu_ready.sem, gelu_ready.at(l, 2))
                for tt in range(TT):
                    act.activation(conv_y[:, tt, :], uv[:, tt, BW:], ACT.Square, accum_out=vstat[:, 0, tt:tt + 1])\
                       .then_inc(vss_ready.sem, 1)
                high.upto(M0 + 4)
                act.wait_ge(k.chunk_done, st.results(l, M0 + 2))
                act.activation(v_tok[:, :, :, 0:BD], k.ps[:, 0, :].rearrange("p (t h n) -> p t h n", t=TT, h=BH), ACT.Copy)\
                   .then_inc(f_evicted.sem, 1)
                high.upto(M0 + 6)
                act.wait_ge(k.chunk_done, st.results(l, M0 + 4))
                act.activation(flat(conv_y[:, :, :]), k.ps[:, 0, :], ACT.Tanh, scale=0.5).then_inc(f_evicted.sem, 1)
                high.upto(M0 + 7)
                act.wait_ge(k.chunk_done, st.results(l, M0 + 5))
                act.activation(pz[:, :, POOL_PAD:], k.ps[:, 1, :].rearrange("p (f n) -> p f n", f=2), ACT.Copy)\
                   .then_inc(f_evicted.sem, 1)
                high.upto(M0 + 8)
                act.wait_ge(k.chunk_done, st.results(l, M0 + 6))
                act.activation(flat(idxF[:, :, :]), k.ps[:, 0, :], ACT.Copy).then_inc(f_evicted.sem, 1)
                act.wait_ge(y0T_done.sem, y0T_done.at(l, 1))
                act.activation(flat(yH[:, 0:2, :]), k.ps[:, 3, :], ACT.Copy).then_inc(y0H_ready.sem, 1)
                high.upto(M0 + 9)
                for i in range(2):
                    act.wait_ge(k.chunk_done, st.results(l, M0 + 7 + i))
                    act.activation(flat(qkF[:, 2 * i:2 * i + 2, :]), k.ps[:, 1 - i, :], ACT.Copy).then_inc(f_evicted.sem, 1)
                    if i == 0:
                        act.wait_ge(rel_done.sem, rel_done.at(l, 1))
                        for h in range(IH):
                            ins = act.activation(rel[:, h, :], k.ps[:, 4 + h, 0:3 * P], ACT.Relu, scale=ID ** -0.5)
                        ins.then_inc(rel_ready.sem, 1)
                    high.upto(M0 + 10 + i)

                def gate_in(i):
                    act.wait_ge(k.chunk_done, st.results(l, G0 + i))
                    act.activation(flat(gates[:, 2 * i:2 * i + 2, :]), k.ps[:, (i + 1) % 2, :], ACT.Tanh, scale=0.5)\
                       .then_inc(f_evicted.sem, 1)
                    high.upto(G0 + i + 3)

                def soft(qt):
                    act.wait_ge(max_ready.sem, max_ready.at(l, 2 - qt))
                    n, lo = (P, 0) if qt == 0 else (2 * P, P)
                    for h in range(BH):
                        ins = act.activation(logit[:, h, lo:lo + n], logit[:, h, lo:lo + n], ACT.Exp,
                                             bias=rmax[:, qt, h:h + 1])
                    ins.then_inc(exp_ready.sem, 1)

                for i in range(7):
                    gate_in(i)
                soft(1)
                soft(0)
                gate_in(7)
                act.wait_ge(pT_done.sem, pT_done.at(l, 1))
                for n in range(2):
                    ins = act.activation(pT[:, 2 * n:2 * n + 2, 1:3, :],
                                         k.ps[:, 2 + n, :].rearrange("p (h b n) -> p h b n", h=2, b=2), ACT.Copy)
                ins.then_inc(pT_ready.sem, 1)
                act.wait_ge(pT_done.sem, pT_done.at(l, 2))
                act.activation(pT[:, :, 0, :], k.ps[:, 4, :].rearrange("p (h n) -> p h n", h=BH), ACT.Copy)\
                   .then_inc(pT_ready.sem, 1)
                gate_in(8)
                gate_in(9)
                act.wait_ge(y2T_done.sem, y2T_done.at(l, 1))
                act.activation(flat(yH[:, 4:6, :]), k.ps[:, 3, :], ACT.Copy).then_inc(y2H_ready.sem, 1)
                for i in range(10, 12):
                    gate_in(i)
                act.wait_ge(xc_ready.sem, xc_ready.at(l, 1))
                for tt in range(TT):
                    act.activation(conv_y[:, tt, :], xc[:, tt, :], ACT.Square, accum_out=cstat[:, 1, tt:tt + 1])\
                       .then_inc(css_ready.sem, 1)
                gate_in(12)
                act.wait_ge(lnT_done.sem, lnT_done.at(l, 1))
                for f in range(2):
                    ins = act.activation(conv_y[:, f, :], k.ps[:, 7, f * SEQ:(f + 1) * SEQ], ACT.Identity,
                                         scale=par[:, PB_LG + f:PB_LG + f + 1], bias=par[:, PB_LB + f:PB_LB + f + 1])
                ins.then_inc(ln_ready.sem, 1)
                act.wait_ge(ln_ready.sem, ln_ready.at(l, 1))
                act.activation(flat(xc[:, :, :]), flat(conv_y[:, :, :]), ACT.Tanh, scale=0.5).then_inc(lt_ready.sem, 1)
                gate_in(13)
                act.wait_ge(y3_ready.sem, y3_ready.at(l, 1))
                act.activation(flat(yH[:, 6:8, :]), flat(conv_y[:, :, :]), ACT.Copy, scale=0.5).then_inc(y3H_ready.sem, 1)
                act.wait_ge(pmm_done.sem, pmm_done.at(l, 1))
                for g in range(4):
                    j, e = g // 2, g % 2
                    half = slice(e * 64, (e + 1) * 64)
                    ins = act.activation(yH[half, 2 + j, :], k.ps[half, 4 + 2 * e, j * SEQ:(j + 1) * SEQ], ACT.Copy,
                                         scale=par[half, PB_PS + j:PB_PS + j + 1])
                ins.then_inc(y1H_ready.sem, 1)
                gate_in(14)
                gate_in(15)
                for i in range(4):
                    high.upto(BR + 3 + i)
                    act.wait_ge(mix_ready.sem, mix_ready.at(l, i + 1))
                    act.activation(flat(k.aH[:, 2 * i:2 * i + 2, :]), gated[i % 2][0], ACT.Copy, scale=0.5)\
                       .then_inc(mixH_ready.sem, 1)
                high.upto(F0[1])
                post_stats(l, 1, F0[1] - 1, lambda: high.upto(F0[1] + 1))
                norm_stats(k, act, l, 2)
                norm_scale(k, act, l, 2)
                norm_high(k, act, l, 2, par[:, PB_N2:PB_DW])
                high.upto(F0[1] + 2)
                mlp(l, high, 1)
                split_ahead(split_high, k, act, st, l + 1, AHEAD_HIGH)
                post_stats(l, 2, CB - 1)

        @block.vector
        def _(dve):
            dve.wait_ge(const_loaded.sem, 16)
            dve.memset(v_tok[:, :, :, BD:BD + 1], 1.0).then_inc(k.x_new.sem, TT)

            def mlp(l, low, f):
                def unit(j, lows, trips=0, q=0):
                    n = (l * 2 + f) * FF_B + q + (j + 1)
                    for c in lows[:1]:
                        split_low(k, dve, st, l, c, trips)
                    dve.wait_ge(silu_ready.sem, n)
                    dve.wait_ge(k.chunk_done, st.results(l, b_chunk(f, j), trips))
                    r = hid_r[:, j % 2, :]
                    dve.tensor_tensor(r, r, k.ps[:, 2 * (j % 2) + 1, :], ALU.mult).then_inc(gated_ready.sem, 1)
                    for c in lows[1:2]:
                        split_low(k, dve, st, l, c, trips)
                    dve.wait_ge(hidH_ready.sem, n)
                    dve.tensor_tensor(hidL[:, j % 2, :], r, hidH[:, j % 2, :].bitcast(F32), ALU.subtract)\
                       .then_inc(hid_ready.sem, 1)
                    for c in lows[2:]:
                        split_low(k, dve, st, l, c, trips)

                first = F0[f]
                unit(0, [first + 3, first + 4])
                with dve.Fori(0, 4) as q:
                    for j in (1, 2):
                        unit(j, [first + 3 * j + i for i in (2, 3, 4)], q * 2, q * 2)
                unit(9, [first + 3 * 9 + i for i in (2, 3, 4)])
                unit(10, [first + 3 * 10 + 2])

            def post(l, ch, n, half):
                for tt in range(TT):
                    var, r, t = (pss[:, i, tt:tt + 1] for i in (1, 2, 3))
                    dve.wait_ge(pss_ready.sem, pss_ready.at(l, TT * n + tt + 1))
                    c = 4 if half else 1
                    dve.tensor_scalar(var, pss[:, 0, tt:tt + 1], c * 0.5 / DM, c * 0.5 * EPS, ALU.mult, ALU.add)\
                       .then_inc(ch.sem, ch.one())
                    dve.wait_ge(ch.sem, ch.at(l))
                    rsqrt(dve, ch, l, r, var, t)
                    if tt == 0:
                        dve.wait_ge(row_loaded.sem, row_loaded.at(l, 16 * (n + 1)))
                    ins = dve.scalar_tensor_tensor(k.xs[:, tt, :].rearrange("p (b n) -> p b n", b=2),
                                                   k.ps[:, 4 + 2 * tt:6 + 2 * tt, :], r,
                                                   gain_row[:, :].rearrange("p (b n) -> p b n", b=2), ALU.mult, ALU.mult)
                    if tt == 0:
                        ins.then_inc(post_ready.sem, 1)
                    else:
                        ins.then_inc(ch.sem, ch.one())
                        dve.wait_ge(ch.sem, ch.at(l))
                        dve.wait_ge(k.x_new.sem, k.x_new.at(l, TT * (n + 1) + 1))
                        dve.tensor_tensor(k.x[:, tt, :], k.x[:, tt, :], k.xs[:, tt, :], ALU.add).then_inc(k.x_new.sem, 1)

            with dve.Fori(0, DEPTH) as l:
                low = Splitter(split_low, k, dve, st, l, AHEAD_LOW)
                ch = Chain(dve_chain.sem, DVE_B)
                norm_rstd(k, dve, ch, l, 0)
                low.upto(1)
                dve.wait_ge(par_loaded.sem, par_loaded.at(l, 32))
                norm_low(k, dve, l, 0, par[:, PB_N1:PB_NM])
                dve.wait_ge(wi_high.sem, wi_high.at(l, 1))
                dve.tensor_tensor(wi_lo[:, :, :], wi, wi_hi[:, :, :].bitcast(F32), ALU.subtract).then_inc(wi_split.sem, 1)
                low.upto(2)
                mlp(l, low, 0)
                low.next = M0
                low.upto(M0)
                post(l, ch, 0, True)
                norm_rstd(k, dve, ch, l, 1)
                low.upto(M0 + 1)
                norm_low(k, dve, l, 1, par[:, PB_NM:PB_N2])
                low.upto(M0 + 2)
                dve.tensor_tensor(ws, ws, mid(tri, 4), ALU.mult).then_inc(ch.sem, ch.one())
                dve.wait_ge(vss_ready.sem, vss_ready.at(l, 2))
                dve.tensor_scalar(vstat[:, 1, :], vstat[:, 0, :], 0.5 / BW, 0.5 * EPS, ALU.mult, ALU.add).then_inc(ch.sem, ch.one())
                dve.wait_ge(ch.sem, ch.at(l))
                rsqrt(dve, ch, l, vstat[:, 2, :], vstat[:, 1, :], vstat[:, 3, :])
                for tt in range(TT):
                    ins = dve.scalar_tensor_tensor(vn[:, tt, :], uv[:, tt, BW:], vstat[:, 2, tt:tt + 1], v_gain[:, :],
                                                   ALU.mult, ALU.mult)
                    if tt == 0:
                        ins.then_inc(ch.sem, ch.one())
                ins.then_inc(vn_ready.sem, 1)
                low.upto(M0 + 4)
                dve.wait_ge(wi_done.sem, wi_done.at(l, 1))
                dve.tensor_scalar(w_idx[:, :, :], k.ps[:, 6, 0:TT * IH].rearrange("p (t h) -> p t h", t=TT), IH ** -0.5, None,
                                  ALU.mult).then_inc(wi_ready.sem, 1)
                low.upto(M0 + 6)
                dve.wait_ge(f_evicted.sem, f_evicted.at(l, 2))
                dve.scalar_tensor_tensor(conv_x[:, :, CONV_PAD:], conv_y[:, :, :], 1.0,
                                         k.ps[:, 1, :].rearrange("p (f n) -> p f n", f=2), ALU.add, ALU.mult)\
                   .then_inc(hc_ready.sem, 1)
                dve.wait_ge(gm_done.sem, gm_done.at(l, 1))
                for g in range(4):
                    cols = slice(g * 64, (g + 1) * 64)
                    ins = dve.scalar_tensor_tensor(y0[:, :, cols], k.ps[:, 2, :].rearrange("p (t n) -> p t n", t=TT)[:, :, cols],
                                                   par[:, PB_GB + g:PB_GB + g + 1], uv[:, :, cols], ALU.add, ALU.mult)
                ins.then_inc(y0_ready.sem, 1)
                low.upto(M0 + 8)
                dve.wait_ge(y0H_ready.sem, y0H_ready.at(l, 1))
                dve.tensor_tensor(flat(yL[:, 0:2, :]), k.ps[:, 3, :], flat(yH[:, 0:2, :]).bitcast(F32), ALU.subtract)\
                   .then_inc(y0_split.sem, 1)
                low.upto(M0 + 9)

                def conv_taps(n):
                    for t in range(conv_taps.next, min(conv_taps.next + n, TAPS)):
                        for f in range(2):
                            w = par[:, PB_DW + 2 * t + f:PB_DW + 2 * t + f + 1]
                            src = conv_x[:, f, t:t + SEQ]
                            if t == POOL_TAPS:
                                ins = dve.tensor_scalar(conv_y[:, f, :], src, w, None, ALU.mult)
                            else:
                                dve.wait_ge(ch.sem, ch.at(l, 1))
                                ins = dve.scalar_tensor_tensor(conv_y[:, f, :], src, w, conv_y[:, f, :], ALU.mult, ALU.add)
                            if (t, f) == (TAPS - 1, 1):
                                ins.then_inc(conv_rest.sem, 1)
                            else:
                                ins.then_inc(ch.sem, ch.one())
                    conv_taps.next += n

                conv_taps.next = POOL_TAPS
                dve.wait_ge(taps_ready.sem, taps_ready.at(l, 1))
                dve.wait_ge(hc_ready.sem, hc_ready.at(l, 1))
                conv_taps(3)
                dve.wait_ge(rel_ready.sem, rel_ready.at(l, 1))
                tiles = ((0, slice(0, P)), (1, slice(P, 3 * P)))
                for h in range(IH):
                    for qt, cols in tiles:
                        w = w_idx[:, qt, h:h + 1]
                        if h == 0:
                            dve.tensor_scalar(score[:, cols], rel[:, h, cols], w, None, ALU.mult).then_inc(ch.sem, ch.one())
                        else:
                            dve.scalar_tensor_tensor(score[:, cols], rel[:, h, cols], w, score[:, cols], ALU.mult, ALU.add).then_inc(ch.sem, ch.one())
                    dve.wait_ge(ch.sem, ch.at(l))
                dve.tensor_tensor(score[:, :], score[:, :], reach, ALU.add).then_inc(ch.sem, ch.one())
                dve.wait_ge(ch.sem, ch.at(l))
                low.upto(M0 + 10)

                def logits(qt):
                    dve.wait_ge(sc_done.sem, sc_done.at(l, 2 - qt))
                    if qt == 1:
                        out, src, b = logit[:, :, P:3 * P], k.ps[:, 2:4, :].rearrange("p b (h n) -> p (b h) n", h=2), bias[:, :, P:3 * P]
                    else:
                        out, b = (v[:, :, 0:P].rearrange("p (b h) n -> p b h n", b=2) for v in (logit, bias))
                        src = k.ps[:, 4:6, 0:SEQ].rearrange("p b (h n) -> p b h n", h=2)
                    dve.scalar_tensor_tensor(out, src, BD ** -0.5, b, ALU.mult, ALU.add).then_inc(l_ready.sem, 1)

                dve.wait_ge(bias_moved.sem, bias_moved.at(0, 16 * (1 + 2 * BH)))
                for r in range(TOPK // 8):
                    value = held(dve, ch.at(l))
                    dve.wait_ge(const_loaded.sem, 16)
                    dve.wait_ge(ch.sem, value)
                    for qt, cols in tiles:
                        dve.max(top8[:, qt, :], score[:, cols]).then_inc(ch.sem, ch.one())
                    value = held(dve, ch.at(l))
                    dve.wait_ge(const_loaded.sem, 16)
                    dve.wait_ge(ch.sem, value)
                    for qt, cols in tiles:
                        dve.match_replace(score[:, cols], top8[:, qt, :], score[:, cols], TAKEN).then_inc(ch.sem, ch.one())
                    if r == 1:
                        logits(1)
                        low.upto(M0 + 11)
                    if r == 3:
                        logits(0)
                        low.upto(M0 + 12)
                    if r == 5:
                        low.upto(M0 + 13)
                    if r == 7:
                        low.upto(M0 + 14)
                dve.wait_ge(ch.sem, ch.at(l))
                dve.tensor_scalar(keep[:, :], score[:, :], TAKEN, -NEG, ALU.is_equal, ALU.mult).then_inc(ch.sem, ch.one())
                dve.wait_ge(ch.sem, ch.at(l))
                dve.scalar_tensor_tensor(keep[:, :], keep[:, :], NEG, reach, ALU.add, ALU.add).then_inc(ch.sem, ch.one())
                dve.wait_ge(ch.sem, ch.at(l))
                dve.wait_ge(l_ready.sem, l_ready.at(l, 2))
                for qt, cols in ((1, slice(P, 3 * P)), (0, slice(0, P))):
                    v = logit[:, :, cols]
                    dve.tensor_tensor(v, v, mid(keep[:, cols], BH), ALU.add).then_inc(ch.sem, ch.one())
                    dve.wait_ge(ch.sem, ch.at(l))
                    dve.tensor_reduce(rmax[:, qt, :], v, AX.X, ALU.max).then_inc(ch.sem, ch.one())
                    dve.wait_ge(ch.sem, ch.at(l))
                    dve.tensor_scalar(rmax[:, qt, :], rmax[:, qt, :], -1.0, None, ALU.mult).then_inc(max_ready.sem, 1)
                for c in (15, 16, 17):
                    low.upto(M0 + c)
                    conv_taps(4)
                low.upto(M0 + 18)
                dve.wait_ge(pv_done.sem, pv_done.at(l, 1))
                y2v = yb2[:, :, :].rearrange("p t (j e n) -> p t j e n", j=2, e=2)
                outs = [k.ps[:, (5, 2)[qt], 0:BH * (BD + 1)].rearrange("p (e j n) -> p e j n", e=2, j=2) for qt in range(TT)]
                for qt in range(TT):
                    dve.reciprocal(rsum[:, qt, :].rearrange("p (e j) -> p e j", e=2), outs[qt][:, :, :, BD]).then_inc(ch.sem, ch.one())
                dve.wait_ge(ch.sem, ch.at(l))
                for qt in range(TT):
                    for e in range(2):
                        ins = dve.tensor_tensor(y2v[:, qt, :, e, :], outs[qt][:, e, :, 0:BD],
                                                last(rsum[:, qt, 2 * e:2 * e + 2], BD), ALU.mult)
                ins.then_inc(y2_ready.sem, 1)
                low.upto(M0 + 19)
                dve.wait_ge(y2H_ready.sem, y2H_ready.at(l, 1))
                dve.tensor_tensor(flat(yL[:, 4:6, :]), k.ps[:, 3, :], flat(yH[:, 4:6, :]).bitcast(F32), ALU.subtract)\
                   .then_inc(y2_split.sem, 1)
                low.upto(M0 + 20)
                dve.wait_ge(ct_done.sem, ct_done.at(l, 1))
                byt = k.ps[:, 6, :].rearrange("p (t n) -> p t n", t=TT)
                dve.tensor_reduce(cstat[:, 0, :], byt, AX.X, ALU.add).then_inc(ch.sem, ch.one())
                dve.wait_ge(ch.sem, ch.at(l))
                dve.tensor_scalar(cstat[:, 0, :], cstat[:, 0, :], -1.0 / BW, None, ALU.mult).then_inc(ch.sem, ch.one())
                dve.wait_ge(ch.sem, ch.at(l))
                for tt in range(TT):
                    ins = dve.tensor_scalar(xc[:, tt, :], byt[:, tt, :], cstat[:, 0, tt:tt + 1], None, ALU.add)
                    if tt == 0:
                        ins.then_inc(ch.sem, ch.one())
                ins.then_inc(xc_ready.sem, 1)
                low.upto(M0 + 21)
                dve.wait_ge(css_ready.sem, css_ready.at(l, 2))
                dve.tensor_scalar(cstat[:, 1, :], cstat[:, 1, :], 0.5 / BW, 0.5 * EPS, ALU.mult, ALU.add).then_inc(ch.sem, ch.one())
                dve.wait_ge(ch.sem, ch.at(l))
                rsqrt(dve, ch, l, cstat[:, 2, :], cstat[:, 1, :], cstat[:, 3, :])
                for tt in range(TT):
                    ins = dve.tensor_scalar(diag[:, tt, :], k.ident, cstat[:, 2, tt:tt + 1], None, ALU.mult)
                    if tt == 0:
                        ins.then_inc(ch.sem, ch.one())
                ins.then_inc(cdiag_ready.sem, 1)
                low.upto(M0 + 22)
                dve.wait_ge(lt_ready.sem, lt_ready.at(l, 1))
                dve.scalar_tensor_tensor(flat(conv_y[:, :, :]), flat(xc[:, :, :]), 1.0, flat(conv_y[:, :, :]), ALU.add, ALU.mult)\
                   .then_inc(y3_ready.sem, 1)
                low.upto(M0 + 23)
                dve.wait_ge(y3H_ready.sem, y3H_ready.at(l, 1))
                dve.scalar_tensor_tensor(flat(yL[:, 6:8, :]), flat(conv_y[:, :, :]), 0.5, flat(yH[:, 6:8, :]).bitcast(F32),
                                         ALU.mult, ALU.subtract).then_inc(y3_split.sem, 1)
                dve.wait_ge(y1H_ready.sem, y1H_ready.at(l, 1))
                for g in range(4):
                    j, e = g // 2, g % 2
                    half = slice(e * 64, (e + 1) * 64)
                    ins = dve.scalar_tensor_tensor(yL[half, 2 + j, :], k.ps[half, 4 + 2 * e, j * SEQ:(j + 1) * SEQ],
                                                   par[half, PB_PS + j:PB_PS + j + 1], yH[half, 2 + j, :].bitcast(F32),
                                                   ALU.mult, ALU.subtract)
                ins.then_inc(y1_split.sem, 1)
                low.upto(BR + 1)
                dve.wait_ge(f_evicted.sem, f_evicted.at(l, 22))

                def mix_low(i):
                    dve.wait_ge(mixH_ready.sem, mixH_ready.at(l, i + 1))
                    dve.scalar_tensor_tensor(flat(k.aL[:, 2 * i:2 * i + 2, :]), gated[i % 2][0], 0.5,
                                             flat(k.aH[:, 2 * i:2 * i + 2, :]).bitcast(F32), ALU.mult, ALU.subtract)\
                       .then_inc(mix_split.sem, 1)

                for i in range(4):
                    low.upto(BR + 1 + i)
                    dve.wait_ge(k.chunk_done, st.results(l, BR + i))
                    if i >= 2:
                        dve.wait_ge(mix_split.sem, mix_split.at(l, i - 1))
                    for n in range(NBR):
                        g = flat(gates[:, 8 * n + 2 * i:8 * n + 2 * i + 2, :])
                        dve.scalar_tensor_tensor(gated[i % 2][n], g, 1.0, k.ps[:, 4 * ((i + 1) % 2) + n, :], ALU.add, ALU.mult)\
                           .then_inc(branch_ready.sem, 1)
                    if i:
                        mix_low(i - 1)
                low.upto(BR + 5)
                mix_low(3)
                low.upto(F0[1])
                post(l, ch, 1, False)
                norm_rstd(k, dve, ch, l, 2)
                low.upto(F0[1] + 1)
                norm_low(k, dve, l, 2, par[:, PB_N2:PB_DW])
                low.upto(F0[1] + 2)
                mlp(l, low, 1)
                split_ahead(split_low, k, dve, st, l + 1, AHEAD_LOW)
                post(l, ch, 2, True)
                assert ch.n == DVE_B, ("dve", ch.n)

        @block.tensor
        def _(pe):
            aop = lambda kt: (k.aH[:, kt, :], k.aL[:, kt, :])
            yop = lambda kt: (yH[:, kt, :], yL[:, kt, :])
            t_out = lambda tt, h: k.ps[:, 4 + 2 * tt + h, :]
            pe.wait_ge(const_loaded.sem, 16)

            def mlp(l, f):
                def up(j, trips=0, q=0):
                    base = (l * 2 + f) * FF_B + q
                    pe.wait_ge(k.lo_ready, st.count(l, a_chunk(f, j), trips))
                    if j >= 2:
                        pe.wait_ge(silu_ready.sem, base + (j - 1))
                    f_chunk(k, pe, a_chunk(f, j), [2 * (j % 2)], [range(8)], aop,
                            (lambda i: k.a_ready.at(l, 8 * f + i + 1)) if j == 0 else None)
                    pe.wait_ge(k.lo_ready, st.count(l, b_chunk(f, j), trips))
                    if j >= 2:
                        pe.wait_ge(gated_ready.sem, base + (j - 1))
                    f_chunk(k, pe, b_chunk(f, j), [2 * (j % 2) + 1], [range(8)], aop)

                def down(j, trips=0, q=0):
                    pe.wait_ge(k.lo_ready, st.count(l, down_chunk(f, j), trips))
                    pe.wait_ge(hid_ready.sem, (l * 2 + f) * FF_B + q + (j + 1))
                    hid = lambda kt: [x[:, j % 2, kt * SEQ:(kt + 1) * SEQ] for x in (hidH, hidL)]
                    t_chunk(k, pe, down_chunk(f, j), range(2), DM, hid, t_out, j == 0, j == FF_B - 1,
                            k.tile_done.sem if j == FF_B - 1 else None)

                up(0)
                up(1)
                down(0)
                with pe.Fori(0, 4) as q:
                    for j in (1, 2):
                        up(j + 1, q * 2, q * 2)
                        down(j, q * 2, q * 2)
                up(10)
                down(9)
                down(10)

            with pe.Fori(0, DEPTH) as l:
                norm_transpose(k, pe, l, 0)
                mlp(l, 0)
                norm_transpose(k, pe, l, 1)
                for half in range(2):
                    pe.wait_ge(k.lo_ready, st.count(l, M0 + half))
                    pe.wait_ge(k.a_ready.sem, k.a_ready.at(l, 4 + 2 * half + 2))
                    t_chunk(k, pe, M0 + half, range(4 * half, 4 * half + 4), 512, aop,
                            lambda tt, h: k.ps[:, 2 + tt, :], half == 0, half == 1)
                pe.wait_ge(k.lo_ready, st.count(l, M0 + 2))
                t_chunk(k, pe, M0 + 2, range(8), 256, aop, lambda tt, h: k.ps[:, 0, tt * BW:(tt + 1) * BW], True, True)
                pe.wait_ge(par_loaded.sem, par_loaded.at(l, 32))
                pe.wait_ge(wi_split.sem, wi_split.at(l, 1))
                for tt in range(TT):
                    for kt in range(KT):
                        a = [x[:, kt, tt * P:(tt + 1) * P] for x in (k.aH, k.aL)]
                        ins = product(pe, k.ps[:, 6, tt * IH:(tt + 1) * IH], a, (wi_hi[:, kt, :], wi_lo[:, kt, :]),
                                      kt == 0, kt == KT - 1)
                ins.then_inc(wi_done.sem, 1)

                def feature(i):
                    pe.wait_ge(k.lo_ready, st.count(l, M0 + i))
                    if i == 5:
                        pe.wait_ge(hc_ready.sem, hc_ready.at(l, 1))
                    elif i == 4:
                        pe.wait_ge(f_evicted.sem, f_evicted.at(l, 1))
                    elif i >= 6:
                        pe.wait_ge(f_evicted.sem, f_evicted.at(l, i - 4))
                    f_chunk(k, pe, M0 + i, [i % 2], [range(8)], aop)

                for i in (3, 4, 5):
                    feature(i)
                pe.wait_ge(vn_ready.sem, vn_ready.at(l, 1))
                for tt in range(TT):
                    for g in range(4):
                        ins = pe.matmul(k.ps[:, 2, tt * BW + g * 64:tt * BW + (g + 1) * 64], ws[:, g, :],
                                        vn[:, tt, g * 64:(g + 1) * 64], start=True, stop=True)
                ins.then_inc(gm_done.sem, 1)
                feature(6)

                def to_features(bank, src, by=None):
                    for f in range(2):
                        for tt in range(TT):
                            out, a = k.ps[:, bank, f * SEQ + tt * P:f * SEQ + (tt + 1) * P], src[:, tt, f * P:(f + 1) * P]
                            if by is None:
                                ins = pe.transpose(out, a, k.ident)
                            else:
                                ins = pe.matmul(out, a, by[:, tt, :], start=True, stop=True)
                    return ins

                pe.wait_ge(y0_ready.sem, y0_ready.at(l, 1))
                to_features(3, y0).then_inc(y0T_done.sem, 1)
                feature(7)
                pe.wait_ge(f_evicted.sem, f_evicted.at(l, 4))
                pe.wait_ge(wi_ready.sem, wi_ready.at(l, 1))
                for h in range(IH):
                    rows_ = slice(h * ID, (h + 1) * ID)
                    pe.matmul(k.ps[:, 4 + h, 0:P], idxF[rows_, 0, 0:P], idxF[rows_, 1, 0:P], start=True, stop=True)
                    ins = pe.matmul(k.ps[:, 4 + h, P:3 * P], idxF[rows_, 0, P:SEQ], idxF[rows_, 1, :], start=True, stop=True)
                ins.then_inc(rel_done.sem, 1)
                feature(8)
                feature(9)

                def scores(qt):
                    n = (qt + 1) * P
                    for h in range(BH):
                        j, e = head_slot(h)
                        rows_ = slice(e * BD, (e + 1) * BD)
                        ins = pe.matmul(k.ps[:, (4, 2)[qt] + e, j * n:(j + 1) * n], qkF[rows_, j, qt * P:(qt + 1) * P],
                                        qkF[rows_, 2 + j, 0:n], start=True, stop=True)
                    ins.then_inc(sc_done.sem, 1)

                pe.wait_ge(f_evicted.sem, f_evicted.at(l, 6))
                pe.wait_ge(y0_split.sem, y0_split.at(l, 1))
                scores(1)
                feature(10)
                pe.wait_ge(rel_ready.sem, rel_ready.at(l, 1))
                scores(0)
                for i in range(11, 17):
                    feature(i)
                pe.wait_ge(exp_ready.sem, exp_ready.at(l, 2))
                for h in range(BH):
                    for kb in range(2):
                        ins = pe.transpose(k.ps[:, 2 + h // 2, (h % 2) * SEQ + kb * P:(h % 2) * SEQ + (kb + 1) * P], logit[:, h, (1 + kb) * P:(2 + kb) * P], k.ident)
                ins.then_inc(pT_done.sem, 1)
                for h in range(BH):
                    ins = pe.transpose(k.ps[:, 4, h * P:(h + 1) * P], logit[:, h, 0:P], k.ident)
                ins.then_inc(pT_done.sem, 1)
                feature(17)
                pe.wait_ge(pT_ready.sem, pT_ready.at(l, 2))
                for qt in range(TT):
                    for h in range(BH):
                        j, e = head_slot(h)
                        out = k.ps[:, (5, 2)[qt], (2 * e + j) * (BD + 1):(2 * e + j + 1) * (BD + 1)]
                        for s in range(qt + 1):
                            ins = pe.matmul(out, pT[:, 2 * e + j, s + qt, :], v_tok[:, s, h, :], start=s == 0, stop=s == qt)
                ins.then_inc(pv_done.sem, 1)
                feature(18)
                pe.wait_ge(y2_ready.sem, y2_ready.at(l, 1))
                to_features(3, yb2).then_inc(y2T_done.sem, 1)
                feature(19)
                pe.wait_ge(conv_done.sem, conv_done.at(l, 1))
                for tt in range(TT):
                    for f in range(2):
                        ins = pe.transpose(k.ps[:, 6, tt * BW + f * P:tt * BW + (f + 1) * P], conv_y[:, f, tt * P:(tt + 1) * P], k.ident)
                ins.then_inc(ct_done.sem, 1)
                feature(20)
                feature(21)
                pe.wait_ge(cdiag_ready.sem, cdiag_ready.at(l, 1))
                to_features(7, xc, diag).then_inc(lnT_done.sem, 1)
                feature(22)
                pe.wait_ge(const_loaded.sem, 16)
                pe.wait_ge(pool_ready.sem, pool_ready.at(l, 1))
                pe.wait_ge(y2_split.sem, y2_split.at(l, 1))
                for g in range(4):
                    j, e = g // 2, g % 2
                    half = slice(e * 64, (e + 1) * 64)
                    ins = pe.matmul(k.ps[half, 4 + 2 * e, j * SEQ:(j + 1) * SEQ], pw[half, j, :], pooled[half, j, :],
                                    start=True, stop=True)
                ins.then_inc(pmm_done.sem, 1)
                feature(23)
                feature(24)
                for i in range(4):
                    pe.wait_ge(k.lo_ready, st.count(l, BR + i))
                    if i == 0:
                        pe.wait_ge(y0_split.sem, y0_split.at(l, 1))
                        pe.wait_ge(y2_split.sem, y2_split.at(l, 1))
                        pe.wait_ge(y3_split.sem, y3_split.at(l, 1))
                        pe.wait_ge(y1_split.sem, y1_split.at(l, 1))
                        pe.wait_ge(f_evicted.sem, f_evicted.at(l, 22))
                    if i >= 2:
                        pe.wait_ge(branch_ready.sem, branch_ready.at(l, NBR * (i - 1)))
                    f_chunk(k, pe, BR + i, [4 * ((i + 1) % 2) + n for n in range(NBR)], [(2 * n, 2 * n + 1) for n in range(NBR)], yop)
                pe.wait_ge(branch_ready.sem, branch_ready.at(l, NBR * 3))
                for i in range(4):
                    pe.wait_ge(k.lo_ready, st.count(l, WO + i))
                    pe.wait_ge(mix_split.sem, mix_split.at(l, i + 1))
                    if i < 2:
                        t_chunk(k, pe, WO + i, range(2 * i, 2 * i + 2), DM, aop, t_out, i == 0, False)
                t_last(k, pe, [(WO + i, lambda kt, i=i: aop(2 * i + kt)) for i in (2, 3)], t_out)
                norm_transpose(k, pe, l, 2)
                mlp(l, 1)


class Names:
    pass


def tensors(nc, k, ctx):
    def sb(name, shape, dt=F32):
        return ctx.enter_context(nc.sbuf_tensor(name, shape, dt))

    k.ps = ctx.enter_context(nc.psum_tensor("ps", [P, 8, 512], F32))
    k.raw = sb("raw", [P, SLOTS, CH])
    k.w_hi, k.w_lo = sb("w_hi", [P, SLOTS, CH], F32R), sb("w_lo", [P, SLOTS, CH], F32R)
    k.x = sb("x", [P, TT, DM])
    k.aH, k.aL = sb("aH", [P, KT, SEQ], F32R), sb("aL", [P, KT, SEQ], F32R)
    k.mixH, k.mixL = sb("mixH", [P, 8 * SEQ], F32R), sb("mixL", [P, 8 * SEQ], F32R)
    k.consts = sb("consts", [P, int(max(KA_END, KB_END))])
    k.rows = sb("rows", [P, ROWS_A])
    k.par_b = k.rows[:, ROWS_A - int(PB_END):ROWS_A]
    k.ss, k.var, k.rstd, k.tmp = (sb(n, [P, 8]) for n in ("ss", "var", "rstd", "tmp"))
    k.x_loaded = ctx.enter_context(nc.semaphore("x_loaded"))
    k.pre_chain = ctx.enter_context(nc.semaphore("pre_chain"))
    k.consts_b_loaded, k.par_b_loaded, k.bias_moved = (
        ctx.enter_context(nc.semaphore(n)) for n in ("consts_b_loaded", "par_b_loaded", "bias_moved"))
    k.raw_loaded = [ctx.enter_context(nc.semaphore(f"raw_loaded{s}")) for s in range(SLOTS)]
    k.hi_ready, k.lo_ready, k.chunk_done, k.stored = (
        ctx.enter_context(nc.semaphore(n)) for n in ("hi_ready", "lo_ready", "chunk_done", "stored"))


def constants_a():
    c = np.zeros((P, KA_END), np.float32)
    t, s = np.arange(SEQ)[:, None], np.arange(SEQ)[None, :]
    dist = t - s
    mult = sum(((dist >= 0) & (dist % r == 0) & (dist // r <= w // r)).astype(np.float32)
               for w, r in ((128, 1), (512, 4), (2048, 16)))
    add = np.where(mult > 0, 0.0, NEG).astype(np.float32)
    c[:, KA_ID:KA_FREQ] = np.eye(P)
    for lo, m in ((KA_ADD, add), (KA_MULT, mult)):
        c[:, lo:lo + P], c[:, lo + P:lo + 3 * P] = m[:P, :P], m[P:]
    causal = np.where(dist >= 0, 0.0, NEG).astype(np.float32).T
    c[:, KA_CAUS:KA_CAUS + SEQ], c[:, KA_CAUS + SEQ:KA_SEL] = causal[:P], causal[P:, P:]
    for h in range(MH):
        c[h, KA_SEL + h * P:KA_SEL + (h + 1) * P] = 1.0
    c[:, KA_FREQ:KA_ADD] = (np.float64(500000.0) ** (-np.arange(0, 2 * RH, 2) / (2 * RH))).astype(np.float32)
    return c


def f_pack(w):
    return [w[:, i:i + 256].reshape(8, P, 256).transpose(1, 0, 2).reshape(P, CH) for i in range(0, w.shape[1], 256)]


def t_pack(w, width):
    n = CH // width
    return [w[i:i + n * P].reshape(n, P, width).transpose(1, 0, 2).reshape(P, CH) for i in range(0, w.shape[0], n * P)]


def columns(*vs):
    return np.concatenate([np.asarray(v).reshape(-1, P).T for v in vs], axis=1)


def pack_first(a, l):
    w, b = a["w_in"][l], a["b_in"][l]
    chunks = []
    for lo in (0, 512, 1024, 2560):
        chunks += t_pack(w[:, lo:lo + 512], 512)
    chunks += f_pack(w[:, 1536:2560])
    gate = np.zeros((P, CH), np.float32)
    gate_b = np.zeros((P, 1), np.float32)
    for lo in (0, 1):
        cols = slice(3584 + lo * MH, 3584 + (lo + 1) * MH)
        gate.reshape(P, 8, 256)[:, :, 32 * lo:32 * lo + MH] = w[:, cols].reshape(8, P, MH).transpose(1, 0, 2)
        gate_b[32 * lo:32 * lo + MH, 0] = b[cols]
    chunks.append(gate)
    chunks += f_pack(w[:, 3072:3584]) + f_pack(w[:, 3592:5640])
    chunks += f_pack(np.concatenate([a["w_proj_att"][l], a["w_proj_mlstm"][l]]))
    chunks += t_pack(a["w_out"][l], DM)
    up, down = f_pack(a["w_ff1"][l]), t_pack(a["w_ff2"][l], DM)
    chunks += [up[0], up[1]]
    for j in range(FF_A):
        chunks += up[j + 2:j + 3] + down[j:j + 1]
    par = columns(a["norm_mix_w"][l], a["norm_mlp_w"][l], b[1536:2560], b[3072:3584], b[3592:5640],
                  a["conv_w"][l].reshape(-1), a["conv_b"][l], a["mlstm_norm_w"][l])
    par = np.concatenate([par, gate_b], axis=1)
    rows = np.concatenate([b[0:1536], b[2560:3072], b[3584:3592]])
    return chunks, par, rows


def constants_b():
    c = np.zeros((P, KB_END), np.float32)
    c[:, KB_ID:KB_ADD] = np.eye(P)
    dist = np.arange(SEQ)[:, None] - np.arange(SEQ)[None, :]
    reach = np.where(dist >= 0, 0.0, OUT_OF_REACH).astype(np.float32)
    c[:, KB_ADD:KB_ADD + P], c[:, KB_ADD + P:KB_CNT] = reach[:P, :P], reach[P:]
    count = c[:, KB_CNT:KB_TRI].reshape(P, 2, SEQ)
    for g, w in enumerate((2, 4, 8, 16)):
        count[64 * (g % 2):64 * (g % 2) + 64, g // 2] = 1.0 / np.minimum(np.arange(1, SEQ + 1), w)
    c[:, KB_CNT:KB_TRI] = count.reshape(P, -1)
    c[:, KB_TRI:KB_END] = np.triu(np.ones((P, P)))
    return c


def hot_distances():
    n = np.arange(SEQ)
    large = 16 + (np.log(np.maximum(n, 1) / 16) / math.log(8) * 16).astype(np.int64)
    bucket = np.where(n < 16, n, np.minimum(large, 31))
    hot = np.zeros((32, SEQ), np.float32)
    hot[bucket[::-1], np.arange(SEQ)] = 1.0
    return hot


def mlp_pack(gu, down):
    a, b, dn = f_pack(gu[:, :256 * FF_B]), f_pack(gu[:, 256 * FF_B:]), t_pack(down, DM)
    chunks = [a[0], b[0]]
    for j in range(FF_B):
        chunks += a[j + 1:j + 2] + b[j + 1:j + 2] + dn[j:j + 1]
    return chunks


def pack_second(a, l):
    w = a["w_in_2"][l]
    chunks = mlp_pack(a["ffn1_w_gu_2"][l], a["ffn1_w_down_2"][l])
    chunks += t_pack(w[:, 0:512], 512)
    chunks += f_pack(w[:, 1280:1536])
    chunks += f_pack(w[:, 1700:2212])
    chunks += f_pack(w[:, 512:768])
    chunks += f_pack(np.concatenate([w[:, 1536:1664]] + [w[:, 1664:1696]] * IH, axis=1))
    chunks += f_pack(w[:, 768:1280])
    chunks += f_pack(w[:, 2212:6308])
    chunks += f_pack(a["w_branch_2"][l].reshape(NBR * BW, DM))
    chunks += t_pack(a["w_out_2"][l], DM)
    chunks += mlp_pack(a["ffn2_w_gu_2"][l], a["ffn2_w_down_2"][l])
    par = np.concatenate([
        columns(a["ffn1_pre_g_2"][l], a["mix_pre_g_2"][l], a["ffn2_pre_g_2"][l], a["conv_dw_2"][l].reshape(-1),
                a["conv_b_2"][l], a["conv_ln_g_2"][l], a["conv_ln_b_2"][l], a["pool_scale_2"][l], a["gm_b_2"][l]),
        w[:, 1696:1700].reshape(KT, P, IH).transpose(1, 0, 2).reshape(P, -1),
        a["gm_ws_2"][l].transpose(2, 0, 1).reshape(P, -1),
        a["pool_w_2"][l].reshape(2, 2, 64, 64).transpose(1, 2, 0, 3).reshape(P, -1)], axis=1)
    return chunks, par


def pack(inputs):
    a = {n: np.asarray(v) for n, v in inputs.items()}
    first = [pack_first(a, l) for l in range(DEPTH)]
    second = [pack_second(a, l) for l in range(DEPTH)]
    gains = [a[n][l] for l in range(DEPTH) for n in ("ffn1_post_g_2", "mix_post_g_2", "ffn2_post_g_2")]
    arrays = {
        "x": a["x"][0],
        "positions": a["positions"].reshape(TT, P).T,
        "w_a": np.stack([c for chunks, _, _ in first for c in chunks]),
        "par_a": np.concatenate([par for _, par, _ in first]),
        "rows_a": np.stack([rows for _, _, rows in first]),
        "final_norm_w": a["final_norm_w"],
        "consts_a": constants_a(),
        "w_b": np.stack([c for chunks, _ in second for c in chunks]),
        "par_b": np.concatenate([par for _, par in second + second[-1:]]),
        "v_gain": np.stack([a["gm_v_g_2"][l] for l in (*range(DEPTH), DEPTH - 1)]),
        "post_gains": np.stack(gains + gains[-1:]),
        "hot_b": hot_distances(),
        "rel_bias": a["rel_bias_2"],
        "consts_b": constants_b(),
    }
    return {n: np.ascontiguousarray(v) for n, v in arrays.items()}


def program(nc, d):
    k = Names()
    with ExitStack() as ctx:
        tensors(nc, k, ctx)
        first_block(nc, k, d, ctx)
        second_block(nc, k, d, ctx)


def kernel(**inputs):
    import concourse.bacc as bacc
    from concourse.bass_utils import run_bass_kernel_spmd

    nc = bacc.Bacc("TRN2", target_bir_lowering=False, num_devices=1)
    arrays = pack(inputs)
    d = Names()
    for name, a in arrays.items():
        vars(d)[name] = nc.dram_tensor("in_" + name, a.shape, mybir.dt.from_np(a.dtype), kind="ExternalInput").ap()
    d.bias_line = nc.dram_tensor("bias_line", (P, BH, 2 * SEQ), F32, kind="Internal").ap()
    d.out = nc.dram_tensor("out", (SEQ, DM), F32, kind="ExternalOutput").ap()
    program(nc, d)
    r = run_bass_kernel_spmd(nc, [{"in_" + n: a for n, a in arrays.items()}], core_ids=[0])
    return r.results[0]["out"].reshape(1, SEQ, DM)
```
